# Optimizing a Trainium2 kernel written in Bass

```python
import math
import jax, jax.numpy as jnp
from jax import lax
import numpy as np

D_MODEL = 1024
BATCH = 1
SEQ = 256
DEPTH = 1

HEAD_DIM = 64
N_BRANCHES = 4
BRANCH_WIDTH = D_MODEL // 4

A_HEADS = BRANCH_WIDTH // HEAD_DIM
A_PATTERNS = ((128, 1), (512, 4), (2048, 16))
A_BLOCK = 128
B_HEADS = BRANCH_WIDTH // HEAD_DIM
B_LATENT = D_MODEL // 16
IDX_HEADS = 8
IDX_DIM = 32
TOPK_MAX = 256
TOPK_DIV = 4
Q_BLOCK = 128
C_HEADS = 4
C_KEY_DIM = 32
C_VAL_DIM = BRANCH_WIDTH // C_HEADS
C_GATE_RANK = 16
C_GATE_TAU = 16.0
C_CHUNK = 64
D_HEADS = 4
D_HEAD_SIZE = BRANCH_WIDTH // D_HEADS
D_DECAY_RANK = 16
D_ICLR_RANK = 16
D_GATE_RANK = 32
D_GN_EPS = 64e-5
D_IN_WIDTH = 3 * BRANCH_WIDTH + D_DECAY_RANK + D_ICLR_RANK + D_GATE_RANK
RPB_BUCKETS = 32
RPB_MAX_DIST = 2048
RPB_HEADS = A_HEADS + B_HEADS
MOE_GROUPS = 4
MOE_PER_GROUP = 8
MOE_EXPERTS = MOE_GROUPS * MOE_PER_GROUP
MOE_TOPK = 2
MOE_HIDDEN = 256
DN_ALPHA = (2 * DEPTH) ** 0.25
DN_BETA = (8 * DEPTH) ** -0.25
LN_EPS = 1e-5

IN_SPLITS = (
    ("a_q", A_HEADS * HEAD_DIM), ("a_k", A_HEADS * HEAD_DIM), ("a_v", A_HEADS * HEAD_DIM),
    ("b_q", B_HEADS * B_LATENT), ("b_ckv", B_LATENT), ("b_iq", IDX_HEADS * IDX_DIM),
    ("b_ik", IDX_DIM), ("b_iw", IDX_HEADS),
    ("c_q", C_HEADS * C_KEY_DIM), ("c_k", C_HEADS * C_KEY_DIM), ("c_v", C_HEADS * C_VAL_DIM),
    ("c_a", C_GATE_RANK), ("c_g", BRANCH_WIDTH),
    ("d", D_IN_WIDTH),
    ("gate", N_BRANCHES * D_MODEL),
)
IN_WIDTH = sum(w for _, w in IN_SPLITS)


def _split_in(h):
    out = {}
    off = 0
    for name, w in IN_SPLITS:
        out[name] = h[..., off:off + w]
        off += w
    return out

def _layer_norm(x, g, b):
    xf = x.astype(jnp.float32)
    mu = jnp.mean(xf, -1, keepdims=True)
    var = jnp.mean(jnp.square(xf - mu), -1, keepdims=True)
    return ((xf - mu) * lax.rsqrt(var + LN_EPS) * g + b).astype(x.dtype)

def _rms_norm(x, g, eps=1e-6):
    xf = x.astype(jnp.float32)
    return (xf * lax.rsqrt(jnp.mean(xf * xf, -1, keepdims=True) + eps) * g).astype(x.dtype)

def _t5_bucket(dist):
    exact = RPB_BUCKETS // 2
    d = jnp.maximum(dist, 0)
    df = jnp.maximum(d, 1).astype(jnp.float32)
    large = exact + (jnp.log(df / exact) / math.log(RPB_MAX_DIST / exact)
                     * (RPB_BUCKETS - exact)).astype(jnp.int32)
    large = jnp.minimum(large, RPB_BUCKETS - 1)
    return jnp.where(d < exact, d, large)

def _dilated_pattern(q, k, v, bias_tab, window, dilation):
    bsz, seq, nh, dh = q.shape
    lr = seq // dilation
    span = window // dilation
    nb = -(-lr // A_BLOCK)
    lp = nb * A_BLOCK
    bd = bsz * dilation

    def regroup(z):
        z = z.reshape(bsz, lr, dilation, nh, dh).transpose(0, 2, 1, 3, 4)
        return z.reshape(bd, lr, nh, dh)

    qr, kr, vr = regroup(q), regroup(k), regroup(v)
    qb = jnp.pad(qr, ((0, 0), (0, lp - lr), (0, 0), (0, 0))).reshape(bd, nb, A_BLOCK, nh, dh)

    def band(z):
        zp = jnp.pad(z, ((0, 0), (A_BLOCK, lp - lr), (0, 0), (0, 0)))
        prev = zp[:, :lp].reshape(bd, nb, A_BLOCK, nh, dh)
        cur = zp[:, A_BLOCK:].reshape(bd, nb, A_BLOCK, nh, dh)
        return jnp.concatenate([prev, cur], axis=2)

    kb, vb = band(kr), band(vr)
    qi = jnp.arange(A_BLOCK)[:, None]
    kj = jnp.arange(2 * A_BLOCK)[None, :]
    rdist = qi + A_BLOCK - kj
    in_band = (rdist >= 0) & (rdist <= span)
    bias = jnp.transpose(bias_tab[_t5_bucket(rdist * dilation)], (2, 0, 1))
    kpos = jnp.arange(nb)[:, None] * A_BLOCK - A_BLOCK + kj
    mask = in_band[None] & (kpos >= 0)[:, None, :]

    s = jnp.einsum('bnqhd,bnkhd->bnhqk', qb, kb).astype(jnp.float32) * dh ** -0.5 + bias
    s = jnp.where(mask[None, :, None], s, -jnp.inf)
    m = jnp.max(s, -1, keepdims=True)
    p = jnp.exp(s - m)
    den = jnp.sum(p, -1)
    o = jnp.einsum('bnhqk,bnkhd->bnqhd', p, vb.astype(jnp.float32))
    o = o / jnp.swapaxes(den, 2, 3)[..., None]
    lse = jnp.swapaxes(m[..., 0] + jnp.log(den), 2, 3)
    o = o.reshape(bd, lp, nh, dh)
    lse = lse.reshape(bd, lp, nh)

    def ungroup(z):
        z = z[:, :lr].reshape((bsz, dilation, lr) + z.shape[2:])
        z = jnp.moveaxis(z, 1, 2)
        return z.reshape((bsz, seq) + z.shape[3:])

    return ungroup(o), ungroup(lse)

def _mixer_a(q, k, v, bias_tab):
    bsz, seq, _ = q.shape
    shp = (bsz, seq, A_HEADS, HEAD_DIM)
    q, k, v = q.reshape(shp), k.reshape(shp), v.reshape(shp)
    outs, lses = [], []
    for window, dilation in A_PATTERNS:
        o, lse = _dilated_pattern(q, k, v, bias_tab, window, dilation)
        outs.append(o)
        lses.append(lse)
    wts = jax.nn.softmax(jnp.stack(lses), axis=0)
    o = jnp.sum(jnp.stack(outs) * wts[..., None], axis=0)
    return o.reshape(bsz, seq, A_HEADS * HEAD_DIM).astype(q.dtype)

def _mixer_b(q, ckv, iq, ik, iw, kv_gain, w_uv, bias_tab):
    bsz, seq, _ = q.shape
    keep = min(TOPK_MAX, seq // TOPK_DIV)
    nblk = seq // Q_BLOCK
    q = q.reshape(bsz, seq, B_HEADS, B_LATENT)
    ckv = _rms_norm(ckv, kv_gain)
    iq = iq.reshape(bsz, seq, IDX_HEADS, IDX_DIM)

    def to_blocks(z):
        return jnp.moveaxis(z.reshape((bsz, nblk, Q_BLOCK) + z.shape[2:]), 1, 0)

    def one_block(args):
        bi, qb, iqb, iwb = args
        tpos = bi * Q_BLOCK + jnp.arange(Q_BLOCK)
        rel = jax.nn.relu(jnp.einsum('bqhd,bsd->bqhs', iqb, ik).astype(jnp.float32) * IDX_DIM ** -0.5)
        score = jnp.einsum('bqhs,bqh->bqs', rel, iwb.astype(jnp.float32)) * IDX_HEADS ** -0.5
        admissible = jnp.arange(seq)[None, :] <= tpos[:, None]
        score = jnp.where(admissible[None], score, -jnp.inf)
        _, idx = lax.top_k(score, keep)
        sel = jax.vmap(lambda c, i: c[i])(ckv, idx)
        logits = jnp.einsum('bqhc,bqkc->bqhk', qb, sel).astype(jnp.float32) * B_LATENT ** -0.5
        dist = tpos[None, :, None] - idx
        bias = jnp.moveaxis(bias_tab[_t5_bucket(dist)], -1, 2)
        logits = jnp.where((dist >= 0)[:, :, None, :], logits + bias, -jnp.inf)
        p = jax.nn.softmax(logits, axis=-1)
        return jnp.einsum('bqhk,bqkc->bqhc', p.astype(sel.dtype), sel)

    ob = lax.map(one_block, (jnp.arange(nblk), to_blocks(q), to_blocks(iq), to_blocks(iw)))
    o = jnp.moveaxis(ob, 0, 1).reshape(bsz, seq, B_HEADS, B_LATENT)
    o = jnp.einsum('bshc,hcd->bshd', o, w_uv)
    return o.reshape(bsz, seq, B_HEADS * HEAD_DIM).astype(q.dtype)

def _mixer_c(q, k, v, a_low, og, a_up, a_bias, norm_gain):
    f32 = jnp.float32
    bsz, seq, _ = q.shape
    nc = seq // C_CHUNK
    log_a = jax.nn.log_sigmoid((a_low @ a_up + a_bias).astype(f32)) / C_GATE_TAU

    def chunks(z, dim):
        return z.astype(f32).reshape(bsz, nc, C_CHUNK, C_HEADS, dim)

    qc = chunks(q, C_KEY_DIM) * C_KEY_DIM ** -0.5
    kc = chunks(k, C_KEY_DIM)
    vc = chunks(v, C_VAL_DIM)
    cum = jnp.cumsum(chunks(log_a, C_KEY_DIM), axis=2)
    last = cum[:, :, -1]
    q_dec = qc * jnp.exp(cum)
    k_inv = kc * jnp.exp(-cum)
    causal = jnp.tril(jnp.ones((C_CHUNK, C_CHUNK), bool))
    att = jnp.where(causal, jnp.einsum('bnihd,bnjhd->bnhij', q_dec, k_inv), 0.0)
    o_intra = jnp.einsum('bnhij,bnjhv->bnihv', att, vc)
    upd = jnp.einsum('bnjhd,bnjhv->bnhdv', kc * jnp.exp(last[:, :, None] - cum), vc)
    dec = jnp.exp(last)

    def step(state, inp):
        d, u = inp
        return d[..., None] * state + u, state

    init = jnp.zeros((bsz, C_HEADS, C_KEY_DIM, C_VAL_DIM), f32)
    _, before = lax.scan(step, init, (jnp.moveaxis(dec, 1, 0), jnp.moveaxis(upd, 1, 0)))
    before = jnp.moveaxis(before, 0, 1)
    o = o_intra + jnp.einsum('bnihd,bnhdv->bnihv', q_dec, before)
    o = o.reshape(bsz, seq, C_HEADS, C_VAL_DIM)
    o = o * lax.rsqrt(jnp.mean(o * o, -1, keepdims=True) + 1e-6)
    o = o.reshape(bsz, seq, BRANCH_WIDTH) * norm_gain
    return (jax.nn.silu(og.astype(f32)) * o).astype(q.dtype)

def _token_shift(z, mu):
    prev = jnp.pad(z, ((0, 0), (1, 0), (0, 0)))[:, :-1]
    return z + (prev - z) * mu

def _mixer_d(seg, mu, w0, w2, a0, a2, g2, k_k, k_a, r_k, gn_w, gn_b):
    f32 = jnp.float32
    out_dtype = seg.dtype
    bsz, seq, _ = seg.shape
    bw = BRANCH_WIDTH
    seg = _token_shift(seg, mu).astype(f32)
    r, k, v = seg[..., :bw], seg[..., bw:2 * bw], seg[..., 2 * bw:3 * bw]
    o1 = 3 * bw
    o2 = o1 + D_DECAY_RANK
    o3 = o2 + D_ICLR_RANK
    wl, al, gl = seg[..., o1:o2], seg[..., o2:o3], seg[..., o3:o3 + D_GATE_RANK]
    w_raw = -jax.nn.softplus(-(w0 + jnp.tanh(wl) @ w2)) - 0.5
    w = jnp.exp(-jnp.exp(w_raw))
    a = jax.nn.sigmoid(a0 + al @ a2)
    g = jax.nn.sigmoid(gl) @ g2

    def heads(z):
        return z.astype(f32).reshape(bsz, seq, D_HEADS, D_HEAD_SIZE)

    kk = heads(k * k_k)
    kk = kk / jnp.maximum(jnp.sqrt(jnp.sum(kk * kk, -1, keepdims=True)), 1e-12)
    k = k * (1.0 + (a - 1.0) * k_a)
    rh, kh, vh, wh, ah = heads(r), heads(k), heads(v), heads(w), heads(a)
    a_vec = -kk
    b_vec = kk * ah

    def step(state, inp):
        rt, wt, kt, vt, at, bt = inp
        sa = jnp.einsum('bhvk,bhk->bhv', state, at)
        state = (state * wt[:, :, None, :] + sa[..., None] * bt[:, :, None, :]
                 + vt[..., None] * kt[:, :, None, :])
        return state, jnp.einsum('bhvk,bhk->bhv', state, rt)

    init = jnp.zeros((bsz, D_HEADS, D_HEAD_SIZE, D_HEAD_SIZE), f32)
    xs = tuple(jnp.moveaxis(z, 1, 0) for z in (rh, wh, kh, vh, a_vec, b_vec))
    _, y = lax.scan(step, init, xs)
    y = jnp.moveaxis(y, 0, 1)
    mu_y = jnp.mean(y, -1, keepdims=True)
    var_y = jnp.mean(jnp.square(y - mu_y), -1, keepdims=True)
    y = ((y - mu_y) * lax.rsqrt(var_y + D_GN_EPS)).reshape(bsz, seq, bw) * gn_w + gn_b
    bonus = jnp.sum(rh * kh * r_k.reshape(D_HEADS, D_HEAD_SIZE), -1, keepdims=True) * vh
    y = (y + bonus.reshape(bsz, seq, bw)) * g
    return y.astype(out_dtype)

def _moe(x, wr_g, br_g, wr_e, br_e, w_gate, w_up, w_down):
    f32 = jnp.float32

    def one_seq(xs):
        lg = (xs @ wr_g).astype(f32) + br_g
        pg = jax.nn.softmax(lg, axis=-1)
        ptop, gsel = lax.top_k(pg, 1)
        le = ((xs @ wr_e).astype(f32) + br_e).reshape(-1, MOE_GROUPS, MOE_PER_GROUP)
        le = jnp.take_along_axis(le, gsel[:, :, None], axis=1)[:, 0]
        lv, esel = lax.top_k(le, MOE_TOPK)
        we = jax.nn.softmax(lv, axis=-1) * ptop
        local = jnp.einsum('sk,ske->se', we, jax.nn.one_hot(esel, MOE_PER_GROUP, dtype=f32))
        gate = (jax.nn.one_hot(gsel[:, 0], MOE_GROUPS, dtype=f32)[:, :, None]
                * local[:, None, :]).reshape(-1, MOE_EXPERTS)
        hg = jnp.einsum('sd,edh->seh', xs, w_gate)
        hu = jnp.einsum('sd,edh->seh', xs, w_up)
        h = jax.nn.silu(hg) * hu * gate[..., None].astype(xs.dtype)
        return jnp.einsum('seh,ehd->sd', h, w_down)

    return lax.map(one_seq, x).astype(x.dtype)

def first_inputs(seed: int = 0) -> dict:
    key = jax.random.key(seed)
    ks = jax.random.split(key, 32)
    f32 = jnp.float32

    def nrm(k, shape, scale):
        return jax.random.normal(k, shape, f32) * scale

    L = DEPTH
    bw = BRANCH_WIDTH
    return {
        "x": nrm(ks[0], (BATCH, SEQ, D_MODEL), 1.0),
        "rpb_table": nrm(ks[1], (RPB_BUCKETS, RPB_HEADS), 0.5),
        "w_in": nrm(ks[2], (L, D_MODEL, IN_WIDTH), D_MODEL ** -0.5),
        "b_kv_gain": 1.0 + nrm(ks[3], (L, B_LATENT), 0.05),
        "b_w_uv": nrm(ks[4], (L, B_HEADS, B_LATENT, HEAD_DIM), B_LATENT ** -0.5),
        "c_a_up": nrm(ks[5], (L, C_GATE_RANK, C_HEADS * C_KEY_DIM), C_GATE_RANK ** -0.5),
        "c_a_bias": nrm(ks[6], (L, C_HEADS * C_KEY_DIM), 0.5),
        "c_norm_gain": 1.0 + nrm(ks[7], (L, bw), 0.05),
        "d_mu": jax.random.uniform(ks[8], (L, D_IN_WIDTH), f32),
        "d_w0": nrm(ks[9], (L, bw), 0.5),
        "d_w2": nrm(ks[10], (L, D_DECAY_RANK, bw), 0.5 * D_DECAY_RANK ** -0.5),
        "d_a0": nrm(ks[11], (L, bw), 0.1),
        "d_a2": nrm(ks[12], (L, D_ICLR_RANK, bw), 0.5 * D_ICLR_RANK ** -0.5),
        "d_g2": nrm(ks[13], (L, D_GATE_RANK, bw), D_GATE_RANK ** -0.5),
        "d_k_k": 0.85 + nrm(ks[14], (L, bw), 0.05),
        "d_k_a": 1.0 + nrm(ks[15], (L, bw), 0.05),
        "d_r_k": nrm(ks[16], (L, bw), 0.1),
        "d_gn_w": 1.0 + nrm(ks[17], (L, bw), 0.05),
        "d_gn_b": nrm(ks[18], (L, bw), 0.01),
        "w_branch": nrm(ks[19], (L, N_BRANCHES, bw, D_MODEL), bw ** -0.5),
        "w_out": nrm(ks[20], (L, D_MODEL, D_MODEL), D_MODEL ** -0.5 * DN_BETA),
        "ln_g": 1.0 + nrm(ks[21], (L, 2, D_MODEL), 0.05),
        "ln_b": nrm(ks[22], (L, 2, D_MODEL), 0.01),
        "router_g": nrm(ks[23], (L, D_MODEL, MOE_GROUPS), D_MODEL ** -0.5),
        "router_g_bias": nrm(ks[24], (L, MOE_GROUPS), 0.01),
        "router_e": nrm(ks[25], (L, D_MODEL, MOE_EXPERTS), D_MODEL ** -0.5),
        "router_e_bias": nrm(ks[26], (L, MOE_EXPERTS), 0.01),
        "moe_w_gate": nrm(ks[27], (L, MOE_EXPERTS, D_MODEL, MOE_HIDDEN), D_MODEL ** -0.5),
        "moe_w_up": nrm(ks[28], (L, MOE_EXPERTS, D_MODEL, MOE_HIDDEN), D_MODEL ** -0.5),
        "moe_w_down": nrm(ks[29], (L, MOE_EXPERTS, MOE_HIDDEN, D_MODEL), MOE_HIDDEN ** -0.5 * DN_BETA),
    }

def first_block(x, rpb_table, w_in, b_kv_gain, b_w_uv, c_a_up, c_a_bias, c_norm_gain,
              d_mu, d_w0, d_w2, d_a0, d_a2, d_g2, d_k_k, d_k_a, d_r_k, d_gn_w, d_gn_b,
              w_branch, w_out, ln_g, ln_b, router_g, router_g_bias, router_e, router_e_bias,
              moe_w_gate, moe_w_up, moe_w_down):
    bsz, seq, _ = x.shape
    for l in range(DEPTH):
        p = _split_in(x @ w_in[l])
        ya = _mixer_a(p["a_q"], p["a_k"], p["a_v"], rpb_table[:, :A_HEADS])
        yb = _mixer_b(p["b_q"], p["b_ckv"], p["b_iq"], p["b_ik"], p["b_iw"],
                      b_kv_gain[l], b_w_uv[l], rpb_table[:, A_HEADS:])
        yc = _mixer_c(p["c_q"], p["c_k"], p["c_v"], p["c_a"], p["c_g"],
                      c_a_up[l], c_a_bias[l], c_norm_gain[l])
        yd = _mixer_d(p["d"], d_mu[l], d_w0[l], d_w2[l], d_a0[l], d_a2[l], d_g2[l],
                      d_k_k[l], d_k_a[l], d_r_k[l], d_gn_w[l], d_gn_b[l])
        ys = jnp.stack([ya.astype(x.dtype), yb.astype(x.dtype), yc.astype(x.dtype), yd.astype(x.dtype)], axis=2)
        gates = jax.nn.sigmoid(p["gate"].reshape(bsz, seq, N_BRANCHES, D_MODEL))
        merged = jnp.sum(gates * jnp.einsum('bsnc,ncd->bsnd', ys, w_branch[l]), axis=2)
        x = _layer_norm(DN_ALPHA * x + merged @ w_out[l], ln_g[l, 0], ln_b[l, 0])
        y = _moe(x, router_g[l], router_g_bias[l], router_e[l], router_e_bias[l],
                 moe_w_gate[l], moe_w_up[l], moe_w_down[l])
        x = _layer_norm(DN_ALPHA * x + y, ln_g[l, 1], ln_b[l, 1])
    return x


DEPTH_2 = 2

GRID_W = 64
CTX_LEN = 256
A_HEADS_2 = 8
A_KV_HEADS = 2
A_GROUP = A_HEADS_2 // A_KV_HEADS
B_HEADS_2 = 8
NA_ROWS = 8
NA_COLS = 16
ROPE_THETA = 10000.0
MLA_HEADS = 16
MLA_Q_LORA = 768
MLA_KV_LORA = 256
MLA_NOPE_DIM = 64
MLA_ROPE_DIM = 32
MLA_V_DIM = 64
D_FF = 2816
CONV_WIDTH = 3
N_MOD = 6
EPS = 1e-6
DEEPNORM_ALPHA = (2 * DEPTH_2) ** 0.25
DEEPNORM_BETA = (8 * DEPTH_2) ** -0.25
HEAD_SCALE = HEAD_DIM ** -0.5
MLA_SCALE = (MLA_NOPE_DIM + MLA_ROPE_DIM) ** -0.5
_A_Q = A_HEADS_2 * HEAD_DIM
_A_KV = A_KV_HEADS * HEAD_DIM
_B_W = B_HEADS_2 * HEAD_DIM
EVEN_IN_DIM = _A_Q + 2 * _A_KV + 3 * _B_W
EVEN_SPLITS = (_A_Q, _A_Q + _A_KV, _A_Q + 2 * _A_KV, _A_Q + 2 * _A_KV + _B_W, _A_Q + 2 * _A_KV + 2 * _B_W)
EVEN_OUT_DIM = (A_HEADS_2 + B_HEADS_2) * HEAD_DIM
ODD_IN_DIM = MLA_Q_LORA + MLA_KV_LORA + MLA_ROPE_DIM
ODD_OUT_DIM = MLA_HEADS * MLA_V_DIM


def _layer_norm_2(x, g, b):
    xf = x.astype(jnp.float32)
    mu = jnp.mean(xf, axis=-1, keepdims=True)
    var = jnp.mean(jnp.square(xf - mu), axis=-1, keepdims=True)
    return ((xf - mu) * lax.rsqrt(var + EPS) * g + b).astype(x.dtype)

def _rms_norm_2(x, g):
    xf = x.astype(jnp.float32)
    return (xf * lax.rsqrt(jnp.mean(jnp.square(xf), axis=-1, keepdims=True) + EPS) * g).astype(x.dtype)

def _axial_rope(length, rot_dim, dtype):
    pos = jnp.arange(length, dtype=jnp.int32)
    rows = (pos // GRID_W).astype(jnp.float32)
    cols = (pos % GRID_W).astype(jnp.float32)
    axis_dim = rot_dim // 2
    inv = ROPE_THETA ** (-jnp.arange(0, axis_dim, 2, dtype=jnp.float32) / axis_dim)
    ang = jnp.concatenate([rows[:, None] * inv, cols[:, None] * inv], axis=-1)
    return jnp.cos(ang).astype(dtype), jnp.sin(ang).astype(dtype)

def _rope(x, cos, sin):
    xp = x.reshape(x.shape[:-1] + (x.shape[-1] // 2, 2))
    x1, x2 = xp[..., 0], xp[..., 1]
    return jnp.stack([x1 * cos - x2 * sin, x1 * sin + x2 * cos], axis=-1).reshape(x.shape)

def _heads(t, n, d):
    b, length, _ = t.shape
    return t.reshape(b, length, n, d).transpose(0, 2, 1, 3)

def _merge_heads(t):
    b, h, length, d = t.shape
    return t.transpose(0, 2, 1, 3).reshape(b, length, h * d)

def _dense_attention(q, k, v, kc, vc, scale):
    b, g, r, length, dk = q.shape
    nb = length // Q_BLOCK
    qb = jnp.moveaxis(q.reshape(b, g, r, nb, Q_BLOCK, dk), 3, 0)

    def one_block(qblk):
        s = jnp.concatenate([jnp.einsum('bgrqd,bgkd->bgrqk', qblk, k),
                             jnp.einsum('bgrqd,bgcd->bgrqc', qblk, kc)], axis=-1)
        p = jax.nn.softmax(s.astype(jnp.float32) * scale, axis=-1).astype(v.dtype)
        return (jnp.einsum('bgrqk,bgkd->bgrqd', p[..., :length], v)
                + jnp.einsum('bgrqc,bgcd->bgrqd', p[..., length:], vc))

    o = lax.map(one_block, qb)
    return jnp.moveaxis(o, 0, 3).reshape(b, g, r, length, -1)

def _context_attention(q, k, v, scale):
    s = jnp.einsum('bgrqd,bgkd->bgrqk', q, k).astype(jnp.float32) * scale
    p = jax.nn.softmax(s, axis=-1).astype(v.dtype)
    return jnp.einsum('bgrqk,bgkd->bgrqd', p, v)

def _neighbourhood_attention(q, k, v, kc, vc, rpb, scale):
    b, h, length, d = q.shape
    rows = length // GRID_W
    wr = min(NA_ROWS, rows)
    qg = q.reshape(b, h, rows, GRID_W, d)
    kg = k.reshape(b, h, rows, GRID_W, d)
    vg = v.reshape(b, h, rows, GRID_W, d)
    col = jnp.arange(GRID_W, dtype=jnp.int32)
    col_start = jnp.clip(col - NA_COLS // 2, 0, GRID_W - NA_COLS)
    col_idx = col_start[:, None] + jnp.arange(NA_COLS, dtype=jnp.int32)[None, :]
    col_bias = rpb[:, :, col_idx - col[:, None] + (NA_COLS - 1)].astype(jnp.float32)
    n_nb = wr * NA_COLS

    def one_row(args):
        r, q_row = args
        rs = jnp.clip(r - wr // 2, 0, rows - wr)
        k_win = lax.dynamic_slice_in_dim(kg, rs, wr, axis=2)[:, :, :, col_idx]
        v_win = lax.dynamic_slice_in_dim(vg, rs, wr, axis=2)[:, :, :, col_idx]
        row_off = rs + jnp.arange(wr, dtype=jnp.int32) - r + (NA_ROWS - 1)
        bias = col_bias[:, row_off].transpose(0, 2, 1, 3)
        s_nb = jnp.einsum('bhqd,bhrqkd->bhqrk', q_row, k_win).astype(jnp.float32) * scale + bias[None]
        s_ctx = jnp.einsum('bhqd,bhcd->bhqc', q_row, kc).astype(jnp.float32) * scale
        p = jax.nn.softmax(jnp.concatenate([s_nb.reshape(b, h, GRID_W, n_nb), s_ctx], axis=-1), axis=-1).astype(v.dtype)
        p_nb = p[..., :n_nb].reshape(b, h, GRID_W, wr, NA_COLS)
        return (jnp.einsum('bhqrk,bhrqkd->bhqd', p_nb, v_win)
                + jnp.einsum('bhqc,bhcd->bhqd', p[..., n_nb:], vc))

    out = lax.map(one_row, (jnp.arange(rows, dtype=jnp.int32), jnp.moveaxis(qg, 2, 0)))
    return jnp.moveaxis(out, 0, 2).reshape(b, h, length, d)

def _even_mixer(h, hc, w_in, q_gain, k_gain, rpb, w_out, need_ctx):
    b, length, _ = h.shape
    cos, sin = _axial_rope(length, HEAD_DIM, h.dtype)

    def project(t):
        qa, ka, va, qb, kb, vb = jnp.split(t @ w_in, EVEN_SPLITS, axis=-1)
        return (_rms_norm_2(_heads(qa, A_HEADS_2, HEAD_DIM), q_gain),
                _rms_norm_2(_heads(ka, A_KV_HEADS, HEAD_DIM), k_gain),
                _heads(va, A_KV_HEADS, HEAD_DIM),
                _heads(qb, B_HEADS_2, HEAD_DIM), _heads(kb, B_HEADS_2, HEAD_DIM), _heads(vb, B_HEADS_2, HEAD_DIM))

    qa, ka, va, qb, kb, vb = project(h)
    qac, kac, vac, qbc, kbc, vbc = project(hc)
    qa = _rope(qa, cos, sin)
    ka = _rope(ka, cos, sin)
    ya = _dense_attention(qa.reshape(b, A_KV_HEADS, A_GROUP, length, HEAD_DIM), ka, va, kac, vac,
                          HEAD_SCALE).reshape(b, A_HEADS_2, length, HEAD_DIM)
    yb = _neighbourhood_attention(qb, kb, vb, kbc, vbc, rpb, HEAD_SCALE)
    y = _merge_heads(jnp.concatenate([ya, yb], axis=1)) @ w_out
    yc = None
    if need_ctx:
        lc = hc.shape[1]
        yac = _context_attention(qac.reshape(b, A_KV_HEADS, A_GROUP, lc, HEAD_DIM), kac, vac,
                                 HEAD_SCALE).reshape(b, A_HEADS_2, lc, HEAD_DIM)
        ybc = _context_attention(qbc[:, :, None], kbc, vbc, HEAD_SCALE)[:, :, 0]
        yc = _merge_heads(jnp.concatenate([yac, ybc], axis=1)) @ w_out
    return y, yc

def _odd_mixer(h, hc, w_in, cq_gain, ckv_gain, w_uq, w_ukv, w_out, need_ctx):
    b, length, _ = h.shape
    cos, sin = _axial_rope(length, MLA_ROPE_DIM, h.dtype)

    def compress(t):
        c_q, c_kv, k_r = jnp.split(t @ w_in, (MLA_Q_LORA, MLA_Q_LORA + MLA_KV_LORA), axis=-1)
        return _rms_norm_2(c_q, cq_gain), _rms_norm_2(c_kv, ckv_gain), k_r

    def up_q(c_q):
        return jnp.split(_heads(c_q @ w_uq, MLA_HEADS, MLA_NOPE_DIM + MLA_ROPE_DIM), (MLA_NOPE_DIM,), axis=-1)

    def up_kv(c_kv, k_r):
        k_nope, v = jnp.split(_heads(c_kv @ w_ukv, MLA_HEADS, MLA_NOPE_DIM + MLA_V_DIM), (MLA_NOPE_DIM,), axis=-1)
        k_shared = jnp.broadcast_to(k_r[:, None], k_nope.shape[:-1] + (MLA_ROPE_DIM,))
        return jnp.concatenate([k_nope, k_shared], axis=-1), v

    c_q, c_kv, k_r = compress(h)
    cc_q, cc_kv, kc_r = compress(hc)
    q_nope, q_rope = up_q(c_q)
    q = jnp.concatenate([q_nope, _rope(q_rope, cos, sin)], axis=-1)
    k, v = up_kv(c_kv, _rope(k_r, cos, sin))
    kc, vc = up_kv(cc_kv, kc_r)
    y = _merge_heads(_dense_attention(q[:, :, None], k, v, kc, vc, MLA_SCALE)[:, :, 0]) @ w_out
    yc = None
    if need_ctx:
        qc = jnp.concatenate(up_q(cc_q), axis=-1)
        yc = _merge_heads(_context_attention(qc[:, :, None], kc, vc, MLA_SCALE)[:, :, 0]) @ w_out
    return y, yc

def _conv_ffn(h, w_up, conv_w, conv_b, w_down):
    gate, val = jnp.split(h @ w_up, 2, axis=-1)
    gate = lax.conv_general_dilated(gate, conv_w[:, None, :], (1,), ((CONV_WIDTH // 2, CONV_WIDTH // 2),),
                                    dimension_numbers=('NWC', 'WIO', 'NWC'), feature_group_count=D_FF) + conv_b
    return (jax.nn.silu(gate) * val) @ w_down

def _adaln(cond, w, b):
    return jnp.split(jax.nn.silu(cond) @ w + b, N_MOD, axis=-1)

def second_inputs(seed: int = 0) -> dict:
    key = jax.random.key(seed)
    ks = iter(jax.random.split(key, 40))

    def nrm(shape, scale):
        return jax.random.normal(next(ks), shape, jnp.float32) * scale

    def gain(n):
        return 1.0 + nrm((n,), 0.1)

    d = D_MODEL
    return {
        'x': nrm((BATCH, SEQ, d), 1.0),
        'c': nrm((BATCH, d), 1.0),
        'ctx': nrm((BATCH, CTX_LEN, d), 1.0),
        'c_ctx': nrm((d,), 1.0),
        'l0_w_ada': nrm((d, N_MOD * d), 0.5 * d ** -0.5),
        'l0_b_ada': nrm((N_MOD * d,), 0.1),
        'l0_w_in': nrm((d, EVEN_IN_DIM), d ** -0.5),
        'l0_q_gain': gain(HEAD_DIM),
        'l0_k_gain': gain(HEAD_DIM),
        'l0_rpb': nrm((B_HEADS_2, 2 * NA_ROWS - 1, 2 * NA_COLS - 1), 0.5),
        'l0_w_out': nrm((EVEN_OUT_DIM, d), DEEPNORM_BETA * EVEN_OUT_DIM ** -0.5),
        'l0_ln1_g': gain(d),
        'l0_ln1_b': nrm((d,), 0.02),
        'l0_w_up': nrm((d, 2 * D_FF), d ** -0.5),
        'l0_conv_w': nrm((CONV_WIDTH, D_FF), CONV_WIDTH ** -0.5),
        'l0_conv_b': nrm((D_FF,), 0.02),
        'l0_w_down': nrm((D_FF, d), DEEPNORM_BETA * D_FF ** -0.5),
        'l0_ln2_g': gain(d),
        'l0_ln2_b': nrm((d,), 0.02),
        'l1_w_ada': nrm((d, N_MOD * d), 0.5 * d ** -0.5),
        'l1_b_ada': nrm((N_MOD * d,), 0.1),
        'l1_w_in': nrm((d, ODD_IN_DIM), d ** -0.5),
        'l1_cq_gain': gain(MLA_Q_LORA),
        'l1_ckv_gain': gain(MLA_KV_LORA),
        'l1_w_uq': nrm((MLA_Q_LORA, MLA_HEADS * (MLA_NOPE_DIM + MLA_ROPE_DIM)), MLA_Q_LORA ** -0.5),
        'l1_w_ukv': nrm((MLA_KV_LORA, MLA_HEADS * (MLA_NOPE_DIM + MLA_V_DIM)), MLA_KV_LORA ** -0.5),
        'l1_w_out': nrm((ODD_OUT_DIM, d), DEEPNORM_BETA * ODD_OUT_DIM ** -0.5),
        'l1_ln1_g': gain(d),
        'l1_ln1_b': nrm((d,), 0.02),
        'l1_w_up': nrm((d, 2 * D_FF), d ** -0.5),
        'l1_conv_w': nrm((CONV_WIDTH, D_FF), CONV_WIDTH ** -0.5),
        'l1_conv_b': nrm((D_FF,), 0.02),
        'l1_w_down': nrm((D_FF, d), DEEPNORM_BETA * D_FF ** -0.5),
        'l1_ln2_g': gain(d),
        'l1_ln2_b': nrm((d,), 0.02),
    }

def second_block(x, c, ctx, c_ctx,
              l0_w_ada, l0_b_ada, l0_w_in, l0_q_gain, l0_k_gain, l0_rpb, l0_w_out, l0_ln1_g, l0_ln1_b,
              l0_w_up, l0_conv_w, l0_conv_b, l0_w_down, l0_ln2_g, l0_ln2_b,
              l1_w_ada, l1_b_ada, l1_w_in, l1_cq_gain, l1_ckv_gain, l1_w_uq, l1_w_ukv, l1_w_out, l1_ln1_g, l1_ln1_b,
              l1_w_up, l1_conv_w, l1_conv_b, l1_w_down, l1_ln2_g, l1_ln2_b):
    layers = (
        dict(w_ada=l0_w_ada, b_ada=l0_b_ada, w_in=l0_w_in, q_gain=l0_q_gain, k_gain=l0_k_gain, rpb=l0_rpb,
             w_out=l0_w_out, ln1_g=l0_ln1_g, ln1_b=l0_ln1_b, w_up=l0_w_up, conv_w=l0_conv_w, conv_b=l0_conv_b,
             w_down=l0_w_down, ln2_g=l0_ln2_g, ln2_b=l0_ln2_b),
        dict(w_ada=l1_w_ada, b_ada=l1_b_ada, w_in=l1_w_in, cq_gain=l1_cq_gain, ckv_gain=l1_ckv_gain,
             w_uq=l1_w_uq, w_ukv=l1_w_ukv, w_out=l1_w_out, ln1_g=l1_ln1_g, ln1_b=l1_ln1_b, w_up=l1_w_up,
             conv_w=l1_conv_w, conv_b=l1_conv_b, w_down=l1_w_down, ln2_g=l1_ln2_g, ln2_b=l1_ln2_b),
    )
    xc = ctx
    for i in range(DEPTH_2):
        p = layers[i]
        need_ctx = i < DEPTH_2 - 1
        sh1, sc1, g1, sh2, sc2, g2 = [m[:, None, :] for m in _adaln(c, p['w_ada'], p['b_ada'])]
        csh1, csc1, cg1, csh2, csc2, cg2 = _adaln(c_ctx, p['w_ada'], p['b_ada'])
        h = x * (1.0 + sc1) + sh1
        hc = xc * (1.0 + csc1) + csh1
        if i % 2 == 0:
            y, yc = _even_mixer(h, hc, p['w_in'], p['q_gain'], p['k_gain'], p['rpb'], p['w_out'], need_ctx)
        else:
            y, yc = _odd_mixer(h, hc, p['w_in'], p['cq_gain'], p['ckv_gain'], p['w_uq'], p['w_ukv'],
                               p['w_out'], need_ctx)
        x = _layer_norm_2(DEEPNORM_ALPHA * x + g1 * y, p['ln1_g'], p['ln1_b'])
        h = x * (1.0 + sc2) + sh2
        x = _layer_norm_2(DEEPNORM_ALPHA * x + g2 * _conv_ffn(h, p['w_up'], p['conv_w'], p['conv_b'], p['w_down']),
                        p['ln2_g'], p['ln2_b'])
        if need_ctx:
            xc = _layer_norm_2(DEEPNORM_ALPHA * xc + cg1 * yc, p['ln1_g'], p['ln1_b'])
            hc = xc * (1.0 + csc2) + csh2
            xc = _layer_norm_2(DEEPNORM_ALPHA * xc + cg2 * _conv_ffn(hc, p['w_up'], p['conv_w'], p['conv_b'], p['w_down']),
                             p['ln2_g'], p['ln2_b'])
    return x


def setup_inputs(seed=0):
    out = dict(first_inputs(seed))
    for name, value in second_inputs(seed + 1).items():
        if name != "x":
            out[name + "_2"] = value
    return out


def reference(
    x, rpb_table, w_in, b_kv_gain, b_w_uv, c_a_up, c_a_bias, c_norm_gain, d_mu, d_w0, d_w2,
    d_a0, d_a2, d_g2, d_k_k, d_k_a, d_r_k, d_gn_w, d_gn_b, w_branch, w_out, ln_g, ln_b,
    router_g, router_g_bias, router_e, router_e_bias, moe_w_gate, moe_w_up, moe_w_down, c_2,
    ctx_2, c_ctx_2, l0_w_ada_2, l0_b_ada_2, l0_w_in_2, l0_q_gain_2, l0_k_gain_2, l0_rpb_2,
    l0_w_out_2, l0_ln1_g_2, l0_ln1_b_2, l0_w_up_2, l0_conv_w_2, l0_conv_b_2, l0_w_down_2,
    l0_ln2_g_2, l0_ln2_b_2, l1_w_ada_2, l1_b_ada_2, l1_w_in_2, l1_cq_gain_2, l1_ckv_gain_2,
    l1_w_uq_2, l1_w_ukv_2, l1_w_out_2, l1_ln1_g_2, l1_ln1_b_2, l1_w_up_2, l1_conv_w_2,
    l1_conv_b_2, l1_w_down_2, l1_ln2_g_2, l1_ln2_b_2,
):
    x = first_block(
        x, rpb_table, w_in, b_kv_gain, b_w_uv, c_a_up, c_a_bias, c_norm_gain, d_mu, d_w0, d_w2,
        d_a0, d_a2, d_g2, d_k_k, d_k_a, d_r_k, d_gn_w, d_gn_b, w_branch, w_out, ln_g, ln_b,
        router_g, router_g_bias, router_e, router_e_bias, moe_w_gate, moe_w_up, moe_w_down,
    )
    return second_block(
        x, c_2, ctx_2, c_ctx_2, l0_w_ada_2, l0_b_ada_2, l0_w_in_2, l0_q_gain_2, l0_k_gain_2,
        l0_rpb_2, l0_w_out_2, l0_ln1_g_2, l0_ln1_b_2, l0_w_up_2, l0_conv_w_2, l0_conv_b_2,
        l0_w_down_2, l0_ln2_g_2, l0_ln2_b_2, l1_w_ada_2, l1_b_ada_2, l1_w_in_2, l1_cq_gain_2,
        l1_ckv_gain_2, l1_w_uq_2, l1_w_ukv_2, l1_w_out_2, l1_ln1_g_2, l1_ln1_b_2, l1_w_up_2,
        l1_conv_w_2, l1_conv_b_2, l1_w_down_2, l1_ln2_g_2, l1_ln2_b_2,
    )


_drawn_inputs = setup_inputs


def setup_inputs(seed=0):
    import zlib

    import numpy as np

    out = dict(_drawn_inputs(seed))
    spreads = {}
    factors = {'b_kv_gain': 5.534,
     'c_a_up': 2.863,
     'c_norm_gain': 4.887,
     'd_w2': 4.626,
     'd_a0': 6.289,
     'd_k_k': 8.0,
     'd_k_a': 4.491,
     'd_gn_w': 6.473,
     'd_gn_b': 8.0,
     'ln_b': 3.063,
     'router_g_bias': 8.0,
     'router_e_bias': 7.97,
     'ctx_2': 5.646,
     'l0_q_gain_2': 8.0,
     'l0_k_gain_2': 8.0,
     'l0_rpb_2': 8.0,
     'l0_ln1_b_2': 2.796,
     'l0_conv_b_2': 8.0,
     'l0_ln2_b_2': 2.796,
     'l1_cq_gain_2': 8.0,
     'l1_ckv_gain_2': 8.0,
     'l1_w_uq_2': 5.625,
     'l1_ln1_b_2': 2.926,
     'l1_conv_b_2': 36.273,
     'l1_ln2_b_2': 2.868}
    for name, (base, spread) in spreads.items():
        noise = np.random.default_rng([zlib.crc32(name.encode()), seed]).standard_normal(out[name].shape)
        drawn = base * np.exp(spread * noise) if base else spread * noise
        out[name] = __import__('jax').numpy.asarray(drawn.astype(out[name].dtype))
    for name, factor in factors.items():
        out[name] = (out[name] * factor).astype(out[name].dtype)
    return out
```

```python
import math
from contextlib import ExitStack

import numpy as np

import concourse.bass as bass
from concourse import mybir

F32 = mybir.dt.float32
ALU = mybir.AluOpType
ACT = mybir.ActivationFunctionType
AX = mybir.AxisListType

P = 128
D = 1024
KC = D // P
S = 256
NBANK = 8
RING = 6
BLOCKS = 16
TILE = BLOCKS * P
NEG = -1e30
TAKEN = -3e38
ALPHA1 = 2.0 ** 0.25
ALPHA2 = 4.0 ** 0.25
EXPERTS = 32
FF = 22
CH = 64
NCH = S // CH
KEEP = 64
W_DECAY = math.exp(-0.5)

IN_NAMES = (("a_q", 256), ("a_k", 256), ("a_v", 256), ("b_q", 256), ("b_ckv", 64), ("b_iq", 256), ("b_ik", 32),
            ("b_iw", 8), ("c_q", 128), ("c_k", 128), ("c_v", 256), ("c_a", 16), ("c_g", 256), ("d", 832),
            ("gate", 4096))
IN_OFF = {}
_o = 0
for _n, _w in IN_NAMES:
    IN_OFF[_n] = _o
    _o += _w
IN_BLOCKS = ["iq0", "iq1", "ik", "iw", "ckv", "bq0", "bq1", "small", "dr0", "dr1", "dk0", "dk1", "dv0", "dv1",
             "cq", "ck", "cv0", "cv1", "cg0", "cg1", "aq0", "aq1", "ak0", "ak1", "av0", "av1"]
R_W, R_A, R_G, R_C = 0, 32, 64, 96


def stream_plan():
    order = [("in", 13), ("ada0", 24), ("ada1", 24), ("merge", 20), ("out", 4)]
    order += [("moe", 3 * EXPERTS)]
    order += [("l0in", 9), ("l0out", 4), ("l0up", 22), ("l0down", 11)]
    order += [("l1in", 5), ("l1uq", 6), ("l1ukv", 2), ("l1out", 4), ("l1up", 22), ("l1down", 11)]
    first, at = {}, 0
    for name, n in order:
        first[name] = at
        at += n
    return first, at


def moe_tiles():
    tiles = []
    for e in range(EXPERTS):
        tiles += [("gate", e), ("up", e)]
        if e:
            tiles.append(("down", e - 1))
    return tiles + [("down", EXPERTS - 1)]


def columns(items):
    at, out = 0, {}
    for name, n in items:
        out[name] = (at, n)
        at += n
    return out, at


CONST_ITEMS = [("ident", 128), ("ones", 128), ("blockones", 128), ("zeros", 128), ("rot", 128),
               ("cos64", 256), ("sin64", 256), ("cosm", 256), ("sinm", 256), ("buckets", 512),
               ("na_mask", 256), ("upper", 64), ("upper_incl", 64), ("lower", 64), ("diag16", 64), ("eye64", 64),
               ("heads_c", 256), ("causal", 512), ("scan_ones", 64)]
PARAM_ITEMS = [("kv_gain", 1), ("c_a_bias", 1), ("c_norm_gain", 2), ("d_mu", 7), ("d_w0", 2), ("d_a0", 2),
               ("d_k_k", 2), ("d_k_a", 2), ("d_r_k", 2), ("d_gn_w", 2), ("d_gn_b", 2),
               ("ln1g", 8), ("ln2g", 8), ("ln1b", 8), ("ln2b", 8),
               ("bada0", 48), ("bada1", 48), ("q_gain", 1), ("k_gain", 1),
               ("l0ln1g", 8), ("l0ln1b", 8), ("l0ln2g", 8), ("l0ln2b", 8),
               ("l1ln1g", 8), ("l1ln1b", 8), ("l1ln2g", 8), ("l1ln2b", 8),
               ("l0conv", 66), ("l0convb", 22), ("l1conv", 66), ("l1convb", 22),
               ("cq_gain", 6), ("ckv_gain", 2), ("cond", 16),
               ("lora", 256), ("w_uv", 256), ("router", 288), ("router_bias", 36), ("rpb_rows", 8)]
CONST, NCONST = columns(CONST_ITEMS)
PARAM, NPARAM = columns(PARAM_ITEMS)


def build(nc, wall, consts, params, xin, ctxin, rpb_pad, out, upto=99):
    first, n_tiles = stream_plan()
    with ExitStack() as ctx:
        def sb(name, shape):
            return ctx.enter_context(nc.sbuf_tensor(name, shape, F32))

        sems = {}

        def sem(name):
            if name not in sems:
                sems[name] = ctx.enter_context(nc.semaphore(name))
            return sems[name]

        ring = sb("ring", [P, RING, TILE])
        con = sb("con", [P, NCONST])
        par = sb("par", [P, NPARAM])
        XC = sb("XC", [P, KC, 2 * S])
        BIG = sb("BIG", [P, 3 * 4096])
        MOD = sb("MOD", [P, 2, 48, 2])
        SC1 = sb("SC1", [P, 2, 2, 8, 2])
        SV = sb("SV", [P, 96])
        arena_n = 17472
        AR = sb("AR", [P, arena_n])
        ps = [ctx.enter_context(nc.psum_tensor(f"bank{b}", [P, 512], F32))[:, :] for b in range(NBANK)]

        def c_(name):
            o, n = CONST[name]
            return con[:, o:o + n]

        def p_(name):
            o, n = PARAM[name]
            return par[:, o:o + n]

        class Arena:

            def __init__(self, region, size, start=0):
                self.region, self.size, self.at = region, size, start

            def take(self, *shape):
                n = int(np.prod(shape))
                a = self.region[:, self.at:self.at + n]
                self.at += n
                assert self.at <= self.size, (self.at, self.size)
                if len(shape) == 1:
                    return a
                names = "abcde"[:len(shape)]
                return a.rearrange(f"p ({' '.join(names)}) -> p {' '.join(names)}",
                                   **{k: v for k, v in zip(names[1:], shape[1:])})

        Z = BIG[:, 0:4096]
        SQ = BIG[:, 4096:8192]
        HB = BIG[:, 8192:12288]
        X1 = XC[:, :, 0:S]

        a1 = Arena(AR, arena_n)
        F = {}
        for name, n in (("iq", 2), ("ik", 1), ("ckv", 1), ("bq", 2), ("cq", 1), ("ck", 1), ("cg", 2), ("aq", 2),
                        ("ak", 2)):
            F[name] = a1.take(n, S)
        cv = a1.take(2, 256)
        av = a1.take(2, 256)
        vb = a1.take(2, 256)
        iw = a1.take(2, 8)
        dS = a1.take(7, S)
        ysT = a1.take(4, 2, S)
        small_act = a1.take(S)
        rows8 = a1.take(512)
        DZ = {n: a1.take(2, S) for n in ("w", "a", "g")}
        c_z = a1.take(S)
        a1_common = a1.at
        dF = a1.take(7, S + 1)
        bA = Arena(BIG, 12288)
        bias1 = bA.take(8, 2, S)
        att1_L = bA.take(3, 512)
        att1_P = bA.take(3, 512)
        att1_PT = bA.take(3, 4, P)
        rel = bA.take(2, 2, S)
        score = bA.take(2, S)
        work = bA.take(2, 2, S)
        top8 = bA.take(2, 8)
        selm = bA.take(2, S)

        cC = Arena(BIG, 12288)
        C = {n: cC.take(S) for n in ("zb", "ab", "ln", "la", "cum", "ec", "en", "ed", "qd", "ki", "kd")}
        c_kdt = cC.take(2, P)
        c_att = cC.take(4, 2, CH)
        c_state = cC.take(3, S)
        c_sm = cC.take(3, S)
        c_o = cC.take(2, S)
        c_sq = cC.take(2, S)
        bD = Arena(BIG, 12288)
        DD = {n: bD.take(2, S) for n in ("lw", "cum", "cm1", "e1", "e2", "e3", "kk", "kp", "b", "Bh", "Kh", "t")}
        Ah = bD.take(2, S)
        Rh = bD.take(2, S)
        yT = bD.take(2, S)
        bn = bD.take(2, S)
        dU = Arena(BIG, 12288, bD.at)
        cU = Arena(AR, arena_n, a1_common)
        U = {n: dU.take(8, CH) for n in ("N", "A", "GRB", "GAK", "GRK", "Vt", "Bt", "Kt")}
        U |= {n: cU.take(8, CH) for n in ("D", "Dt", "D2", "D2t", "D4", "D4t", "Z", "W", "Lo")}
        U["D8"], U["D8t"] = U["D"], U["Dt"]
        U["Pm"], U["Pt"], U["P2t"], U["Y1"], U["T"] = U["D2"], U["D2t"], U["D4"], U["D4t"], U["Lo"]
        x_u = cU.take(2, 2, CH)
        m_st = cU.take(5, 2, CH)
        cM = Arena(AR, arena_n, a1_common)
        tmpm = cM.take(2, 2, 2, S)
        gates = cM.take(2, 4, S)
        mergedT = HB[:, 0:2048].rearrange("p (k t) -> p k t", k=KC)

        def ln_bufs(n):
            z = Z[:, 0:KC * n].rearrange("p (k t) -> p k t", k=KC)
            sq = SQ[:, 0:KC * n].rearrange("p (k t) -> p k t", k=KC)
            return z, sq

        lnst = sb("lnst", [P, 3, 512])

        aM = Arena(AR, arena_n)
        gate_bc = aM.take(EXPERTS, S)
        m_sg = aM.take(2, 2, S)
        m_t = aM.take(2, 2, S)
        m_h = aM.take(2, 2, S)
        lg = aM.take(2, 36)
        rt = aM.take(2, 12, 32)
        gateT = aM.take(S)

        a2 = Arena(AR, arena_n)
        Q0 = a2.take(5, 512)
        qb = a2.take(4, 512)
        kb = a2.take(4, 512)
        V0 = a2.take(4, 640)
        yT0 = a2.take(8, 512)
        na_bias = a2.take(8, 2, S)
        H = HB.rearrange("p (k t) -> p k t", k=KC)
        aP = Arena(SQ, 4096)
        att2_P = aP.take(3, 512)
        att2_PT = aP.take(3, 4, P)
        aL = Arena(Z, 4096)
        att2_L = aL.take(3, 512)
        tq = aL.take(5, 512)
        tq2 = aP.region[:, 0:2560].rearrange("p (a b) -> p a b", a=5)

        aF = Arena(AR, arena_n)
        u_ff = aF.take(FF, 512)
        gp = aF.take(2, 2, S + 2)
        cg_ = aF.take(2, 512)
        sg_ = aF.take(2, 512)
        tff = aF.take(2, 512)

        a3 = Arena(AR, arena_n)
        cq1 = a3.take(6, S)
        ckv1 = a3.take(2, 512)
        kr1 = a3.take(512)
        sq1 = a3.take(8, 512)
        q1 = a3.take(16, S)
        V1 = a3.take(4, 1024)
        kT1 = a3.take(2, 512)
        yT1 = Z[:, 2048:4096].rearrange("p (k t) -> p k t", k=KC)
        tq1 = SQ[:, 3072:4096].rearrange("p (a b) -> p a b", a=2)

        scr_t5 = nc.dram_tensor("t5_rows", [8, P, 512], F32, kind="Internal").ap()
        scr_na = nc.dram_tensor("na_rows", [8, CH, 896], F32, kind="Internal").ap()
        scr_gate = nc.dram_tensor("gate_rows", [EXPERTS, S], F32, kind="Internal").ap()

        bank_ready = [sem(f"bank_ready{b}") for b in range(NBANK)]
        bank_free = [sem(f"bank_free{b}") for b in range(NBANK)]
        w_ready = [sem(f"weights_in_slot{s}") for s in range(RING)]
        w_used = sem("weight_tiles_used")

        def spec(q, k, v, o, bias=None, nk=S, scale=0.125):
            return dict(q=q, k=k, v=v, o=o, bias=bias, nk=nk, scale=scale)

        att1, att2, att3 = [], [], []
        for br, (fq, fk, fv) in enumerate(((F["aq"], F["ak"], av), (F["bq"], None, vb))):
            for h in range(4):
                r = slice(64 * (h % 2), 64 * (h % 2) + 64)
                for i in range(2):
                    k = fk[r, h // 2, :] if br == 0 else F["ckv"][r, 0, :]
                    att1.append(spec(fq[r, h // 2, i * P:(i + 1) * P], k,
                                     [fv[:, t, h * 64:(h + 1) * 64] for t in range(2)],
                                     ysT[r, br, h // 2, i * P:(i + 1) * P], bias=bias1[:, 4 * br + h, i, :]))
        for h in range(16):
            r = slice(64 * (h % 2), 64 * (h % 2) + 64)
            for i in range(4):
                if h < 8:
                    j, g = h // 2, h % 2
                    q, kk, v0 = Q0[r, j, :], Q0[r, 4, :], 64 * g
                else:
                    j = (h - 8) // 2
                    q, kk, v0 = qb[r, j, :], kb[r, j, :], P + 64 * (h - 8)
                y = yT0[r, h // 2, i * P:(i + 1) * P]
                if i < 2:
                    b = na_bias[:, h - 8, i, :] if h >= 8 else None
                    att2.append(spec(q[:, i * P:(i + 1) * P], kk, [V0[:, t, v0:v0 + 64] for t in range(4)], y, b, 512))
                else:
                    att2.append(spec(q[:, i * P:(i + 1) * P], kk[:, S:2 * S],
                                     [V0[:, t, v0:v0 + 64] for t in (2, 3)], y, None, S))
        for h in range(16):
            for i in range(2):
                att3.append(spec(q1[0:96, h, i * P:(i + 1) * P], kT1[0:96, h % 2, :],
                                 [V1[:, t, h * 64:(h + 1) * 64] for t in range(4)],
                                 yT1[64 * (h % 2):64 * (h % 2) + 64, h // 2, i * P:(i + 1) * P],
                                 None, 512, 96 ** -0.5))

        def att_order(st, n):
            for i in range(n + 3):
                if st == "att3" and i % 2 == 0 and i < n:
                    yield ("kT", i // 2)
                if i < n:
                    yield (st, "S", i)
                if 0 <= i - 2 < n:
                    yield (st, "T", i - 2)
                if 0 <= i - 3 < n:
                    yield (st, "O", i - 3)

        before_ = {"att1": 0, "att2": len(att1), "att3": len(att1) + len(att2)}
        exp_before = {"att1": 0, "att2": len(att1), "att3": len(att1) + 16}

        def nth(which):
            return KC * "abcdef".index(which)

        FAM1 = ["N", "A", "GRB", "GAK", "GRK", "Vt", "Bt", "Kt"]
        FAM2 = ["D2", "D2t", "Z1", "W1", "D4", "D4t", "Z2", "W2", "D8", "D8t", "Z3", "W3", "Pm", "Pt", "P2t", "Y1", "T"]
        plan = []

        def add(*names):
            plan.extend(names)

        add("t5")
        add(*[("in", b) for b in range(26)])
        add("ckvms", "vb")
        add(*[("ix", i, b) for i in range(2) for b in range(4)])
        add("dw", "da", "dg", "ca")
        add(("ada", 0), ("ada", 1))
        add(*att_order("att1", 16))
        add("ckd", *[("catt", h) for h in range(4)], *[("cupd", c) for c in range(3)], *[("co", hp, q) for hp in range(2) for q in range(2)], "coms")
        add("kkn")
        for fam in FAM1 + FAM2:
            add((fam, 0), (fam, 1))
        for c in range(NCH):
            for what in ("X", "U", "Yc", "M"):
                if what == "M" and c == NCH - 1:
                    continue
                add((what, c, 0), (what, c, 1))
        add("bonus", "ymean", "yvar")
        for m in range(KC):
            add(("gt", m, 0), ("gt", m, 1), ("br", m, 0), ("br", m, 1))
        add(*[("out1", m) for m in range(KC)], ("mean", "a"), ("var", "a"))
        add(("rt", 0), ("rt", 1), "gateT")
        plan.append("MOE")
        add(("mean", "b"), ("var", "b"))
        add(*[("l0in", m) for m in range(18)])
        add(*[("qms", m) for m in range(5)], *[("rope0", m) for m in range(5)])
        add(*att_order("att2", 64))
        add(*[("l0out", m) for m in range(KC)], ("mean", "c"), ("var", "c"))
        for j in range(FF):
            add(("l0g", j), ("l0v", j))
        add(*[("l0down", m) for m in range(KC)], ("mean", "d"), ("var", "d"))
        add(*[("l1in", m) for m in range(9)], "cqms", "ckvms1")
        add("krope", *[("uq", m) for m in range(8)], *[("qrope", m) for m in range(8)])
        plan.append("UKV")
        add(*[("v1", t, hf) for hf in range(2) for t in range(4)])
        add(*att_order("att3", 32))
        add(*[("l1out", m) for m in range(KC)], ("mean", "e"), ("var", "e"))
        for j in range(FF):
            add(("l1g", j), ("l1v", j))
        add(*[("l1down", m) for m in range(KC)], ("mean", "f"), ("var", "f"))
        job, at, uses = {}, 0, [0] * NBANK
        moe_uses = None
        for name in plan:
            if name == "MOE":
                moe_uses = list(uses)
                continue
            if name == "UKV":
                continue
            b = at % NBANK
            uses[b] += 1
            job[name] = (b, uses[b])
            at += 1

        def bank(eng, name):
            b, use = job[name]
            eng.wait_ge(bank_ready[b], use)
            return ps[b]

        def evacuated(eng, name):
            b, use = job[name]
            eng.wait_ge(bank_free[b], use)

        def frees(ins, name):
            ins.then_inc(bank_free[job[name][0]], 1)

        def bc(ap, n):
            return ap.unsqueeze(1).broadcast_to([ap.shape[0], n, ap.shape[1]])

        block = ctx.enter_context(nc.Block())

        @block.sync
        def _(sp):
            for t in range(RING):
                sp.dma_start(ring[:, t, :], wall[t]).then_inc(w_ready[t], 16)
            rounds = n_tiles // RING
            with sp.Fori(1, rounds) as r:
                for s in range(RING):
                    sp.wait_ge(w_used, r * RING + (s - RING + 1))
                    sp.dma_start(ring[:, s, :], wall[r * RING + s]).then_inc(w_ready[s], 16)
            for t in range(rounds * RING, n_tiles):
                sp.wait_ge(w_used, t - RING + 1)
                sp.dma_start(ring[:, t % RING, :], wall[t]).then_inc(w_ready[t % RING], 16)
            for k in range(KC):
                sp.wait_ge(sem("result_chunks"), k + 1)
                sp.dma_start(out[k], X1[:, k, :]).then_inc(sem("stored"), 16)
            sp.wait_ge(sem("stored"), 16 * KC)

        @block.gpsimd
        def _(gp_):
            gp_.dma_start(scr_na, bass.AP(rpb_pad.tensor, 0, [[896, 8], [0, CH], [1, 896]])).then_inc(sem("na_rows"), 16)
            gp_.wait_ge(sem("t5_row_ready"), 1)
            for h in range(8):
                gp_.dma_start(bass.AP(scr_t5.tensor, h * P * 512, [[P * 512, 1], [512, P], [1, 512]]),
                              rows8[h:h + 1, :].unsqueeze(1).broadcast_to([1, P, 512])).then_inc(sem("t5_rows"), 16)
            gp_.wait_ge(sem("t5_rows"), 16 * 8)
            for i in range(2):
                src = bass.AP(scr_t5.tensor, 255 - P * i, [[511, P], [P * 512, 8], [1, S]])
                gp_.dma_start(bias1[:, :, i, :], src).then_inc(sem("bias1"), 16)
            gp_.wait_ge(sem("gateT_ready"), 1)
            gp_.dma_start(scr_gate, gateT[0:EXPERTS, :]).then_inc(sem("gate_rows"), 16)
            gp_.wait_ge(sem("gate_rows"), 16)
            gp_.dma_start(gate_bc, bass.AP(scr_gate.tensor, 0, [[0, P], [S, EXPERTS], [1, S]])).then_inc(sem("gate_bc"), 16)
            gp_.wait_ge(sem("na_rows"), 16)
            gp_.wait_ge(sem("moe_hidden"), EXPERTS)
            for h in range(8):
                for i in range(2):
                    for r in range(2):
                        src = bass.AP(scr_na.tensor, h * CH * 896 + (3 - 2 * i - r) * P + 63,
                                      [[895, CH], [P, 4], [1, CH]])
                        dst = na_bias[64 * r:64 * r + 64, h, i, :].rearrange("p (a b) -> p a b", a=4)
                        gp_.dma_start(dst, src).then_inc(sem("na_bias"), 16)

        @block.tensor
        def _(pe):
            state = {"tile": None, "pending": False, "at": 0}

            def open_(name):
                b, use = job[name]
                while plan[state["at"]] in ("MOE", "UKV"):
                    state["at"] += 1
                assert plan[state["at"]] == name, (plan[state["at"]], name)
                state["at"] += 1
                if use > 1:
                    pe.wait_ge(bank_free[b], use - 1)
                return ps[b]

            def mm(o, lhsT, rhs, start=True, stop=True, done=None, **kw):
                ins = nc.tensor.matmul(o, lhsT, rhs, start=start, stop=stop, **kw)
                note(ins, done)

            def note(ins, done):
                if done is not None:
                    ins.then_inc(bank_ready[job[done][0]], 1)
                elif state["pending"]:
                    ins.then_inc(w_used, 1)
                    state["pending"] = False

            def tile(stage, n, r=None):
                t = first[stage] + n
                if t != state["tile"]:
                    if state["tile"] is not None:
                        assert not state["pending"] and t == state["tile"] + 1, (stage, n, state)
                        state["pending"] = True
                    need = 16 * (t // RING + 1)
                    pe.wait_ge(w_ready[t % RING], need if r is None else r * 16 + need)
                    state["tile"] = t
                return ring[:, t % RING, :]

            def wblk(stage, n):
                return tile(stage, n // BLOCKS)[:, (n % BLOCKS) * P:(n % BLOCKS + 1) * P]

            def linear(name, stage, n0, nk, x, o=None, done=True):
                b = open_(name) if o is None else o
                for k in range(nk):
                    mm(b, wblk(stage, n0 + k), x(k), k == 0, k == nk - 1, name if done and k == nk - 1 else None)

            def transpose(o, i, ident, done=None):
                note(nc.tensor.transpose(o, i, ident), done)

            ident = c_("ident")

            def attention(st, specs, before):
                for item in att_order(st, len(specs)):
                    if item[0] == "kT":
                        h = item[1]
                        b = open_(item)
                        for k in range(2):
                            mm(b[0:64, :], tile("l1ukv", 1)[:, k * 1024 + h * 64:k * 1024 + h * 64 + 64],
                               ckv1[:, k, :], k == 0, k == 1, item if k == 1 else None)
                        continue
                    _, what, i = item
                    s = specs[i]
                    b = open_(item)
                    nk = s["nk"]
                    if what == "S":
                        before(i)
                        mm(b[:, 0:nk], s["q"], s["k"], done=item)
                    elif what == "T":
                        pe.wait_ge(sem("att_probs"), before_[st] + i + 1)
                        Pb = att1_P if st == "att1" else att2_P
                        for t in range(nk // P):
                            transpose(b[:, t * P:(t + 1) * P], Pb[:, i % 3, t * P:(t + 1) * P], ident,
                                      item if t == nk // P - 1 else None)
                    else:
                        evacuated(pe, (st, "T", i))
                        PT = att1_PT if st == "att1" else att2_PT
                        r0 = 64 * (s["o"].start_partition() // 64)
                        for t in range(nk // P):
                            mm(b[r0:r0 + 64, 0:P], s["v"][t], PT[:, i % 3, t, :], t == 0, t == nk // P - 1,
                               item if t == nk // P - 1 else None)

            def norm_sums(which, n):
                z, sq = ln_bufs(n)
                for what, src in (("mean", z), ("var", sq)):
                    b = open_((what, which))
                    for k in range(KC):
                        pe.wait_ge(sem(f"{what}_in"), nth(which) + k + 1)
                        mm(b[:, 0:n], c_("ones"), src[:, k, :], k == 0, k == KC - 1,
                           (what, which) if k == KC - 1 else None)

            pe.wait_ge(sem("params_in"), 16)
            pe.wait_ge(sem("consts_in"), 16)
            b = open_("t5")
            mm(b[0:8, :], p_("rpb_rows")[0:34, :], c_("buckets")[0:34, :], done="t5")
            pe.wait_ge(sem("x_in"), 16)
            for n, name in enumerate(IN_BLOCKS):
                if name in ("iw", "cv0", "cv1", "av0", "av1"):
                    w = 8 if name == "iw" else P
                    b = open_(("in", n))
                    for t in range(2):
                        for k in range(KC):
                            mm(b[:, t * w:(t + 1) * w], X1[:, k, t * P:(t + 1) * P], wblk("in", n * KC + k)[:, 0:w],
                               k == 0, k == KC - 1, ("in", n) if t == 1 and k == KC - 1 else None)
                else:
                    b = open_(("in", n))
                    linear(("in", n), "in", n * KC, KC, lambda k: X1[:, k, :], b[:, 0:S])
            b = open_("ckvms")
            pe.wait_ge(sem("ckv_sq"), 1)
            mm(b[:, 0:S], c_("blockones"), rel[:, 0, 0, :], done="ckvms")
            b = open_("vb")
            pe.wait_ge(sem("ckv_normed"), 1)
            for t in range(2):
                mm(b[:, t * 256:(t + 1) * 256], F["ckv"][0:64, 0, t * P:(t + 1) * P], p_("w_uv")[0:64, :],
                   done="vb" if t else None)
            for i in range(2):
                for q in range(4):
                    b = open_(("ix", i, q))
                    r = slice(32 * q, 32 * q + 32)
                    for m in range(2):
                        mm(b[:, m * S:(m + 1) * S], F["iq"][r, m, i * P:(i + 1) * P], F["ik"][r, 0, :],
                           done=("ix", i, q) if m else None)
            pe.wait_ge(sem("small_act"), 4)
            for name, r0, k in (("dw", R_W, 16), ("da", R_A, 16), ("dg", R_G, 32)):
                b = open_(name)
                for m in range(2):
                    mm(b[:, m * S:(m + 1) * S], p_("lora")[r0:r0 + k, m * P:(m + 1) * P], small_act[r0:r0 + k, :],
                       done=name if m else None)
            b = open_("ca")
            mm(b[:, 0:S], p_("lora")[R_C:R_C + 16, 0:P], small_act[R_C:R_C + 16, :], done="ca",
               tile_position=(96, 0))
            pe.wait_ge(sem("cond_silu"), 1)
            cond = p_("cond").rearrange("p (k s) -> p k s", k=KC)
            for l in range(2):
                b = open_(("ada", l))
                for m in range(48):
                    for k in range(KC):
                        mm(b[:, 2 * m:2 * m + 2], wblk(f"ada{l}", m * KC + k), cond[:, k, :], k == 0, k == KC - 1,
                           ("ada", l) if m == 47 and k == KC - 1 else None)
            for i in (24, 25):
                evacuated(pe, ("in", i))
            evacuated(pe, "vb")
            attention("att1", att1, lambda i: None)
            if upto <= 1:
                return
            b = open_("ckd")
            pe.wait_ge(sem("c_feat"), 1)
            for t in range(2):
                transpose(b[:, t * P:(t + 1) * P], C["kd"][:, t * P:(t + 1) * P], ident, "ckd" if t else None)
            for h in range(4):
                b = open_(("catt", h))
                r = slice(32 * h, 32 * h + 32)
                for c in range(NCH):
                    o = b[64 * (c % 2):64 * (c % 2) + 64, (c // 2) * CH:(c // 2 + 1) * CH]
                    mm(o, C["ki"][r, c * CH:(c + 1) * CH], C["qd"][r, c * CH:(c + 1) * CH],
                       done=("catt", h) if c == NCH - 1 else None, tile_position=(32 * h, 64 * (c % 2)))
            evacuated(pe, "ckd")
            for c in range(3):
                b = open_(("cupd", c))
                r = slice(64 * (c % 2), 64 * (c % 2) + 64)
                mm(b[:, 0:S], c_kdt[r, c // 2, :], cv[r, c // 2, :], done=("cupd", c))
            for h in range(4):
                evacuated(pe, ("catt", h))
            pe.wait_ge(sem("c_states"), 3)
            for hp in range(2):
                for par_ in range(2):
                    b = open_(("co", hp, par_))
                    r = slice(64 * par_, 64 * par_ + 64)
                    for n in range(2):
                        c = 2 * n + par_
                        for q in range(2):
                            h = 2 * hp + q
                            mm(b[64 * q:64 * q + 64, n * CH:(n + 1) * CH], cv[r, n, h * 64:(h + 1) * 64],
                               c_att[r, h, n, :], True, c == 0, skip_group_check=True)
                        if c:
                            mm(b[:, n * CH:(n + 1) * CH], c_sm[:, c - 1, hp * P:(hp + 1) * P],
                               C["qd"][:, c * CH:(c + 1) * CH], False, True, ("co", hp, par_) if n else None,
                               skip_group_check=True)
            b = open_("coms")
            pe.wait_ge(sem("c_sq"), 1)
            mm(b, c_("blockones"), c_sq.rearrange("p a b -> p (a b)"), done="coms")
            if upto <= 2:
                return
            b = open_("kkn")
            pe.wait_ge(sem("d_kk_sq"), 1)
            mm(b, c_("blockones"), DD["t"].rearrange("p a b -> p (a b)"), done="kkn")
            pe.wait_ge(sem("d_feat"), 1)

            def family(name, f):
                for p in range(2):
                    b = open_((name, p))
                    r = slice(64 * p, 64 * p + 64)
                    for u in range(8):
                        lhsT, rhs = f(r, u)
                        mm(b[r, u * CH:(u + 1) * CH], lhsT, rhs, done=(name, p) if u == 7 else None)

            def tok(x):
                return lambda r, u: x[r, u // NCH, (u % NCH) * CH:(u % NCH + 1) * CH]

            def unit(x):
                return lambda r, u: U[x][r, u, :]

            def pair(a, b2):
                return lambda r, u: (a(r, u), b2(r, u))

            eye = lambda r, u: ident[r, r.start:r.start + 64]
            family("N", pair(tok(DD["Bh"]), tok(Ah)))
            family("A", pair(tok(Ah), tok(DD["Bh"])))
            family("GRB", pair(tok(DD["Bh"]), tok(Rh)))
            family("GAK", pair(tok(DD["Kh"]), tok(Ah)))
            family("GRK", pair(tok(DD["Kh"]), tok(Rh)))
            family("Vt", pair(lambda r, u: dS[r, 5 + u // NCH, (u % NCH) * CH:(u % NCH + 1) * CH], eye))
            family("Bt", pair(tok(DD["Bh"]), eye))
            family("Kt", pair(tok(DD["Kh"]), eye))
            pe.wait_ge(sem("d_split"), 5)
            steps = [("D2", "Dt", "D"), ("D2t", "D", "Dt"), ("Z1", "D2t", "Z"), ("W1", "D2", "W"),
                     ("D4", "D2t", "D2"), ("D4t", "D2", "D2t"), ("Z2", "D4t", "Z"), ("W2", "D4", "W"),
                     ("D8", "D4t", "D4"), ("D8t", "D4", "D4t"), ("Z3", "D8t", "Z"), ("W3", "D8", "W"),
                     ("Pm", "W", "Lo"), ("Pt", "Lo", "W"), ("P2t", "Pm", "Pt"), ("Y1", "P2t", "Z"), ("T", "Pt", "Y1")]
            wrote = {"D": None, "Dt": None, "Z": None, "W": None, "Lo": None}
            for name, l, r_ in steps:
                for src in (l, r_):
                    if wrote.get(src):
                        for p in range(2):
                            evacuated(pe, (wrote[src], p))
                family(name, pair(unit(l), unit(r_)))
                wrote[{"Z1": "Z", "Z2": "Z", "Z3": "Z", "W1": "W", "W2": "W", "W3": "W"}.get(name, name)] = name
            for p in range(2):
                evacuated(pe, ("T", p))
            for c in range(NCH):
                def per_pair(what, terms):
                    for p in range(2):
                        b = open_((what, c, p))
                        r = slice(64 * p, 64 * p + 64)
                        for m in range(2):
                            ts = terms(r, m)
                            for n, (l, r_) in enumerate(ts):
                                mm(b[r, m * CH:(m + 1) * CH], l, r_, n == 0, n == len(ts) - 1,
                                   (what, c, p) if m == 1 and n == len(ts) - 1 else None)
                cs = slice(c * CH, (c + 1) * CH)
                if c:
                    pe.wait_ge(sem("d_state"), 2 * c)
                per_pair("X", lambda r, m: ([(Ah[r, m, cs], m_st[r, c, m, :])] if c else [])
                         + [(U["GAK"][r, 4 * m + c, :], U["Vt"][r, 4 * m + c, :])])
                for p in range(2):
                    evacuated(pe, ("X", c, p))
                per_pair("U", lambda r, m: [(U["T"][r, 4 * m + c, :], x_u[r, 0, m, :])])
                for p in range(2):
                    evacuated(pe, ("U", c, p))
                per_pair("Yc", lambda r, m: ([(m_st[r, c, m, :], Rh[r, m, cs])] if c else [])
                         + [(x_u[r, 1, m, :], U["GRB"][r, 4 * m + c, :]), (U["Vt"][r, 4 * m + c, :], U["GRK"][r, 4 * m + c, :])])
                if c < NCH - 1:
                    per_pair("M", lambda r, m: [(U["Bt"][r, 4 * m + c, :], x_u[r, 1, m, :]),
                                                (U["Kt"][r, 4 * m + c, :], U["Vt"][r, 4 * m + c, :])])
            for name, src, s_ in (("bonus", bn, "d_bonus_in"), ("ymean", yT, "d_y"), ("yvar", DD["t"], "d_ysq")):
                b = open_(name)
                pe.wait_ge(sem(s_), 1)
                mm(b, c_("blockones"), src.rearrange("p a b -> p (a b)"), done=name)
            if upto <= 3:
                return
            pe.wait_ge(sem("ys_ready"), 4)
            for m in range(KC):
                for half in range(2):
                    b = open_(("gt", m, half))
                    for n in (2 * half, 2 * half + 1):
                        for k in range(KC):
                            mm(b[:, (n % 2) * S:(n % 2 + 1) * S], wblk("merge", m * 40 + n * KC + k), X1[:, k, :],
                               k == 0, k == KC - 1, ("gt", m, half) if n % 2 and k == KC - 1 else None)
                for half in range(2):
                    b = open_(("br", m, half))
                    for n in (2 * half, 2 * half + 1):
                        for k in range(2):
                            mm(b[:, (n % 2) * S:(n % 2 + 1) * S], wblk("merge", m * 40 + 32 + n * 2 + k),
                               ysT[:, n, k, :], k == 0, k == 1, ("br", m, half) if n % 2 and k == 1 else None)
            pe.wait_ge(sem("merged"), KC)
            for m in range(KC):
                b = open_(("out1", m))
                linear(("out1", m), "out", m * KC, KC, lambda k: mergedT[:, k, :], b[:, 0:S])
            norm_sums("a", S)
            pe.wait_ge(sem("ln_out"), KC)
            router = p_("router").rearrange("p (k n) -> p k n", k=KC)
            for t in range(2):
                b = open_(("rt", t))
                for k in range(KC):
                    mm(b[:, 0:36], X1[:, k, t * P:(t + 1) * P], router[:, k, :], k == 0, k == KC - 1,
                       ("rt", t) if k == KC - 1 else None)
            b = open_("gateT")
            for t in range(2):
                pe.wait_ge(sem("gate_ready"), t + 1)
                transpose(b[0:EXPERTS, t * P:(t + 1) * P], rt[:, t, 11, :], ident, "gateT" if t else None)
            if upto <= 4:
                return
            for bb in range(NBANK):
                pe.wait_ge(bank_free[bb], moe_uses[bb])
            for bb in range(4):
                mm(ps[4 + bb][:, :], c_("zeros"), con[:, 0:512], True, False, skip_group_check=True)

            def hidden(e_par, base, r=None):
                for part in range(2):
                    b = ps[2 * e_par + part]
                    w = tile("moe", base + part, r)
                    for m in range(2):
                        for k in range(KC):
                            ins = nc.tensor.matmul(b[:, m * S:(m + 1) * S], w[:, (m * KC + k) * P:(m * KC + k + 1) * P],
                                                   X1[:, k, :], start=k == 0, stop=k == KC - 1)
                            if m == 1 and k == KC - 1:
                                ins.then_inc(sem("moe_gate" if part == 0 else "moe_up"), 1)
                            else:
                                note(ins, None)

            def down(e_par, n, r=None, last=False):
                w = tile("moe", n, r)
                for m in range(KC):
                    for k in range(2):
                        ins = nc.tensor.matmul(ps[4 + m // 2][:, (m % 2) * S:(m % 2 + 1) * S],
                                               w[:, (k * KC + m) * P:(k * KC + m + 1) * P], m_h[:, e_par, k, :],
                                               start=False, stop=last and k == 1 and m % 2 == 1, skip_group_check=True)
                        if m == KC - 1 and k == 1:
                            ins.then_inc(sem("moe_down"), 1)
                        else:
                            note(ins, None)

            hidden(0, 0)
            with pe.Fori(0, (EXPERTS - 2) // 2) as r:
                t0 = state["tile"]
                for s in range(2):
                    hidden((1 + s) % 2, 2 + 3 * s, r)
                    pe.wait_ge(sem("moe_hidden"), r * 2 + (s + 1))
                    down(s % 2, 4 + 3 * s, r)
            state["tile"] = t0 + 3 * (EXPERTS - 2)
            hidden(1, 2 + 3 * (EXPERTS - 2))
            pe.wait_ge(sem("moe_hidden"), EXPERTS - 1)
            down(0, 4 + 3 * (EXPERTS - 2))
            pe.wait_ge(sem("moe_hidden"), EXPERTS)
            down(1, 5 + 3 * (EXPERTS - 2), last=True)
            pe.wait_ge(sem("z_written"), KC)
            norm_sums("b", S)
            if upto <= 5:
                return
            pe.wait_ge(sem("h_ready"), 2 * KC)
            for n in range(18):
                b = open_(("l0in", n))
                if n == 5 or n >= 14:
                    for t in range(4):
                        for k in range(KC):
                            mm(b[:, t * P:(t + 1) * P], H[:, k, t * P:(t + 1) * P], wblk("l0in", n * KC + k),
                               k == 0, k == KC - 1, ("l0in", n) if t == 3 and k == KC - 1 else None)
                else:
                    linear(("l0in", n), "l0in", n * KC, KC, lambda k: H[:, k, :], b)
            for m in range(5):
                b = open_(("qms", m))
                pe.wait_ge(sem("q0_sq"), m + 1)
                mm(b, c_("blockones"), tq2[:, m, :], done=("qms", m))
            for m in range(5):
                b = open_(("rope0", m))
                pe.wait_ge(sem("q0_normed"), m + 1)
                mm(b[:, 0:S], c_("rot"), Q0[:, m, 0:S], done=("rope0", m))
            pe.wait_ge(sem("q0_roped"), 5)
            for n in range(17, 5, -1):
                evacuated(pe, ("l0in", n))
            evacuated(pe, ("l0in", 5))
            attention("att2", att2, lambda i: None)
            evacuated(pe, ("att2", "O", 63))
            for m in range(KC):
                b = open_(("l0out", m))
                linear(("l0out", m), "l0out", m * KC, KC, lambda k: yT0[:, k, :], b)
            norm_sums("c", 512)

            def ffn(l, n):
                pe.wait_ge(sem("h_ready"), (4 if l == 0 else 7) * KC)
                hh = H if l == 0 else HB[:, 0:KC * S].rearrange("p (k t) -> p k t", k=KC)
                for j in range(FF):
                    for q, nm in enumerate((f"l{l}g", f"l{l}v")):
                        b = open_((nm, j))
                        linear((nm, j), f"l{l}up", j * 16 + q * KC, KC, lambda k: hh[:, k, :], b[:, 0:n])
                pe.wait_ge(sem("ff_hidden"), l * FF + FF)
                for m in range(KC):
                    b = open_((f"l{l}down", m))
                    linear((f"l{l}down", m), f"l{l}down", m * FF, FF, lambda k: u_ff[:, k, 0:n], b[:, 0:n])

            ffn(0, 512)
            norm_sums("d", 512)
            if upto <= 6:
                return
            pe.wait_ge(sem("h_ready"), 6 * KC)
            for n in range(9):
                b = open_(("l1in", n))
                w = 512 if n < 3 else S
                linear(("l1in", n), "l1in", n * KC, KC, lambda k: H[:, k, 0:w], b[:, 0:w])
            b = open_("cqms")
            pe.wait_ge(sem("cq_sq"), 1)
            for k in range(6):
                mm(b[:, 0:S], c_("ones"), sq1[:, k, 0:S], k == 0, k == 5, "cqms" if k == 5 else None)
            b = open_("ckvms1")
            for k in range(2):
                mm(b, c_("ones"), sq1[:, 6 + k, :], k == 0, k == 1, "ckvms1" if k == 1 else None)
            b = open_("krope")
            evacuated(pe, ("l1in", 2))
            mm(b[64:96, 0:S], c_("rot")[64:96, 64:96], kr1[64:96, 0:S], done="krope")
            pe.wait_ge(sem("cq_normed"), 6)
            tile("l1in", 4)
            for m in range(8):
                b = open_(("uq", m))
                for q in range(2):
                    for k in range(6):
                        mm(b[:, q * S:(q + 1) * S], wblk("l1uq", (2 * m + q) * 6 + k), cq1[:, k, :], k == 0, k == 5,
                           ("uq", m) if q and k == 5 else None)
            for m in range(8):
                b = open_(("qrope", m))
                evacuated(pe, ("uq", m))
                mm(b[0:96, :], c_("rot")[0:96, 0:96], q1[0:96, 2 * m:2 * m + 2, :].rearrange("p a b -> p (a b)"),
                   done=("qrope", m))
            pe.wait_ge(sem("ckv_normed1"), 2)
            for hf in range(2):
                for t in range(4):
                    b = open_(("v1", t, hf))
                    for k in range(2):
                        mm(b, ckv1[:, k, t * P:(t + 1) * P],
                           tile("l1ukv", 0)[:, k * 1024 + hf * 512:k * 1024 + (hf + 1) * 512], k == 0, k == 1,
                           ("v1", t, hf) if k else None)
            pe.wait_ge(sem("q1_roped"), 8)
            pe.wait_ge(sem("kr_placed"), 2)

            def before3(i):
                evacuated(pe, ("kT", i // 2))

            for hf in range(2):
                for t in range(4):
                    evacuated(pe, ("v1", t, hf))
            attention("att3", att3, before3)
            evacuated(pe, ("att3", "O", 31))
            for m in range(KC):
                b = open_(("l1out", m))
                linear(("l1out", m), "l1out", m * KC, KC, lambda k: yT1[:, k, :], b[:, 0:S])
            norm_sums("e", S)
            ffn(1, S)
            norm_sums("f", S)

        @block.scalar
        def _(act):
            seq = [0]
            chain = sem("act_seq")

            def step(ins, name=None):
                if name is None:
                    seq[0] += 1
                    ins.then_inc(chain, 1)
                    act.wait_ge(chain, seq[0])
                else:
                    counts[name] = counts.get(name, 0) + 1
                    ins.then_inc(sem(name), 1)
                    act.wait_ge(sem(name), counts[name])

            counts = {}

            def tell(ins, name):
                counts[name] = counts.get(name, 0) + 1
                ins.then_inc(sem(name), 1)

            f = nc.scalar.activation

            def attention(st, specs, Pb, PT, L):
                n = len(specs)
                for i in range(n + 3):
                    if i < n:
                        s = specs[i]
                        nk = s["nk"]
                        act.wait_ge(sem("att_negmax"), before_[st] + i + 1)
                        if i >= 3:
                            act.wait_ge(bank_ready[job[(st, "T", i - 3)][0]], job[(st, "T", i - 3)][1])
                        den = SV[:, 8 + i % 4:9 + i % 4]
                        nm = SV[:, i % 4:i % 4 + 1]
                        if s["bias"] is not None:
                            tell(f(Pb[:, i % 3, 0:nk], L[:, i % 3, 0:nk], ACT.Exp, bias=nm, accum_out=den), "att_exp")
                        else:
                            ins = f(Pb[:, i % 3, 0:nk], bank(act, (st, "S", i))[:, 0:nk], ACT.Exp, bias=nm,
                                    scale=s["scale"], accum_out=den)
                            frees(ins, (st, "S", i))
                    j = i - 2
                    if 0 <= j < n:
                        nk = specs[j]["nk"]
                        b = bank(act, (st, "T", j))
                        if j >= 3:
                            act.wait_ge(bank_ready[job[(st, "O", j - 3)][0]], job[(st, "O", j - 3)][1])
                        frees(f(PT[:, j % 3, 0:nk // P, :], b[:, 0:nk].rearrange("p (a b) -> p a b", b=P), ACT.Copy),
                              (st, "T", j))

            def layer_norm(which, n, gname, bname, dst, eps=None):
                z, sq = ln_bufs(n)
                for k in range(KC):
                    act.wait_ge(sem("centred"), nth(which) + k + 1)
                    tell(f(sq[:, k, :], z[:, k, :], ACT.Square), "var_in")
                act.wait_ge(sem("var_eps"), nth(which) // KC + 1)
                tell(f(lnst[:, 2, 0:n], lnst[:, 1, 0:n], ACT.Sqrt), "ln_std")
                for k in range(KC):
                    act.wait_ge(sem("scaled"), nth(which) + k + 1)
                    tell(f(dst(k), z[:, k, :], ACT.Identity, bias=p_(bname)[:, k:k + 1], scale=p_(gname)[:, k:k + 1]),
                         "ln_out")

            act.dma_start(X1, xin.rearrange("k p t -> p k t")).then_inc(sem("x_in"), 16)
            act.dma_start(par[:, :], params).then_inc(sem("params_in"), 16)
            act.dma_start(con[:, :], consts).then_inc(sem("consts_in"), 16)
            act.dma_start(XC[:, :, S:2 * S], ctxin.rearrange("k p t -> p k t")).then_inc(sem("ctx_in"), 16)
            act.wait_ge(sem("params_in"), 16)
            tell(f(p_("cond"), p_("cond"), ACT.Silu), "cond_silu")
            dst = {"ik": F["ik"][:, 0, :], "ckv": F["ckv"][:, 0, :], "cq": F["cq"][:, 0, :], "ck": F["ck"][:, 0, :],
                   "small": dF[:, 0, 1:]}
            for m in range(2):
                for nm in ("iq", "bq", "cg", "aq", "ak"):
                    dst[f"{nm}{m}"] = F[nm][:, m, :]
                for q, nm in enumerate(("dr", "dk", "dv")):
                    dst[f"{nm}{m}"] = dF[:, 1 + 2 * q + m, 1:]
            for n, name in enumerate(IN_BLOCKS):
                b = bank(act, ("in", n))
                if name == "iw":
                    o, src = iw[:, :, :], b[:, 0:16].rearrange("p (a b) -> p a b", a=2)
                elif name[:2] in ("cv", "av"):
                    m = int(name[2])
                    o = (cv if name[0] == "c" else av)[:, :, m * P:(m + 1) * P]
                    src = b[:, 0:S].rearrange("p (a b) -> p a b", a=2)
                else:
                    o, src = dst[name], b[:, 0:S]
                frees(f(o, src, ACT.Silu if name[:2] == "cg" else ACT.Copy), ("in", n))
            act.wait_ge(sem("ckv_ms"), 1)
            tell(f(rel[:, 0, 1, :], rel[:, 0, 0, :], ACT.Sqrt), "ckv_rms")
            frees(f(vb, bank(act, "vb").rearrange("p (a b) -> p a b", a=2), ACT.Copy), "vb")
            for i in range(2):
                for q in range(4):
                    n = 4 * i + q
                    if n >= 2:
                        act.wait_ge(sem("rel_used"), n - 1)
                    else:
                        act.wait_ge(sem("ckv_normed"), 1)
                    b = bank(act, ("ix", i, q))
                    frees(f(rel[:, n % 2, :, :], b.rearrange("p (a b) -> p a b", a=2), ACT.Relu, scale=32 ** -0.5),
                          ("ix", i, q))
            act.wait_ge(sem("d_shifted"), 7)
            for r0, fn in ((R_W, ACT.Tanh), (R_A, ACT.Copy), (R_G, ACT.Sigmoid), (R_C, ACT.Copy)):
                tell(f(small_act[r0:r0 + 32, :], dS[r0:r0 + 32, 0, :], fn), "small_act")
            for name in ("dw", "da"):
                b = bank(act, name)
                for m in range(2):
                    ins = f(DZ[name[1]][:, m, :], b[:, m * S:(m + 1) * S], ACT.Sigmoid,
                            bias=p_("d_w0" if name == "dw" else "d_a0")[:, m:m + 1])
                    if m:
                        frees(ins, name)
            frees(f(DZ["g"], bank(act, "dg").rearrange("p (a b) -> p a b", a=2), ACT.Copy), "dg")
            frees(f(c_z, bank(act, "ca")[:, 0:S], ACT.Copy), "ca")
            attention("att1", att1, att1_P, att1_PT, att1_L)
            if upto <= 1:
                return
            act.wait_ge(sem("c_zb"), 1)
            step(f(C["ab"], C["zb"], ACT.Abs))
            step(f(C["ab"], C["ab"], ACT.Exp, scale=-1.0))
            tell(f(C["ln"], C["ab"], ACT.Ln, bias=1.0), "c_softplus")
            act.wait_ge(sem("c_cum"), 1)
            f(C["ec"], C["cum"], ACT.Exp)
            f(C["en"], C["cum"], ACT.Exp, scale=-1.0)
            for c in range(NCH):
                ins = f(C["ed"][:, c * CH:(c + 1) * CH], C["cum"][:, c * CH:(c + 1) * CH], ACT.Exp, scale=-1.0,
                        bias=C["cum"][:, c * CH + CH - 1:c * CH + CH])
            tell(ins, "c_exps")
            frees(f(c_kdt, bank(act, "ckd")[:, 0:S].rearrange("p (a b) -> p a b", a=2), ACT.Copy), "ckd")
            for hp in range(2):
                for q in range(2):
                    o = c_o[:, hp, :].rearrange("p (n q t) -> p n q t", n=2, q=2)[:, :, q, :]
                    frees(f(o, bank(act, ("co", hp, q))[:, 0:P].rearrange("p (a b) -> p a b", a=2), ACT.Copy),
                          ("co", hp, q))
            for hp in range(2):
                for q in range(2):
                    evacuated(act, ("co", hp, q))
            tell(f(c_sq, c_o, ACT.Square), "c_sq")
            act.wait_ge(sem("c_ms"), 1)
            tell(f(c_sq, c_sq, ACT.Sqrt), "c_rms")
            if upto <= 2:
                return
            act.wait_ge(sem("d_kk"), 1)
            tell(f(DD["t"], DD["kk"], ACT.Square), "d_kk_sq")
            tell(f(DD["e1"], bank(act, "kkn").rearrange("p (a b) -> p a b", a=2), ACT.Sqrt), "d_kk_norm")
            frees(f(DD["e2"][:, 0, 0:1], DD["cum"][:, 0, 0:1], ACT.Copy), "kkn") if False else None
            act.wait_ge(sem("d_cum"), 1)
            act.wait_ge(sem("d_kk_unit"), 1)
            f(DD["e1"], DD["cm1"], ACT.Exp)
            f(DD["e2"], DD["cum"], ACT.Exp)
            tell(f(DD["e3"], DD["cum"], ACT.Exp, scale=-1.0), "d_exps")
            for fam in ("Vt", "Bt", "Kt"):
                for p in range(2):
                    r = slice(64 * p, 64 * p + 64)
                    frees(f(U[fam][r, :, :], bank(act, (fam, p))[r, :].rearrange("p (a b) -> p a b", a=8), ACT.Copy),
                          (fam, p))
            for fam in FAM2:
                if fam[0] in "ZW" or fam in ("Y1", "T"):
                    continue
                p = 1
                r = slice(64, P)
                frees(f(U[fam][r, :, :], bank(act, (fam, p))[r, :].rearrange("p (a b) -> p a b", a=8), ACT.Copy),
                      (fam, p))
            for c in range(NCH):
                for what, n in (("X", 0), ("U", 1)):
                    r = slice(64, P)
                    frees(f(x_u[r, n, :, :], bank(act, (what, c, 1))[r, 0:P].rearrange("p (a b) -> p a b", a=2),
                            ACT.Copy), (what, c, 1))
            act.wait_ge(sem("d_centred"), 1)
            tell(f(DD["t"], yT, ACT.Square), "d_ysq")
            act.wait_ge(sem("d_var"), 1)
            tell(f(DD["e1"], DD["e1"], ACT.Sqrt), "d_std")
            if upto <= 3:
                return
            for m in range(KC):
                if m >= 2:
                    act.wait_ge(sem("gates_used"), m - 1)
                for half in range(2):
                    frees(f(gates[:, m % 2, 2 * half:2 * half + 2, :],
                            bank(act, ("gt", m, half)).rearrange("p (a b) -> p a b", a=2), ACT.Sigmoid), ("gt", m, half))
            layer_norm("a", S, "ln1g", "ln1b", lambda k: X1[:, k, :])
            for t in range(2):
                act.wait_ge(sem("rt_neg"), t + 1)
                tell(f(rt[:, t, 0, 0:4], lg[:, t, 0:4], ACT.Exp, bias=SV[:, 16 + t:17 + t],
                       accum_out=SV[:, 20 + t:21 + t]), "rt_gexp")
                act.wait_ge(sem("rt_diff"), t + 1)
                tell(f(SV[:, 32 + t:33 + t], SV[:, 28 + t:29 + t], ACT.Exp), "rt_eexp")
            frees(f(gateT[0:EXPERTS, :], bank(act, "gateT")[0:EXPERTS, 0:S], ACT.Copy), "gateT")
            evacuated(act, "gateT")
            tell(f(SV[0:1, 40:41], gateT[0:1, 0:1], ACT.Copy), "gateT_ready")
            if upto <= 4:
                return

            def expert(par_, n):
                act.wait_ge(sem("moe_gate"), n + 1)
                if not isinstance(n, int) or n >= 2:
                    act.wait_ge(sem("moe_hidden"), n - 1)
                f(m_sg[:, par_, :, :], ps[2 * par_].rearrange("p (a b) -> p a b", a=2), ACT.Silu)\
                    .then_inc(sem("moe_silu"), 1)

            act.wait_ge(sem("moe_gate"), 1)
            f(m_sg[:, 0, :, :], ps[0].rearrange("p (a b) -> p a b", a=2), ACT.Silu).then_inc(sem("moe_silu"), 1)
            expert(1, 1)
            expert(0, 2)
            with act.Fori(0, (EXPERTS - 4) // 2) as r:
                for s in range(2):
                    expert((1 + s) % 2, r * 2 + (3 + s))
            expert(1, EXPERTS - 1)
            layer_norm("b", S, "ln2g", "ln2b", lambda k: X1[:, k, :])
            if upto <= 5:
                return
            for n in range(18):
                b = bank(act, ("l0in", n))
                if n == 5:
                    o = V0[:, :, 0:P]
                elif n >= 14:
                    o = V0[:, :, P + (n - 14) * P:P + (n - 13) * P]
                elif n < 5:
                    o = Q0[:, n, :]
                elif n < 10:
                    o = qb[:, n - 6, :]
                else:
                    o = kb[:, n - 10, :]
                src = b.rearrange("p (a b) -> p a b", a=4) if n == 5 or n >= 14 else b[:, :]
                frees(f(o, src, ACT.Copy), ("l0in", n))
            for m in range(5):
                evacuated(act, ("l0in", m))
                tell(f(tq2[:, m, :], Q0[:, m, :], ACT.Square), "q0_sq")
            for m in range(5):
                act.wait_ge(sem("q0_ms"), m + 1)
                tell(f(tq[:, m, :], tq[:, m, :], ACT.Sqrt), "q0_rms")
            attention("att2", att2, att2_P, att2_PT, att2_L)

            def gated(name, l, which, n):
                for m in range(KC):
                    b = bank(act, (name, m))
                    if m >= 2:
                        act.wait_ge(sem("z_written"), nth(which) - KC + m - 1)
                    g = 16 if "out" in name else 40
                    ts = lnst[:, m % 2, 0:n]
                    ins = f(ts[:, 0:S], b[:, 0:S], ACT.Copy, scale=MOD[:, l, g + m, 0:1])
                    if n > S:
                        ins = f(ts[:, S:n], b[:, S:n], ACT.Copy, scale=MOD[:, l, g + m, 1:2])
                    frees(ins, (name, m))

            gated("l0out", 0, "c", 512)
            layer_norm("c", 512, "l0ln1g", "l0ln1b", lambda k: XC[:, k, :])

            def ffn(l, n):
                ns = n // S
                for j in range(FF):
                    b = bank(act, (f"l{l}g", j))
                    if j >= 2:
                        act.wait_ge(sem("conv_done"), l * FF + j - 1)
                    else:
                        act.wait_ge(sem("pad_zero"), l + 1)
                    frees(f(gp[:, j % 2, 0:ns, 1:S + 1], b[:, 0:n].rearrange("p (a b) -> p a b", a=ns), ACT.Copy),
                          (f"l{l}g", j))
                    act.wait_ge(sem("conv_done"), l * FF + j + 1)
                    if j >= 2:
                        act.wait_ge(sem("ff_hidden"), l * FF + j - 1)
                    tell(f(sg_[:, j % 2, 0:n], cg_[:, j % 2, 0:n], ACT.Silu), "ff_silu")

            ffn(0, 512)
            gated("l0down", 0, "d", 512)
            layer_norm("d", 512, "l0ln2g", "l0ln2b", lambda k: XC[:, k, :])
            if upto <= 6:
                return
            for n in range(9):
                b = bank(act, ("l1in", n))
                if n < 2:
                    o, src = ckv1[:, n, :], b[:, :]
                elif n == 2:
                    o, src = kr1[64:96, :], b[64:96, :]
                else:
                    o, src = cq1[:, n - 3, :], b[:, 0:S]
                frees(f(o, src, ACT.Copy), ("l1in", n))
            for n in range(9):
                evacuated(act, ("l1in", n))
            f(sq1[:, 0:6, 0:S], cq1, ACT.Square)
            tell(f(sq1[:, 6:8, :], ckv1, ACT.Square), "cq_sq")
            act.wait_ge(sem("cq_ms"), 2)
            f(lnst[:, 0, 0:S], lnst[:, 0, 0:S], ACT.Sqrt)
            tell(f(lnst[:, 1, :], lnst[:, 1, :], ACT.Sqrt), "cq_rms")
            for m in range(8):
                frees(f(q1[0:96, 2 * m:2 * m + 2, :], bank(act, ("uq", m))[0:96, :].rearrange("p (a b) -> p a b", a=2),
                        ACT.Copy), ("uq", m))
            for hf in range(2):
                for t in range(4):
                    frees(f(V1[:, t, hf * 512:(hf + 1) * 512], bank(act, ("v1", t, hf))[:, :], ACT.Copy), ("v1", t, hf))
            attention("att3", att3, att2_P, att2_PT, None)
            gated("l1out", 1, "e", S)
            layer_norm("e", S, "l1ln1g", "l1ln1b", lambda k: X1[:, k, :])
            ffn(1, S)
            gated("l1down", 1, "f", S)
            z, sq = ln_bufs(S)
            layer_norm("f", S, "l1ln2g", "l1ln2b", lambda k: X1[:, k, :])

        @block.vector
        def _(dve):
            seq = [0]
            chain = sem("dve_seq")
            counts = {}
            V = nc.vector

            def step(ins, name=None):
                if name is None:
                    seq[0] += 1
                    ins.then_inc(chain, 1)
                    dve.wait_ge(chain, seq[0])
                else:
                    counts[name] = counts.get(name, 0) + 1
                    ins.then_inc(sem(name), 1)
                    dve.wait_ge(sem(name), counts[name])

            def tell(ins, name):
                counts[name] = counts.get(name, 0) + 1
                ins.then_inc(sem(name), 1)

            def attention(st, specs, Pb, L):
                n = len(specs)
                for i in range(n + 4):
                    if st == "att3" and i % 2 == 0 and i < n:
                        h = i // 2
                        b = bank(dve, ("kT", h))
                        if h >= 2:
                            dve.wait_ge(bank_ready[job[(st, "S", i - 3)][0]], job[(st, "S", i - 3)][1])
                        frees(V.tensor_copy(kT1[0:64, h % 2, :], b[0:64, :]), ("kT", h))
                    if i < n:
                        s = specs[i]
                        nk = s["nk"]
                        b = bank(dve, (st, "S", i))
                        nm = SV[:, i % 4:i % 4 + 1]
                        if s["bias"] is not None:
                            if i >= 3 and counts_exp(specs, i - 3):
                                dve.wait_ge(sem("att_exp"), exp_before[st] + counts_exp(specs, i - 3))
                            nb = s["bias"].shape[1]
                            ins = V.scalar_tensor_tensor(L[:, i % 3, 0:nb], b[:, 0:nb], s["scale"], s["bias"],
                                                         ALU.mult, ALU.add)
                            if nk > nb:
                                ins = V.tensor_scalar(L[:, i % 3, nb:nk], b[:, nb:nk], s["scale"], None, ALU.mult)
                            frees(ins, (st, "S", i))
                            evacuated(dve, (st, "S", i))
                            step(V.tensor_reduce(nm, L[:, i % 3, 0:nk], AX.X, ALU.max, negate=True), "att_negmax")
                        else:
                            raw = SV[:, 4 + i % 4:5 + i % 4]
                            step(V.tensor_reduce(raw, b[:, 0:nk], AX.X, ALU.max))
                            step(V.tensor_scalar(nm, raw, -s["scale"], None, ALU.mult), "att_negmax")
                    j = i - 1
                    if 0 <= j < n:
                        s = specs[j]
                        if s["bias"] is not None:
                            dve.wait_ge(sem("att_exp"), exp_before[st] + counts_exp(specs, j))
                        else:
                            evacuated(dve, (st, "S", j))
                        rd = SV[:, 12 + j % 4:13 + j % 4]
                        step(V.reciprocal(rd, SV[:, 8 + j % 4:9 + j % 4]))
                        step(V.tensor_scalar(Pb[:, j % 3, 0:s["nk"]], Pb[:, j % 3, 0:s["nk"]], rd, None, ALU.mult),
                             "att_probs")
                    j = i - 4
                    if 0 <= j < n:
                        o = specs[j]["o"]
                        r0 = 64 * (o.start_partition() // 64)
                        frees(V.tensor_copy(o, bank(dve, (st, "O", j))[r0:r0 + 64, 0:P]), (st, "O", j))

            def counts_exp(specs, i):
                return sum(s["bias"] is not None for s in specs[:i + 1])

            def layer_norm(which, n, eps):
                z, sq = ln_bufs(n)
                b = bank(dve, ("mean", which))
                frees(V.tensor_scalar(lnst[:, 0, 0:n], b[:, 0:n], -1.0 / D, None, ALU.mult), ("mean", which))
                evacuated(dve, ("mean", which))
                for k in range(KC):
                    tell(V.tensor_tensor(z[:, k, :], z[:, k, :], lnst[:, 0, 0:n], ALU.add), "centred")
                b = bank(dve, ("var", which))
                ins = V.tensor_scalar(lnst[:, 1, 0:n], b[:, 0:n], 1.0 / D, eps, ALU.mult, ALU.add)
                frees(ins, ("var", which))
                evacuated(dve, ("var", which))
                step(V.tensor_copy(SV[0:1, 44:45], lnst[0:1, 1, 0:1]), "var_eps")
                dve.wait_ge(sem("ln_std"), nth(which) // KC + 1)
                step(V.reciprocal(lnst[:, 2, 0:n], lnst[:, 2, 0:n]))
                dve.wait_ge(sem("centred"), nth(which) + KC)
                for k in range(KC):
                    tell(V.tensor_tensor(z[:, k, :], z[:, k, :], lnst[:, 2, 0:n], ALU.mult), "scaled")

            step(V.memset(dF[:, :, 0:1], 0.0), "d_pad")
            frees(V.tensor_copy(rows8[0:8, :], bank(dve, "t5")[0:8, :]), "t5")
            evacuated(dve, "t5")
            step(V.tensor_copy(SV[0:1, 45:46], rows8[0:1, 0:1]), "t5_row_ready")
            evacuated(dve, ("in", 4))
            tell(V.tensor_tensor(rel[:, 0, 0, :], F["ckv"][:, 0, :], F["ckv"][:, 0, :], ALU.mult), "ckv_sq")
            b = bank(dve, "ckvms")
            ins = V.tensor_scalar(rel[:, 0, 0, :], b[:, 0:S], 1.0 / 64, 1e-6, ALU.mult, ALU.add)
            frees(ins, "ckvms")
            evacuated(dve, "ckvms")
            step(V.tensor_copy(SV[0:1, 46:47], rel[0:1, 0, 0, 0:1]), "ckv_ms")
            dve.wait_ge(sem("ckv_rms"), 1)
            step(V.reciprocal(rel[:, 0, 1, :], rel[:, 0, 1, :]))
            step(V.scalar_tensor_tensor(F["ckv"][:, 0, :], F["ckv"][:, 0, :], p_("kv_gain"), rel[:, 0, 1, :],
                                        ALU.mult, ALU.mult), "ckv_normed")
            for n in range(7, 14):
                evacuated(dve, ("in", n))
            step(V.tensor_tensor(dS, dF[:, :, 0:S], dF[:, :, 1:S + 1], ALU.subtract))
            for n in range(7):
                step(V.scalar_tensor_tensor(dS[:, n, :], dS[:, n, :], p_("d_mu")[:, n:n + 1], dF[:, n, 1:S + 1],
                                            ALU.mult, ALU.add), "d_shifted")
            evacuated(dve, ("in", 3))
            for i in range(2):
                for q in range(4):
                    n = 4 * i + q
                    evacuated(dve, ("ix", i, q))
                    for m in range(2):
                        h = 4 * m + q
                        if n % 4 == 0 and m == 0:
                            ins = V.tensor_scalar(score[:, i, :], rel[:, n % 2, m, :], iw[:, i, h:h + 1], None, ALU.mult)
                        else:
                            ins = V.scalar_tensor_tensor(score[:, i, :], rel[:, n % 2, m, :], iw[:, i, h:h + 1],
                                                         score[:, i, :], ALU.mult, ALU.add)
                        if m:
                            step(ins, "rel_used")
                        else:
                            step(ins)
                step(V.scalar_tensor_tensor(work[:, i, 0, :], score[:, i, :], 8 ** -0.5,
                                            c_("causal")[:, i * S:(i + 1) * S], ALU.mult, ALU.add))
                for k in range(KEEP // 8):
                    step(V.max(top8[:, i, :], work[:, i, k % 2, :]))
                    step(V.match_replace(work[:, i, (k + 1) % 2, :], top8[:, i, :], work[:, i, k % 2, :], TAKEN))
                step(V.tensor_scalar(selm[:, i, :], work[:, i, 0, :], -2e38, NEG, ALU.is_gt, ALU.mult))
            dve.wait_ge(sem("bias1"), 32)
            for i in range(2):
                step(V.tensor_tensor(bias1[:, 4:8, i, :], bias1[:, 4:8, i, :], bc(selm[:, i, :], 4), ALU.add))
            for l in range(2):
                b = bank(dve, ("ada", l))
                o, n = PARAM[f"bada{l}"]
                ins = V.tensor_tensor(MOD[:, l, :, :], b[:, 0:96].rearrange("p (a b) -> p a b", b=2),
                                      par[:, o:o + n].unsqueeze(2).broadcast_to([P, 48, 2]), ALU.add)
                frees(ins, ("ada", l))
                evacuated(dve, ("ada", l))
                for q, g in enumerate((8, 32)):
                    step(V.tensor_scalar(SC1[:, l, q, :, :], MOD[:, l, g:g + 8, :], 1.0, None, ALU.add), "mods")
            attention("att1", att1, att1_P, att1_L)
            if upto <= 1:
                return
            evacuated(dve, "ca")
            step(V.tensor_scalar(C["zb"], c_z, p_("c_a_bias"), None, ALU.add), "c_zb")
            dve.wait_ge(sem("c_softplus"), 1)
            step(V.scalar_tensor_tensor(C["la"], C["zb"], 0.0, C["ln"], ALU.min, ALU.subtract))
            step(V.tensor_scalar(C["la"], C["la"], 1.0 / 16, None, ALU.mult))
            for c in range(NCH):
                cs = slice(c * CH, (c + 1) * CH)
                ins = V.tensor_tensor_scan(C["cum"][:, cs], c_("scan_ones"), C["la"][:, cs], 0.0, ALU.mult, ALU.add)
            step(ins, "c_cum")
            dve.wait_ge(sem("c_exps"), 1)
            V.scalar_tensor_tensor(C["qd"], F["cq"][:, 0, :], 32 ** -0.5, C["ec"], ALU.mult, ALU.mult)
            V.tensor_tensor(C["ki"], F["ck"][:, 0, :], C["en"], ALU.mult)
            step(V.tensor_tensor(C["kd"], F["ck"][:, 0, :], C["ed"], ALU.mult), "c_feat")
            for h in range(4):
                b = bank(dve, ("catt", h))
                frees(V.tensor_tensor(c_att[:, h, :, :], b[:, 0:P].rearrange("p (a b) -> p a b", a=2),
                                      bc(c_("upper_incl"), 2), ALU.mult), ("catt", h))
            for c in range(3):
                b = bank(dve, ("cupd", c))
                if c == 0:
                    ins = V.tensor_copy(c_state[:, 0, :], b[:, 0:S])
                else:
                    dec = C["ec"][:, c * CH + CH - 1:c * CH + CH]
                    ins = V.scalar_tensor_tensor(c_state[:, c, :], c_state[:, c - 1, :], dec, b[:, 0:S], ALU.mult,
                                                 ALU.add)
                frees(ins, ("cupd", c))
                evacuated(dve, ("cupd", c))
                step(V.tensor_tensor(c_sm[:, c, :], c_state[:, c, :], c_("heads_c"), ALU.mult), "c_states")
            b = bank(dve, "coms")
            ins = V.tensor_scalar(c_sq, b.rearrange("p (a b) -> p a b", a=2), 1.0 / 64, 1e-6, ALU.mult, ALU.add)
            frees(ins, "coms")
            evacuated(dve, "coms")
            step(V.tensor_copy(SV[0:1, 47:48], c_sq[0:1, 0, 0:1]), "c_ms")
            dve.wait_ge(sem("c_rms"), 1)
            step(V.reciprocal(c_sq, c_sq))
            step(V.tensor_tensor(c_o, c_o, c_sq, ALU.mult))
            for m in range(2):
                ins = V.scalar_tensor_tensor(ysT[:, 2, m, :], c_o[:, m, :], p_("c_norm_gain")[:, m:m + 1],
                                             F["cg"][:, m, :], ALU.mult, ALU.mult)
            step(ins, "ys_ready")
            if upto <= 2:
                return
            r_, k_, v_ = dS[:, 1:3, :], dS[:, 3:5, :], dS[:, 5:7, :]
            evacuated(dve, "dw")
            evacuated(dve, "da")
            evacuated(dve, "dg")
            for m in range(2):
                ins = V.tensor_scalar(DD["kk"][:, m, :], k_[:, m, :], p_("d_k_k")[:, m:m + 1], None, ALU.mult)
            step(ins, "d_kk")
            step(V.tensor_scalar(DD["lw"], DZ["w"], -W_DECAY, None, ALU.mult))
            for m in range(2):
                for c in range(NCH):
                    cs = slice(c * CH, (c + 1) * CH)
                    ins = V.tensor_tensor_scan(DD["cum"][:, m, cs], c_("scan_ones"), DD["lw"][:, m, cs], 0.0,
                                               ALU.mult, ALU.add)
            step(ins)
            step(V.tensor_tensor(DD["cm1"], DD["cum"], DD["lw"], ALU.subtract), "d_cum")
            for m in range(2):
                step(V.tensor_scalar(DD["kp"][:, m, :], DZ["a"][:, m, :], 1.0, p_("d_k_a")[:, m:m + 1], ALU.subtract,
                                     ALU.mult))
            step(V.scalar_tensor_tensor(DD["kp"], DD["kp"], 1.0, k_, ALU.add, ALU.mult))
            dve.wait_ge(sem("d_kk_norm"), 1)
            step(V.tensor_scalar(DD["e1"], DD["e1"], 1e-12, None, ALU.max))
            step(V.reciprocal(DD["e1"], DD["e1"]))
            frees(V.tensor_tensor(DD["kk"], DD["kk"], DD["e1"], ALU.mult), "kkn")
            evacuated(dve, "kkn")
            step(V.tensor_tensor(DD["b"], DD["kk"], DZ["a"], ALU.mult), "d_kk_unit")
            dve.wait_ge(sem("d_exps"), 1)
            V.scalar_tensor_tensor(Ah, DD["kk"], -1.0, DD["e1"], ALU.mult, ALU.mult)
            V.tensor_tensor(Rh, r_, DD["e2"], ALU.mult)
            V.tensor_tensor(DD["Bh"], DD["b"], DD["e3"], ALU.mult)
            step(V.tensor_tensor(DD["Kh"], DD["kp"], DD["e3"], ALU.mult), "d_feat")
            step(V.tensor_tensor(bn, r_, DD["kp"], ALU.mult))
            for m in range(2):
                step(V.tensor_scalar(bn[:, m, :], bn[:, m, :], p_("d_r_k")[:, m:m + 1], None, ALU.mult))
            step(V.tensor_copy(SV[0:1, 48:49], bn[0:1, 0, 0:1]), "d_bonus_in")
            masks = {"N": "upper", "A": "lower", "GRB": "upper_incl", "GAK": "upper", "GRK": "upper_incl"}
            for fam, mask in masks.items():
                for p in range(2):
                    r = slice(64 * p, 64 * p + 64)
                    frees(V.tensor_tensor(U[fam][r, :, :], bank(dve, (fam, p))[r, :].rearrange("p (a b) -> p a b", a=8),
                                          bc(c_(mask)[r, :], 8), ALU.mult), (fam, p))
            for fam in ("N", "A"):
                for p in range(2):
                    evacuated(dve, (fam, p))
            step(V.tensor_tensor(U["D"], U["N"], bc(c_("diag16"), 8), ALU.mult), "d_split")
            step(V.tensor_tensor(U["Dt"], U["A"], bc(c_("diag16"), 8), ALU.mult), "d_split")
            step(V.tensor_tensor(U["Lo"], U["N"], U["D"], ALU.subtract), "d_split")
            step(V.tensor_tensor(U["Z"], U["D"], bc(c_("eye64"), 8), ALU.add), "d_split")
            step(V.tensor_tensor(U["W"], U["Dt"], bc(c_("eye64"), 8), ALU.add), "d_split")
            for fam in FAM2:
                add_to = "Z" if fam[0] == "Z" else "W" if fam[0] == "W" else {"Y1": "Z", "T": "Y1"}.get(fam)
                for p in range(2):
                    r = slice(64 * p, 64 * p + 64)
                    if add_to is None and p == 1:
                        continue
                    b = bank(dve, (fam, p))[r, :].rearrange("p (a b) -> p a b", a=8)
                    if add_to is None:
                        ins = V.tensor_copy(U[fam][r, :, :], b)
                    else:
                        dst = U[add_to] if fam[0] in "ZW" else U[fam]
                        ins = V.tensor_tensor(dst[r, :, :], U[add_to][r, :, :], b, ALU.add)
                    frees(ins, (fam, p))
                    evacuated(dve, (fam, p))
            for c in range(NCH):
                r = slice(0, 64)
                for what, n in (("X", 0), ("U", 1)):
                    frees(V.tensor_copy(x_u[r, n, :, :], bank(dve, (what, c, 0))[r, 0:P].rearrange("p (a b) -> p a b", a=2)),
                          (what, c, 0))
                for p in range(2):
                    r = slice(64 * p, 64 * p + 64)
                    frees(V.tensor_copy(yT[r, :, c * CH:(c + 1) * CH],
                                        bank(dve, ("Yc", c, p))[r, 0:P].rearrange("p (a b) -> p a b", a=2)), ("Yc", c, p))
                if c < NCH - 1:
                    for p in range(2):
                        r = slice(64 * p, 64 * p + 64)
                        b = bank(dve, ("M", c, p))[r, 0:P].rearrange("p (a b) -> p a b", a=2)
                        if c == 0:
                            ins = V.tensor_copy(m_st[r, 4, :, :], b)
                        else:
                            ins = V.tensor_tensor(m_st[r, 4, :, :], m_st[r, c, :, :], b, ALU.add)
                        frees(ins, ("M", c, p))
                        evacuated(dve, ("M", c, p))
                        for m in range(2):
                            ins = V.tensor_scalar(m_st[r, c + 1, m, :], m_st[r, 4, m, :],
                                                  DD["e2"][r, m, c * CH + CH - 1:c * CH + CH], None, ALU.mult)
                        step(ins, "d_state")
            for p in range(2):
                for c in range(NCH):
                    evacuated(dve, ("Yc", c, p))
            step(V.tensor_copy(SV[0:1, 49:50], yT[0:1, 0, 0:1]), "d_y")
            flat2 = "p (a b) -> p a b"
            frees(V.tensor_tensor(bn, bank(dve, "bonus").rearrange(flat2, a=2), v_, ALU.mult), "bonus")
            b = bank(dve, "ymean").rearrange(flat2, a=2)
            frees(V.scalar_tensor_tensor(yT, b, -1.0 / 64, yT, ALU.mult, ALU.add), "ymean")
            evacuated(dve, "ymean")
            step(V.tensor_copy(SV[0:1, 50:51], yT[0:1, 0, 0:1]), "d_centred")
            b = bank(dve, "yvar").rearrange(flat2, a=2)
            frees(V.tensor_scalar(DD["e1"], b, 1.0 / 64, 64e-5, ALU.mult, ALU.add), "yvar")
            evacuated(dve, "yvar")
            step(V.tensor_copy(SV[0:1, 51:52], DD["e1"][0:1, 0, 0:1]), "d_var")
            dve.wait_ge(sem("d_std"), 1)
            step(V.reciprocal(DD["e1"], DD["e1"]))
            step(V.tensor_tensor(yT, yT, DD["e1"], ALU.mult))
            for m in range(2):
                step(V.tensor_scalar(yT[:, m, :], yT[:, m, :], p_("d_gn_w")[:, m:m + 1], p_("d_gn_b")[:, m:m + 1],
                                     ALU.mult, ALU.add))
            evacuated(dve, "bonus")
            step(V.tensor_tensor(yT, yT, bn, ALU.add))
            step(V.tensor_tensor(ysT[:, 3, :, :], yT, DZ["g"], ALU.mult), "ys_ready")
            for i in (12, 13, 14, 15, 8, 9, 10, 11, 0, 1, 2, 3, 4, 5, 6, 7):
                evacuated(dve, ("att1", "O", i))
            step(V.tensor_copy(SV[0:1, 52:53], ysT[0:1, 0, 0, 0:1]), "ys_ready")
            step(V.tensor_copy(SV[0:1, 53:54], ysT[0:1, 1, 0, 0:1]), "ys_ready")
            if upto <= 3:
                return
            z, _ = ln_bufs(S)
            for m in range(KC):
                for half in range(2):
                    evacuated(dve, ("gt", m, half))
                    b = bank(dve, ("br", m, half)).rearrange(flat2, a=2)
                    frees(V.tensor_tensor(tmpm[:, m % 2, half, :, :], b, gates[:, m % 2, 2 * half:2 * half + 2, :],
                                          ALU.mult), ("br", m, half))
                for half in range(2):
                    evacuated(dve, ("br", m, half))
                step(V.tensor_tensor(tmpm[:, m % 2, 0, :, :], tmpm[:, m % 2, 0, :, :], tmpm[:, m % 2, 1, :, :], ALU.add),
                     "gates_used")
                step(V.tensor_tensor(mergedT[:, m, :], tmpm[:, m % 2, 0, 0, :], tmpm[:, m % 2, 0, 1, :], ALU.add),
                     "merged")
            for m in range(KC):
                b = bank(dve, ("out1", m))
                frees(V.scalar_tensor_tensor(z[:, m, :], X1[:, m, :], ALPHA1, b[:, 0:S], ALU.mult, ALU.add),
                      ("out1", m))
                evacuated(dve, ("out1", m))
                step(V.tensor_copy(SV[0:1, 54:55], z[0:1, m, 0:1]), "mean_in")
            layer_norm("a", S, 1e-5)

            def first_max(t, vals, m, eq, incl, oh, w):
                step(V.tensor_scalar(eq, vals, m, None, ALU.is_equal))
                step(V.tensor_tensor_scan(incl, c_("scan_ones")[:, 0:w], eq, 0.0, ALU.mult, ALU.max))
                step(V.tensor_copy(oh[:, 0:1], incl[:, 0:1]))
                step(V.tensor_tensor(oh[:, 1:w], incl[:, 1:w], incl[:, 0:w - 1], ALU.subtract))

            for t in range(2):
                def sv(n):
                    return SV[:, n + t:n + t + 1]

                b = bank(dve, ("rt", t))
                frees(V.tensor_tensor(lg[:, t, :], b[:, 0:36], p_("router_bias"), ALU.add), ("rt", t))
                evacuated(dve, ("rt", t))
                step(V.tensor_reduce(sv(18), lg[:, t, 0:4], AX.X, ALU.max))
                step(V.tensor_scalar(sv(16), sv(18), -1.0, None, ALU.mult), "rt_neg")
                R = [rt[:, t, n, :] for n in range(12)]
                first_max(t, lg[:, t, 0:4], sv(18), R[1][:, 0:4], R[2][:, 0:4], R[3][:, 0:4], 4)
                ohg = R[3][:, 0:4].unsqueeze(2).broadcast_to([P, 4, 8])
                step(V.tensor_scalar(R[4][:, 0:4], R[3][:, 0:4], 1.0, -NEG, ALU.subtract, ALU.mult))
                step(V.tensor_tensor(R[5].rearrange("p (a b) -> p a b", a=4),
                                     lg[:, t, 4:36].rearrange("p (a b) -> p a b", a=4), ohg, ALU.mult))
                step(V.tensor_tensor(R[5].rearrange("p (a b) -> p a b", a=4), R[5].rearrange("p (a b) -> p a b", a=4),
                                     R[4][:, 0:4].unsqueeze(2).broadcast_to([P, 4, 8]), ALU.add))
                step(V.tensor_reduce(sv(22), R[5], AX.X, ALU.max))
                first_max(t, R[5], sv(22), R[6], R[7], R[8], 32)
                step(V.scalar_tensor_tensor(R[5], R[8], 4 * NEG, R[5], ALU.mult, ALU.add))
                step(V.tensor_reduce(sv(24), R[5], AX.X, ALU.max))
                first_max(t, R[5], sv(24), R[6], R[7], R[9], 32)
                step(V.tensor_tensor(sv(28), sv(24), sv(22), ALU.subtract), "rt_diff")
                dve.wait_ge(sem("rt_gexp"), t + 1)
                dve.wait_ge(sem("rt_eexp"), t + 1)
                step(V.tensor_scalar(sv(34), sv(32), 1.0, sv(20), ALU.add, ALU.mult))
                step(V.reciprocal(sv(36), sv(34)))
                step(V.scalar_tensor_tensor(R[10], R[9], sv(32), R[8], ALU.mult, ALU.add))
                step(V.tensor_scalar(R[11], R[10], sv(36), None, ALU.mult), "gate_ready")
            if upto <= 4:
                return
            dve.wait_ge(sem("gate_bc"), 16)

            def expert(par_, n, gate, w_down):
                dve.wait_ge(sem("moe_silu"), n + 1)
                step_m(V.tensor_tensor(m_t[:, par_, :, :], m_sg[:, par_, :, :], gate, ALU.mult), n)
                dve.wait_ge(sem("moe_up"), n + 1)
                if w_down:
                    dve.wait_ge(sem("moe_down"), n - 1)
                V.tensor_tensor(m_h[:, par_, :, :], m_t[:, par_, :, :],
                                ps[2 * par_ + 1].rearrange("p (a b) -> p a b", a=2), ALU.mult)\
                    .then_inc(sem("moe_hidden"), 1)

            def step_m(ins, n):
                ins.then_inc(sem("moe_gated"), 1)
                dve.wait_ge(sem("moe_gated"), n + 1)

            def gate_of(e):
                return gate_bc[:, bass.ds(e, 1), :].broadcast_to([P, 2, S]) if not isinstance(e, int) \
                    else gate_bc[:, e:e + 1, :].broadcast_to([P, 2, S])

            expert(0, 0, gate_of(0), False)
            expert(1, 1, gate_of(1), False)
            expert(0, 2, gate_of(2), True)
            with dve.Fori(0, (EXPERTS - 4) // 2) as r:
                for s in range(2):
                    expert((1 + s) % 2, r * 2 + (3 + s), gate_of(r * 2 + (3 + s)), True)
            expert(1, EXPERTS - 1, gate_of(EXPERTS - 1), True)
            dve.wait_ge(sem("moe_down"), EXPERTS)
            for m in range(KC):
                step(V.scalar_tensor_tensor(z[:, m, :], X1[:, m, :], ALPHA1, ps[4 + m // 2][:, (m % 2) * S:(m % 2 + 1) * S],
                                            ALU.mult, ALU.add), "z_written")
                step(V.tensor_copy(SV[0:1, 54:55], z[0:1, m, 0:1]), "mean_in")
            layer_norm("b", S, 1e-5)

            def modulate(l, q, n, which):
                hh = H if n == 512 else HB[:, 0:KC * S].rearrange("p (k t) -> p k t", k=KC)
                sh = 24 * q
                for k in range(KC):
                    dve.wait_ge(sem("ln_out"), nth(which) + k + 1)
                    for s in range(n // S):
                        tell(V.tensor_scalar(hh[:, k, s * S:(s + 1) * S], XC[:, k, s * S:(s + 1) * S],
                                             SC1[:, l, q, k, s:s + 1], MOD[:, l, sh + k, s:s + 1], ALU.mult, ALU.add),
                             "h_ready")

            if upto <= 5:
                return
            dve.wait_ge(sem("ctx_in"), 16)
            dve.wait_ge(sem("mods"), 4)
            modulate(0, 0, 512, "b")
            for m in range(5):
                b = bank(dve, ("qms", m))
                frees(V.tensor_scalar(tq[:, m, :], b[:, :], 1.0 / 64, 1e-6, ALU.mult, ALU.add), ("qms", m))
                evacuated(dve, ("qms", m))
                step(V.tensor_copy(SV[0:1, 55:56], tq[0:1, m, 0:1]), "q0_ms")
            for m in range(5):
                dve.wait_ge(sem("q0_rms"), m + 1)
                step(V.reciprocal(tq[:, m, :], tq[:, m, :]))
                g = p_("q_gain") if m < 4 else p_("k_gain")
                step(V.scalar_tensor_tensor(Q0[:, m, :], Q0[:, m, :], g, tq[:, m, :], ALU.mult, ALU.mult), "q0_normed")
            for m in range(5):
                b = bank(dve, ("rope0", m))
                frees(V.tensor_tensor(tq[:, m, 0:S], b[:, 0:S], c_("sin64"), ALU.mult), ("rope0", m))
                evacuated(dve, ("rope0", m))
                step(V.tensor_tensor(Q0[:, m, 0:S], Q0[:, m, 0:S], c_("cos64"), ALU.mult))
                step(V.tensor_tensor(Q0[:, m, 0:S], Q0[:, m, 0:S], tq[:, m, 0:S], ALU.add), "q0_roped")
            dve.wait_ge(sem("na_bias"), 16 * 32)
            for h in range(8):
                step(V.tensor_tensor(na_bias[:, h, :, :], na_bias[:, h, :, :], bc(c_("na_mask"), 2), ALU.add))
            attention("att2", att2, att2_P, att2_L)

            def residual(name, l, which, n):
                zz, _ = ln_bufs(n)
                for m in range(KC):
                    evacuated(dve, (name, m))
                    step(V.scalar_tensor_tensor(zz[:, m, :], XC[:, m, 0:n], ALPHA2, lnst[:, m % 2, 0:n], ALU.mult,
                                                ALU.add), "z_written")
                    step(V.tensor_copy(SV[0:1, 54:55], zz[0:1, m, 0:1]), "mean_in")

            residual("l0out", 0, "c", 512)
            layer_norm("c", 512, 1e-6)
            modulate(0, 1, 512, "c")

            def ffn(l, n):
                ns = n // S
                cw = p_(f"l{l}conv").rearrange("p (w j) -> p w j", w=3)
                cb = p_(f"l{l}convb")
                step(V.memset(gp[:, :, :, :], 0.0), "pad_zero")
                for j in range(FF):
                    evacuated(dve, (f"l{l}g", j))
                    if j >= 2:
                        dve.wait_ge(sem("ff_silu"), l * FF + j - 1)
                    g = gp[:, j % 2, 0:ns, :]
                    c = cg_[:, j % 2, 0:n].rearrange("p (a b) -> p a b", a=ns)
                    step(V.tensor_scalar(c, g[:, :, 0:S], cw[:, 0, j:j + 1], cb[:, j:j + 1], ALU.mult, ALU.add))
                    step(V.scalar_tensor_tensor(c, g[:, :, 1:S + 1], cw[:, 1, j:j + 1], c, ALU.mult, ALU.add))
                    step(V.scalar_tensor_tensor(c, g[:, :, 2:S + 2], cw[:, 2, j:j + 1], c, ALU.mult, ALU.add),
                         "conv_done")
                    if j:
                        hidden(l, j - 1, n)
                hidden(l, FF - 1, n)

            def hidden(l, j, n):
                dve.wait_ge(sem("ff_silu"), l * FF + j + 1)
                b = bank(dve, (f"l{l}v", j))
                ins = V.tensor_tensor(u_ff[:, j, 0:n], sg_[:, j % 2, 0:n], b[:, 0:n], ALU.mult)
                frees(ins, (f"l{l}v", j))
                evacuated(dve, (f"l{l}v", j))
                step(V.tensor_copy(SV[0:1, 56:57], u_ff[0:1, j, 0:1]), "ff_hidden")

            ffn(0, 512)
            residual("l0down", 0, "d", 512)
            layer_norm("d", 512, 1e-6)
            if upto <= 6:
                return
            modulate(1, 0, 512, "d")
            b = bank(dve, "cqms")
            frees(V.tensor_scalar(lnst[:, 0, 0:S], b[:, 0:S], 1.0 / 768, 1e-6, ALU.mult, ALU.add), "cqms")
            b = bank(dve, "ckvms1")
            frees(V.tensor_scalar(lnst[:, 1, :], b[:, :], 1.0 / 256, 1e-6, ALU.mult, ALU.add), "ckvms1")
            evacuated(dve, "cqms")
            step(V.tensor_copy(SV[0:1, 57:58], lnst[0:1, 0, 0:1]), "cq_ms")
            evacuated(dve, "ckvms1")
            step(V.tensor_copy(SV[0:1, 57:58], lnst[0:1, 1, 0:1]), "cq_ms")
            dve.wait_ge(sem("cq_rms"), 1)
            V.reciprocal(lnst[:, 0, 0:S], lnst[:, 0, 0:S])
            step(V.reciprocal(lnst[:, 1, :], lnst[:, 1, :]))
            for k in range(6):
                tell(V.scalar_tensor_tensor(cq1[:, k, :], cq1[:, k, :], p_("cq_gain")[:, k:k + 1], lnst[:, 0, 0:S],
                                            ALU.mult, ALU.mult), "cq_normed")
            for k in range(2):
                tell(V.scalar_tensor_tensor(ckv1[:, k, :], ckv1[:, k, :], p_("ckv_gain")[:, k:k + 1], lnst[:, 1, :],
                                            ALU.mult, ALU.mult), "ckv_normed1")
            kr = slice(64, 96)
            b = bank(dve, "krope")
            frees(V.tensor_tensor(tq1[kr, 0, 0:S], b[kr, 0:S], c_("sinm")[kr, :], ALU.mult), "krope")
            evacuated(dve, "krope")
            step(V.tensor_tensor(kr1[kr, 0:S], kr1[kr, 0:S], c_("cosm")[kr, :], ALU.mult))
            step(V.tensor_tensor(kr1[kr, 0:S], kr1[kr, 0:S], tq1[kr, 0, 0:S], ALU.add))
            for q in range(2):
                step(V.tensor_copy(kT1[kr, q, :], kr1[kr, :]), "kr_placed")
            for m in range(8):
                b = bank(dve, ("qrope", m))[0:96, :].rearrange(flat2, a=2)
                t = tq1[0:96, m % 2, :].rearrange(flat2, a=2)
                qq = q1[0:96, 2 * m:2 * m + 2, :]
                frees(V.tensor_tensor(t, b, bc(c_("sinm")[0:96, :], 2), ALU.mult), ("qrope", m))
                evacuated(dve, ("qrope", m))
                step(V.tensor_tensor(qq, qq, bc(c_("cosm")[0:96, :], 2), ALU.mult))
                step(V.tensor_tensor(qq, qq, t, ALU.add), "q1_roped")
            attention("att3", att3, att2_P, None)
            residual("l1out", 1, "e", S)
            layer_norm("e", S, 1e-6)
            modulate(1, 1, S, "e")
            ffn(1, S)
            residual("l1down", 1, "f", S)
            layer_norm("f", S, 1e-6)
            for k in range(KC):
                dve.wait_ge(sem("ln_out"), nth("f") + k + 1)
                step(V.tensor_copy(SV[0:1, 58:59], X1[0:1, k, 0:1]), "result_chunks")


def shape_constants():
    c = np.zeros((P, NCONST), np.float32)

    def put(name, a, rows=P):
        o, n = CONST[name]
        c[:rows, o:o + n] = a

    put("ident", np.eye(P))
    put("ones", np.ones((P, P)))
    half = np.arange(P) // 64
    put("blockones", (half[:, None] == half[None, :]))
    rot = np.zeros((P, P))
    for i in range(0, P, 2):
        rot[i + 1, i] = -1.0
        rot[i, i + 1] = 1.0
    put("rot", rot)
    pos = np.arange(S)

    def rope(dim):
        inv = (np.float32(10000.0) ** (-np.arange(0, dim // 2, 2, dtype=np.float32) / np.float32(dim // 2)))
        ang = np.concatenate([(pos // 64)[:, None].astype(np.float32) * inv,
                              (pos % 64)[:, None].astype(np.float32) * inv], -1).astype(np.float32)
        return np.repeat(np.cos(ang), 2, 1).T, np.repeat(np.sin(ang), 2, 1).T

    co, si = rope(64)
    put("cos64", np.tile(co, (2, 1)))
    put("sin64", np.tile(si, (2, 1)))
    co, si = rope(32)
    a = np.zeros((P, S))
    a[0:64] = 1.0
    a[64:96] = co
    put("cosm", a)
    a = np.zeros((P, S))
    a[64:96] = si
    put("sinm", a)
    dist = 255 - np.arange(512)
    dd = np.maximum(dist, 0)
    df = np.maximum(dd, 1).astype(np.float32)
    large = 16 + (np.log(df / np.float32(16)) / np.float32(math.log(128.0)) * np.float32(16)).astype(np.int32)
    bucket = np.where(dd < 16, dd, np.minimum(large, 31))
    t = np.zeros((34, 512))
    ok = dist >= 0
    t[bucket[ok], np.nonzero(ok)[0]] = 1.0
    count = ok * ((dist <= 128) * 1 + (dist % 4 == 0) + (dist % 16 == 0))
    t[32] = np.where(count > 0, np.log(np.maximum(count, 1)), NEG)
    t[33] = np.where(ok, 0.0, NEG)
    put("buckets", t, 34)
    col = np.arange(64)
    start = np.clip(col - 8, 0, 48)
    inside = (col[None, :] >= start[:, None]) & (col[None, :] < start[:, None] + 16)
    put("na_mask", np.tile(np.where(inside, 0.0, NEG), (2, 4)))
    i, j = np.arange(64)[:, None], np.arange(64)[None, :]
    put("upper", np.tile(i < j, (2, 1)))
    put("upper_incl", np.tile(i <= j, (2, 1)))
    put("lower", np.tile(i > j, (2, 1)))
    put("diag16", np.tile(i // 16 == j // 16, (2, 1)))
    put("eye64", np.tile(i == j, (2, 1)))
    put("heads_c", (np.arange(P) // 32)[:, None] == (np.arange(256) // 64)[None, :])
    q = np.arange(P)[:, None]
    put("causal", np.concatenate([np.where(np.arange(S)[None, :] <= q + P * n, 0.0, NEG) for n in range(2)], 1))
    put("scan_ones", np.ones((P, 64)))
    return c


def lay_out(v):
    f32 = np.float32

    def blocks(w, order="mk"):
        kk, mm = w.shape
        b = w.reshape(kk // P, P, mm // P, P)
        b = b.transpose(2, 0, 1, 3) if order == "mk" else b.transpose(0, 2, 1, 3)
        return b.reshape(-1, P, P)

    def tiles(bl):
        n = -(-len(bl) // BLOCKS)
        if len(bl) < n * BLOCKS:
            bl = np.concatenate([bl, np.zeros((n * BLOCKS - len(bl), P, P), f32)])
        return bl.reshape(n, BLOCKS, P, P).transpose(0, 2, 1, 3).reshape(n, P, TILE)

    wi = v["w_in"][0]

    def cols(name, a=0, b=None):
        o = IN_OFF[name]
        return wi[:, o + a:o + (b if b is not None else dict(IN_NAMES)[name])]

    small = np.zeros((D, P), f32)
    small[:, R_W:R_W + 16] = cols("d", 768, 784)
    small[:, R_A:R_A + 16] = cols("d", 784, 800)
    small[:, R_G:R_G + 32] = cols("d", 800, 832)
    small[:, R_C:R_C + 16] = cols("c_a")
    iwp = np.zeros((D, P), f32)
    iwp[:, 0:8] = cols("b_iw")
    w1 = np.concatenate([cols("b_iq"), np.tile(cols("b_ik"), (1, 4)), iwp, np.tile(cols("b_ckv"), (1, 2)),
                         cols("b_q"), small, cols("d", 0, 768), cols("c_q"), cols("c_k"), cols("c_v"), cols("c_g"),
                         cols("a_q"), cols("a_k"), cols("a_v")], 1)
    parts = [tiles(blocks(w1))]
    for l in range(2):
        parts.append(tiles(blocks(v[f"l{l}_w_ada_2"])))
    gt = blocks(cols("gate")).reshape(4, KC, KC, P, P)
    br = np.stack([blocks(v["w_branch"][0, n]).reshape(KC, 2, P, P) for n in range(4)])
    mg = np.concatenate([gt.transpose(1, 0, 2, 3, 4).reshape(KC, 32, P, P),
                         br.transpose(1, 0, 2, 3, 4).reshape(KC, 8, P, P)], 1).reshape(-1, P, P)
    parts.append(tiles(mg))
    parts.append(tiles(blocks(v["w_out"][0])))
    moe = {"gate": v["moe_w_gate"][0], "up": v["moe_w_up"][0], "down": v["moe_w_down"][0]}
    parts.append(np.concatenate([tiles(blocks(moe[kind][e], "km" if kind == "down" else "mk"))
                                 for kind, e in moe_tiles()]))
    w = v["l0_w_in_2"]
    qa = w[:, 0:512].reshape(D, 2, 4, 64).transpose(0, 2, 1, 3).reshape(D, 512)
    parts.append(tiles(blocks(np.concatenate([qa, w[:, 512:]], 1))))
    w = v["l0_w_out_2"]
    wa = w[0:512].reshape(2, 4, 64, D).transpose(1, 0, 2, 3).reshape(512, D)
    parts.append(tiles(blocks(np.concatenate([wa, w[512:]], 0))))

    def ff(l):
        up = blocks(v[f"l{l}_w_up_2"]).reshape(2, FF, KC, P, P).transpose(1, 0, 2, 3, 4).reshape(-1, P, P)
        return [tiles(up), tiles(blocks(v[f"l{l}_w_down_2"]))]

    parts += ff(0)
    w = v["l1_w_in_2"]
    krp = np.zeros((D, P), f32)
    krp[:, 64:96] = w[:, 1024:1056]
    parts.append(tiles(blocks(np.concatenate([w[:, 768:1024], krp, w[:, 0:768]], 1))))
    uq = np.zeros((768, 16, P), f32)
    uq[:, :, 0:96] = v["l1_w_uq_2"].reshape(768, 16, 96)
    parts.append(tiles(blocks(uq.reshape(768, 2048))))
    ukv = v["l1_w_ukv_2"].reshape(2, P, 16, 2, 64)
    for which in (1, 0):
        parts.append(ukv[:, :, :, which, :].transpose(1, 0, 2, 3).reshape(1, P, TILE))
    parts.append(tiles(blocks(v["l1_w_out_2"])))
    parts += ff(1)
    wall = np.concatenate(parts)
    assert wall.shape[0] == stream_plan()[1], (wall.shape, stream_plan()[1], [x.shape[0] for x in parts])

    par = np.zeros((P, NPARAM), f32)

    def put(name, a, r0=0):
        o, n = PARAM[name]
        a = np.asarray(a, f32)
        par[r0:r0 + a.shape[0], o:o + a.shape[1]] = a

    def col(a):
        return np.asarray(a, f32).reshape(-1, P).T

    put("kv_gain", np.tile(v["b_kv_gain"][0], 2)[:, None])
    put("c_a_bias", col(v["c_a_bias"][0]))
    put("c_norm_gain", col(v["c_norm_gain"][0]))
    mu = v["d_mu"][0]
    o = PARAM["d_mu"][0]
    par[R_W:R_W + 16, o] = mu[768:784]
    par[R_A:R_A + 16, o] = mu[784:800]
    par[R_G:R_G + 32, o] = mu[800:832]
    par[:, o + 1:o + 7] = col(mu[:768])
    for nm in ("d_w0", "d_a0", "d_k_k", "d_k_a", "d_r_k", "d_gn_w", "d_gn_b"):
        put(nm, col(v[nm][0]))
    for n in range(2):
        put(f"ln{n + 1}g", col(v["ln_g"][0, n]))
        put(f"ln{n + 1}b", col(v["ln_b"][0, n]))
    for l in range(2):
        put(f"bada{l}", col(v[f"l{l}_b_ada_2"]))
        for n in range(1, 3):
            for s in "gb":
                put(f"l{l}ln{n}{s}", col(v[f"l{l}_ln{n}_{s}_2"]))
        put(f"l{l}conv", np.concatenate([col(v[f"l{l}_conv_w_2"][n]) for n in range(3)], 1))
        put(f"l{l}convb", col(v[f"l{l}_conv_b_2"]))
    put("q_gain", np.tile(v["l0_q_gain_2"], 2)[:, None])
    put("k_gain", np.tile(v["l0_k_gain_2"], 2)[:, None])
    put("cq_gain", col(v["l1_cq_gain_2"]))
    put("ckv_gain", col(v["l1_ckv_gain_2"]))
    put("cond", np.stack([col(v["c_2"][0]), col(v["c_ctx_2"])], 2).reshape(P, 16))
    put("lora", v["d_w2"][0], R_W)
    put("lora", v["d_a2"][0], R_A)
    put("lora", v["d_g2"][0], R_G)
    put("lora", v["c_a_up"][0], R_C)
    put("w_uv", v["b_w_uv"][0].transpose(1, 0, 2).reshape(64, 256))
    r = np.concatenate([v["router_g"][0], v["router_e"][0]], 1)
    put("router", r.reshape(KC, P, 36).transpose(1, 0, 2).reshape(P, 288))
    put("router_bias", np.tile(np.concatenate([v["router_g_bias"][0], v["router_e_bias"][0]])[None], (P, 1)))
    rows = np.zeros((34, 8), f32)
    rows[0:32] = v["rpb_table"]
    rows[32, 0:4] = 1.0
    rows[33, 4:8] = 1.0
    put("rpb_rows", rows)
    rpb = np.zeros((8, 7, P), f32)
    rpb[:, :, 48:79] = v["l0_rpb_2"][:, 4:11, :]
    xt = np.ascontiguousarray(v["x"][0].T).reshape(KC, P, S)
    ct = np.ascontiguousarray(v["ctx_2"][0].T).reshape(KC, P, S)
    return {"wall": wall, "consts": shape_constants(), "params": par, "xin": xt, "ctxin": ct,
            "rpb_pad": rpb.reshape(8, 896)}


def kernel(**inputs):
    import concourse.bacc as bacc
    from concourse.bass_utils import run_bass_kernel_spmd

    nc = bacc.Bacc("TRN2", target_bir_lowering=False, num_devices=1)
    arrays = {k: np.ascontiguousarray(a) for k, a in lay_out({k: np.asarray(a) for k, a in inputs.items()}).items()}
    aps = [nc.dram_tensor(k, a.shape, F32, kind="ExternalInput").ap() for k, a in arrays.items()]
    out = nc.dram_tensor("out", [KC, P, S], F32, kind="ExternalOutput").ap()
    build(nc, *aps, out)
    r = run_bass_kernel_spmd(nc, [arrays], core_ids=[0])
    return np.ascontiguousarray(r.results[0]["out"].reshape(D, S).T[None])
```

```python
import math
from contextlib import ExitStack

import numpy as np

import concourse.bass as bass
from concourse import mybir

F32 = mybir.dt.float32
F32R = mybir.dt.float32r
ALU = mybir.AluOpType
ACT = mybir.ActivationFunctionType
AX = mybir.AxisListType

P = 128
D = 1024
KC = D // P
S = 256
NBANK = 8
RING = 6
SPLIT_RING = 3
BLOCKS = 8
TILE = BLOCKS * P
NEG = -1e30
TAKEN = -3e38
ALPHA1 = 2.0 ** 0.25
ALPHA2 = 4.0 ** 0.25
EXPERTS = 32
FF = 22
HF = FF // 2
ADA = 6 * D
CH = 64
NCH = S // CH
KEEP = 64
W_DECAY = math.exp(-0.5)

IN_NAMES = (("a_q", 256), ("a_k", 256), ("a_v", 256), ("b_q", 256), ("b_ckv", 64), ("b_iq", 256), ("b_ik", 32),
            ("b_iw", 8), ("c_q", 128), ("c_k", 128), ("c_v", 256), ("c_a", 16), ("c_g", 256), ("d", 832),
            ("gate", 4096))
IN_OFF = {}
_o = 0
for _n, _w in IN_NAMES:
    IN_OFF[_n] = _o
    _o += _w
IN_BLOCKS = ["iq0", "iq1", "ik", "iw", "ckv", "bq0", "bq1", "small", "dr0", "dr1", "dk0", "dk1", "dv0", "dv1",
             "cq", "ck", "cv0", "cv1", "cg0", "cg1", "aq0", "aq1", "ak0", "ak1", "av0", "av1"]
R_W, R_A, R_G, R_C = 0, 32, 64, 96


def stream_plan():
    order = [("in", 26), ("ada0", ADA // 128), ("ada1", ADA // 128), ("merge", 40), ("out", 8)]
    order += [("moe", 6 * EXPERTS)]
    order += [("l0in", 18), ("l0out", 8), ("l0upA", 24), ("l0downA", HF), ("l0upB", 20), ("l0downB", HF)]
    order += [("l1in", 9), ("l1uq", 12), ("l1ukv", 4), ("l1out", 8), ("l1upA", 24), ("l1downA", HF), ("l1upB", 20),
              ("l1downB", HF)]
    first, at = {}, 0
    for name, n in order:
        first[name] = at
        at += n
    return first, at, dict(order)


SPLIT = ("moe", "l0upA", "l0downA", "l0upB", "l0downB", "l1upA", "l1downA", "l1upB", "l1downB")
UP_A = HF + 1


def moe_tiles():
    tiles = []
    for e in range(EXPERTS):
        tiles += [("gate", e), ("up", e)]
        if e:
            tiles.append(("down", e - 1))
    return tiles + [("down", EXPERTS - 1)]


def columns(items):
    at, out = 0, {}
    for name, n in items:
        out[name] = (at, n)
        at += n
    return out, at


CONST_ITEMS = [("ident", 128), ("ones", 128), ("blockones", 128), ("zeros", 128), ("rot", 128),
               ("cos64", 256), ("sin64", 256), ("cosm", 256), ("sinm", 256), ("buckets", 512),
               ("na_mask", 256), ("upper", 64), ("upper_incl", 64), ("lower", 64), ("diag16", 64), ("eye64", 64),
               ("heads_c", 256), ("causal", 512), ("scan_ones", 64)]
PARAM_ITEMS = [("kv_gain", 1), ("c_a_bias", 1), ("c_norm_gain", 2), ("d_mu", 7), ("d_w0", 2), ("d_a0", 2),
               ("d_k_k", 2), ("d_k_a", 2), ("d_r_k", 2), ("d_gn_w", 2), ("d_gn_b", 2),
               ("ln1g", 8), ("ln2g", 8), ("ln1b", 8), ("ln2b", 8),
               ("bada0", 48), ("bada1", 48), ("q_gain", 1), ("k_gain", 1),
               ("l0ln1g", 8), ("l0ln1b", 8), ("l0ln2g", 8), ("l0ln2b", 8),
               ("l1ln1g", 8), ("l1ln1b", 8), ("l1ln2g", 8), ("l1ln2b", 8),
               ("l0conv", 66), ("l0convb", 22), ("l1conv", 66), ("l1convb", 22),
               ("cq_gain", 6), ("ckv_gain", 2), ("cond", 16),
               ("lora", 256), ("w_uv", 256), ("router", 288), ("router_bias", 36), ("rpb_rows", 8)]
CONST, NCONST = columns(CONST_ITEMS)
PARAM, NPARAM = columns(PARAM_ITEMS)


def build(nc, wall, consts, params, xin, ctxin, rpb_pad, out, upto=99):
    first, n_tiles, stage_tiles = stream_plan()
    split_order = [first[st] + n for st in SPLIT for n in range(stage_tiles[st])]
    split_at = {t: i for i, t in enumerate(split_order)}
    whole_at = {t: i for i, t in enumerate(t for t in range(n_tiles) if t not in split_at)}
    moe0 = first["moe"]

    def run_end(t):
        while t < n_tiles and (t in split_at) == ((t - 1) in split_at or t == 0):
            t += 1
        return t
    with ExitStack() as ctx:
        def sb(name, shape, dtype=F32):
            return ctx.enter_context(nc.sbuf_tensor(name, shape, dtype))

        def as_f32r(name, cols):
            return nc.alloc_sbuf_tensor_at(name, [P, cols], F32R, offset=nc.sbuf_base - 4 * cols)

        sems = {}

        def sem(name):
            if name not in sems:
                sems[name] = ctx.enter_context(nc.semaphore(name))
            return sems[name]

        ring = sb("ring", [P, RING, TILE])
        w_hi = sb("w_hi", [P, SPLIT_RING, TILE], F32R)
        w_lo = sb("w_lo", [P, SPLIT_RING, TILE], F32R)
        con = sb("con", [P, NCONST])
        par = sb("par", [P, NPARAM])
        XC = sb("XC", [P, KC, 2 * S])
        BIG = sb("BIG", [P, 3 * 4096])
        BIGR = as_f32r("BIG_f32r", 3 * 4096)
        MOD = sb("MOD", [P, 2, 48, 2])
        SC1 = sb("SC1", [P, 2, 2, 8, 2])
        SV = sb("SV", [P, 96])
        arena_n = 17472
        AR = sb("AR", [P, arena_n])
        ARR = as_f32r("AR_f32r", arena_n)
        ada_mat = sb("ada_mat", [P, 2, P])
        ps = [ctx.enter_context(nc.psum_tensor(f"bank{b}", [P, 512], F32))[:, :] for b in range(NBANK)]

        def c_(name):
            o, n = CONST[name]
            return con[:, o:o + n]

        def p_(name):
            o, n = PARAM[name]
            return par[:, o:o + n]

        class Arena:

            def __init__(self, region, size, start=0, region_f32r=None):
                self.region, self.size, self.at, self.region_f32r = region, size, start, region_f32r

            def take_f32r(self, *shape):
                return self.take(*shape, region=self.region_f32r)

            def take(self, *shape, region=None):
                n = int(np.prod(shape))
                a = (self.region if region is None else region)[:, self.at:self.at + n]
                self.at += n
                assert self.at <= self.size, (self.at, self.size)
                if len(shape) == 1:
                    return a
                names = "abcde"[:len(shape)]
                return a.rearrange(f"p ({' '.join(names)}) -> p {' '.join(names)}",
                                   **{k: v for k, v in zip(names[1:], shape[1:])})

        Z = BIG[:, 0:4096]
        SQ = BIG[:, 4096:8192]
        HB = BIG[:, 8192:12288]
        X1 = XC[:, :, 0:S]

        a1 = Arena(AR, arena_n)
        F = {}
        for name, n in (("iq", 2), ("ik", 1), ("ckv", 1), ("bq", 2), ("cq", 1), ("ck", 1), ("cg", 2), ("aq", 2),
                        ("ak", 2)):
            F[name] = a1.take(n, S)
        cv = a1.take(2, 256)
        av = a1.take(2, 256)
        vb = a1.take(2, 256)
        iw = a1.take(2, 8)
        dS = a1.take(7, S)
        ysT = a1.take(4, 2, S)
        small_act = a1.take(S)
        rows8 = a1.take(512)
        DZ = {n: a1.take(2, S) for n in ("w", "a", "g")}
        c_z = a1.take(S)
        a1_common = a1.at
        dF = a1.take(7, S + 1)
        dF_end = a1.at
        bA = Arena(BIG, 12288)
        bias1 = bA.take(8, 2, S)
        att1_L = bA.take(3, 512)
        att1_P = bA.take(3, 512)
        att1_PT = bA.take(3, 4, P)
        rel = bA.take(2, 2, S)
        score = bA.take(2, S)
        work = bA.take(2, 2, S)
        top8 = bA.take(2, 8)
        selm = bA.take(2, S)

        cC = Arena(BIG, 12288)
        C = {n: cC.take(S) for n in ("zb", "ab", "ln", "la", "cum", "ec", "en", "ed", "qd", "ki", "kd")}
        c_kdt = cC.take(2, P)
        c_att = cC.take(4, 2, CH)
        c_state = cC.take(3, S)
        c_sm = cC.take(3, S)
        c_o = cC.take(2, S)
        c_sq = cC.take(2, S)
        bD = Arena(BIG, 12288)
        DD = {n: bD.take(2, S) for n in ("lw", "cum", "cm1", "e1", "e2", "e3", "kk", "kp", "b", "Bh", "Kh", "t")}
        Ah = bD.take(2, S)
        Rh = bD.take(2, S)
        yT = bD.take(2, S)
        bn = bD.take(2, S)
        dU = Arena(BIG, 12288, bD.at)
        cU = Arena(AR, arena_n, a1_common)
        U = {n: dU.take(8, CH) for n in ("N", "A", "GRB", "GAK", "GRK", "Vt", "Bt", "Kt")}
        U |= {n: cU.take(8, CH) for n in ("D", "Dt", "D2", "D2t", "D4", "D4t", "Z", "W", "Lo")}
        U["D8"], U["D8t"] = U["D"], U["Dt"]
        U["Pm"], U["Pt"], U["P2t"], U["Y1"], U["T"] = U["D2"], U["D2t"], U["D4"], U["D4t"], U["Lo"]
        x_u = cU.take(2, 2, CH)
        m_st = cU.take(5, 2, CH)
        ada_rows = Arena(AR, arena_n, dF_end).take(4, 512)
        cM = Arena(AR, arena_n, a1_common)
        tmpm = cM.take(2, 2, 2, S)
        gates = cM.take(2, 4, S)
        mergedT = HB[:, 0:2048].rearrange("p (k t) -> p k t", k=KC)

        def ln_bufs(n):
            z = Z[:, 0:KC * n].rearrange("p (k t) -> p k t", k=KC)
            sq = SQ[:, 0:KC * n].rearrange("p (k t) -> p k t", k=KC)
            return z, sq

        lnst = sb("lnst", [P, 3, 512])

        aM = Arena(AR, arena_n, 0, ARR)
        gate_bc = aM.take(EXPERTS, S)
        m_sg = aM.take(2, 2, S)
        m_t = aM.take(2, 2, S)
        mh_hi = aM.take_f32r(2, 2, S)
        mh_lo = aM.take_f32r(2, 2, S)
        lg = aM.take(2, 36)
        rt = aM.take(2, 12, 32)
        gateT = aM.take(S)

        def in_split(n):
            return [BIGR[:, o:o + KC * n].rearrange("p (k t) -> p k t", k=KC) for o in (8192, 4096)]

        mx_hi = BIGR[:, 8192:10240].rearrange("p (k t) -> p k t", k=KC)
        mx_lo = BIGR[:, 10240:12288].rearrange("p (k t) -> p k t", k=KC)

        a2 = Arena(AR, arena_n)
        Q0 = a2.take(5, 512)
        qb = a2.take(4, 512)
        kb = a2.take(4, 512)
        V0 = a2.take(4, 640)
        yT0 = a2.take(8, 512)
        na_bias = a2.take(8, 2, S)
        H = HB.rearrange("p (k t) -> p k t", k=KC)
        aP = Arena(SQ, 4096)
        att2_P = aP.take(3, 512)
        att2_PT = aP.take(3, 4, P)
        aL = Arena(Z, 4096)
        att2_L = aL.take(3, 512)
        tq = aL.take(5, 512)
        tq2 = aP.region[:, 0:2560].rearrange("p (a b) -> p a b", a=5)

        aF = Arena(AR, arena_n, 0, ARR)
        u_hi = aF.take_f32r(HF, 512)
        u_lo = aF.take_f32r(HF, 512)
        u_raw = aF.take(2, 512)
        gp = aF.take(2, 2, S + 2)
        cg_ = aF.take(2, 512)
        sg_ = aF.take(2, 512)

        a3 = Arena(AR, arena_n)
        cq1 = a3.take(6, S)
        ckv1 = a3.take(2, 512)
        kr1 = a3.take(512)
        sq1 = a3.take(8, 512)
        q1 = a3.take(16, S)
        V1 = a3.take(4, 1024)
        kT1 = a3.take(2, 512)
        yT1 = Z[:, 2048:4096].rearrange("p (k t) -> p k t", k=KC)
        tq1 = SQ[:, 3072:4096].rearrange("p (a b) -> p a b", a=2)

        scr_t5 = nc.dram_tensor("t5_rows", [8, P, 512], F32, kind="Internal").ap()
        scr_na = nc.dram_tensor("na_rows", [8, CH, 896], F32, kind="Internal").ap()
        scr_ada = nc.dram_tensor("ada_results", [2, 2, ADA], F32, kind="Internal").ap()
        scr_gate = nc.dram_tensor("gate_rows", [EXPERTS, S], F32, kind="Internal").ap()

        bank_ready = [sem(f"bank_ready{b}") for b in range(NBANK)]
        bank_free = [sem(f"bank_free{b}") for b in range(NBANK)]
        w_ready = [sem(f"weights_in_slot{s}") for s in range(RING)]
        w_free = sem("ring_slots_freed")
        w_high = sem("weight_high_parts")
        w_split = sem("weight_tiles_split")
        w_used = sem("split_tiles_used")

        def spec(q, k, v, o, bias=None, nk=S, scale=0.125):
            return dict(q=q, k=k, v=v, o=o, bias=bias, nk=nk, scale=scale)

        att1, att2, att3 = [], [], []
        for br, (fq, fk, fv) in enumerate(((F["aq"], F["ak"], av), (F["bq"], None, vb))):
            for h in range(4):
                r = slice(64 * (h % 2), 64 * (h % 2) + 64)
                for i in range(2):
                    k = fk[r, h // 2, :] if br == 0 else F["ckv"][r, 0, :]
                    att1.append(spec(fq[r, h // 2, i * P:(i + 1) * P], k,
                                     [fv[:, t, h * 64:(h + 1) * 64] for t in range(2)],
                                     ysT[r, br, h // 2, i * P:(i + 1) * P], bias=bias1[:, 4 * br + h, i, :]))
        for h in range(16):
            r = slice(64 * (h % 2), 64 * (h % 2) + 64)
            for i in range(4):
                if h < 8:
                    j, g = h // 2, h % 2
                    q, kk, v0 = Q0[r, j, :], Q0[r, 4, :], 64 * g
                else:
                    j = (h - 8) // 2
                    q, kk, v0 = qb[r, j, :], kb[r, j, :], P + 64 * (h - 8)
                y = yT0[r, h // 2, i * P:(i + 1) * P]
                if i < 2:
                    b = na_bias[:, h - 8, i, :] if h >= 8 else None
                    att2.append(spec(q[:, i * P:(i + 1) * P], kk, [V0[:, t, v0:v0 + 64] for t in range(4)], y, b, 512))
                else:
                    att2.append(spec(q[:, i * P:(i + 1) * P], kk[:, S:2 * S],
                                     [V0[:, t, v0:v0 + 64] for t in (2, 3)], y, None, S))
        for h in range(16):
            for i in range(2):
                att3.append(spec(q1[0:96, h, i * P:(i + 1) * P], kT1[0:96, h % 2, :],
                                 [V1[:, t, h * 64:(h + 1) * 64] for t in range(4)],
                                 yT1[64 * (h % 2):64 * (h % 2) + 64, h // 2, i * P:(i + 1) * P],
                                 None, 512, 96 ** -0.5))

        def att_order(st, n):
            for i in range(n + 3):
                if st == "att3" and i % 2 == 0 and i < n:
                    yield ("kT", i // 2)
                if i < n:
                    yield (st, "S", i)
                if 0 <= i - 2 < n:
                    yield (st, "T", i - 2)
                if 0 <= i - 3 < n:
                    yield (st, "O", i - 3)

        before_ = {"att1": 0, "att2": len(att1), "att3": len(att1) + len(att2)}
        exp_before = {"att1": 0, "att2": len(att1), "att3": len(att1) + 16}

        def nth(which):
            return KC * "abcdef".index(which)

        FAM1 = ["N", "A", "GRB", "GAK", "GRK", "Vt", "Bt", "Kt"]
        FAM2 = ["D2", "D2t", "Z1", "W1", "D4", "D4t", "Z2", "W2", "D8", "D8t", "Z3", "W3", "Pm", "Pt", "P2t", "Y1", "T"]
        plan = []

        def add(*names):
            plan.extend(names)

        add("t5")
        add(*[("in", b) for b in range(26)])
        add("ckvms", "vb")
        add(*[("ix", i, b) for i in range(2) for b in range(4)])
        add("dw", "da", "dg", "ca")
        add(*[("ada", l, g, q) for l in range(2) for g in range(ADA // 1024) for q in range(2)])
        add(*att_order("att1", 16))
        add("ckd", *[("catt", h) for h in range(4)], *[("cupd", c) for c in range(3)], *[("co", hp, q) for hp in range(2) for q in range(2)], "coms")
        add("kkn")
        for fam in FAM1 + FAM2:
            add((fam, 0), (fam, 1))
        for c in range(NCH):
            for what in ("X", "U", "Yc", "M"):
                if what == "M" and c == NCH - 1:
                    continue
                add((what, c, 0), (what, c, 1))
        add("bonus", "ymean", "yvar")
        add(("adaT", 0), ("adaT", 1))
        for m in range(KC):
            add(("gt", m, 0), ("gt", m, 1), ("br", m, 0), ("br", m, 1))
        add(*[("out1", m) for m in range(KC)], ("mean", "a"), ("var", "a"))
        add(("rt", 0), ("rt", 1), "gateT")
        plan.append("MOE")
        add(("mean", "b"), ("var", "b"))
        add(*[("l0in", m) for m in range(18)])
        add(*[("qms", m) for m in range(5)], *[("rope0", m) for m in range(5)])
        add(*att_order("att2", 64))
        add(*[("l0out", m) for m in range(KC)], ("mean", "c"), ("var", "c"))
        for half, chunks in enumerate((range(UP_A), range(UP_A, FF))):
            for j in chunks:
                add(("l0g", j), ("l0v", j))
            add(*[("l0down", half, m) for m in range(KC)])
        add(("mean", "d"), ("var", "d"))
        add(*[("l1in", m) for m in range(9)], "cqms", "ckvms1")
        add("krope", *[("uq", m) for m in range(8)], *[("qrope", m) for m in range(8)])
        plan.append("UKV")
        add(*[("v1", t, hf) for hf in range(2) for t in range(4)])
        add(*att_order("att3", 32))
        add(*[("l1out", m) for m in range(KC)], ("mean", "e"), ("var", "e"))
        for half, chunks in enumerate((range(UP_A), range(UP_A, FF))):
            for j in chunks:
                add(("l1g", j), ("l1v", j))
            add(*[("l1down", half, m) for m in range(KC)])
        add(("mean", "f"), ("var", "f"))
        job, at, uses = {}, 0, [0] * NBANK
        moe_uses = None
        for name in plan:
            if name == "MOE":
                moe_uses = list(uses)
                continue
            if name == "UKV":
                continue
            b = at % NBANK
            uses[b] += 1
            job[name] = (b, uses[b])
            at += 1

        def bank(eng, name):
            b, use = job[name]
            eng.wait_ge(bank_ready[b], use)
            return ps[b]

        def evacuated(eng, name):
            b, use = job[name]
            eng.wait_ge(bank_free[b], use)

        def frees(ins, name):
            ins.then_inc(bank_free[job[name][0]], 1)

        def bc(ap, n):
            return ap.unsqueeze(1).broadcast_to([ap.shape[0], n, ap.shape[1]])

        block = ctx.enter_context(nc.Block())

        @block.sync
        def _(sp):
            for t in range(RING):
                sp.dma_start(ring[:, t, :], wall[t]).then_inc(w_ready[t], 16)
            t = RING
            while t < n_tiles:
                old = t - RING
                place = split_at if old in split_at else whole_at
                freed = w_split if old in split_at else w_free
                end = min(run_end(old + 1) + RING, n_tiles)
                rounds = (end - t) // RING
                if rounds > 1:
                    with sp.Fori(0, rounds) as r:
                        for q in range(RING):
                            sp.wait_ge(freed, r * RING + (place[old] + q + 1))
                            sp.dma_start(ring[:, (t + q) % RING, :], wall[r * RING + (t + q)])\
                                .then_inc(w_ready[(t + q) % RING], 16)
                    t += rounds * RING
                while t < end:
                    sp.wait_ge(freed, place[t - RING] + 1)
                    sp.dma_start(ring[:, t % RING, :], wall[t]).then_inc(w_ready[t % RING], 16)
                    t += 1
            for k in range(KC):
                sp.wait_ge(sem("result_chunks"), k + 1)
                sp.dma_start(out[k], X1[:, k, :]).then_inc(sem("stored"), 16)
            sp.wait_ge(sem("stored"), 16 * KC)

        @block.gpsimd
        def _(gp_):
            gp_.dma_start(scr_na, bass.AP(rpb_pad.tensor, 0, [[896, 8], [0, CH], [1, 896]])).then_inc(sem("na_rows"), 16)
            gp_.wait_ge(sem("t5_row_ready"), 1)
            for h in range(8):
                gp_.dma_start(bass.AP(scr_t5.tensor, h * P * 512, [[P * 512, 1], [512, P], [1, 512]]),
                              rows8[h:h + 1, :].unsqueeze(1).broadcast_to([1, P, 512])).then_inc(sem("t5_rows"), 16)
            gp_.wait_ge(sem("t5_rows"), 16 * 8)
            for i in range(2):
                src = bass.AP(scr_t5.tensor, 255 - P * i, [[511, P], [P * 512, 8], [1, S]])
                gp_.dma_start(bias1[:, :, i, :], src).then_inc(sem("bias1"), 16)
            n = 0
            for l in range(2):
                for g in range(ADA // 512):
                    gp_.wait_ge(sem("ada_row"), n + 1)
                    n += 1
                    gp_.dma_start(scr_ada[l, :, g * 512:(g + 1) * 512], ada_rows[0:2, g % 4, :])\
                        .then_inc(sem(f"ada_row_stored{g % 4}"), 16)
                for q in range(4):
                    gp_.wait_ge(sem(f"ada_row_stored{q}"), 16 * 3 * (l + 1))
                gp_.dma_start(ada_mat[0:96, l, :], scr_ada[l].rearrange("s (m p) -> (s m) p", p=P))\
                    .then_inc(sem(f"ada_mat{l}"), 16)
            gp_.wait_ge(sem("gateT_ready"), 1)
            gp_.dma_start(scr_gate, gateT[0:EXPERTS, :]).then_inc(sem("gate_rows"), 16)
            gp_.wait_ge(sem("gate_rows"), 16)
            gp_.dma_start(gate_bc, bass.AP(scr_gate.tensor, 0, [[0, P], [S, EXPERTS], [1, S]])).then_inc(sem("gate_bc"), 16)
            gp_.wait_ge(sem("na_rows"), 16)
            gp_.wait_ge(sem("moe_hidden"), EXPERTS)
            for h in range(8):
                for i in range(2):
                    for r in range(2):
                        src = bass.AP(scr_na.tensor, h * CH * 896 + (3 - 2 * i - r) * P + 63,
                                      [[895, CH], [P, 4], [1, CH]])
                        dst = na_bias[64 * r:64 * r + 64, h, i, :].rearrange("p (a b) -> p a b", a=4)
                        gp_.dma_start(dst, src).then_inc(sem("na_bias"), 16)

        @block.tensor
        def _(pe):
            state = {"tile": None, "held": 1, "pending": None, "at": 0}

            def open_(name):
                b, use = job[name]
                while plan[state["at"]] in ("MOE", "UKV"):
                    state["at"] += 1
                assert plan[state["at"]] == name, (plan[state["at"]], name)
                state["at"] += 1
                if use > 1:
                    pe.wait_ge(bank_free[b], use - 1)
                return ps[b]

            def mm(o, lhsT, rhs, start=True, stop=True, done=None, **kw):
                ins = nc.tensor.matmul(o, lhsT, rhs, start=start, stop=stop, **kw)
                note(ins, done)

            def note(ins, done):
                if done is not None:
                    ins.then_inc(bank_ready[job[done][0]], 1)
                elif state["pending"] is not None:
                    ins.then_inc(*state["pending"])
                    state["pending"] = None

            def tile(stage, n):
                t = first[stage] + n
                if t != state["tile"]:
                    if state["tile"] is not None:
                        assert t == state["tile"] + 1, (stage, n, state)
                        free = w_used if state["tile"] in split_at else w_free
                        more = 0
                        if state["pending"] is not None:
                            assert state["pending"][0] is free
                            more = state["pending"][1]
                        state["pending"] = (free, state["held"] + more)
                        state["held"] = 1
                    if t in split_at:
                        pe.wait_ge(w_split, split_at[t] + 1)
                    else:
                        pe.wait_ge(w_ready[t % RING], 16 * (t // RING + 1))
                    state["tile"] = t
                if t in split_at:
                    return w_hi[:, split_at[t] % SPLIT_RING, :], w_lo[:, split_at[t] % SPLIT_RING, :]
                return ring[:, t % RING, :]

            def hold(stage, n0, n):
                ws = [tile(stage, n0)]
                for q in range(1, n):
                    t = first[stage] + n0 + q
                    pe.wait_ge(w_ready[t % RING], 16 * (t // RING + 1))
                    ws.append(ring[:, t % RING, :])
                state["tile"], state["held"] = first[stage] + n0 + n - 1, n
                return ws

            def split_product(o, w, blk, x_hi, x_lo, start, stop, done=None, **kw):
                cs = slice(blk * P, (blk + 1) * P)
                terms = ((w[0], x_lo), (w[1], x_hi), (w[0], x_hi))
                for n, (a, b_) in enumerate(terms):
                    ins = nc.tensor.matmul(o, a[:, cs], b_, start=start and n == 0, stop=stop and n == 2, **kw)
                    if n == 2 and done is not None:
                        ins.then_inc(done, 1)
                    elif n == 0:
                        note(ins, None)

            def split_linear(name, stage, n0, nk, x, o):
                for k in range(nk):
                    w = tile(stage, (n0 + k) // BLOCKS)
                    split_product(o, w, (n0 + k) % BLOCKS, x[0][:, k, :], x[1][:, k, :], k == 0, k == nk - 1,
                                  bank_ready[job[name][0]] if k == nk - 1 else None)

            def wblk(stage, n):
                return tile(stage, n // BLOCKS)[:, (n % BLOCKS) * P:(n % BLOCKS + 1) * P]

            def linear(name, stage, n0, nk, x, o=None, done=True):
                b = open_(name) if o is None else o
                for k in range(nk):
                    mm(b, wblk(stage, n0 + k), x(k), k == 0, k == nk - 1, name if done and k == nk - 1 else None)

            def transpose(o, i, ident, done=None):
                note(nc.tensor.transpose(o, i, ident), done)

            ident = c_("ident")

            def attention(st, specs, before, ukv=None):
                for item in att_order(st, len(specs)):
                    if item[0] == "kT":
                        h = item[1]
                        b = open_(item)
                        for k in range(2):
                            mm(b[0:64, :], ukv[2 + k][:, h * 64:h * 64 + 64],
                               ckv1[:, k, :], k == 0, k == 1, item if k == 1 else None)
                        continue
                    _, what, i = item
                    s = specs[i]
                    b = open_(item)
                    nk = s["nk"]
                    if what == "S":
                        before(i)
                        mm(b[:, 0:nk], s["q"], s["k"], done=item)
                    elif what == "T":
                        pe.wait_ge(sem("att_probs"), before_[st] + i + 1)
                        Pb = att1_P if st == "att1" else att2_P
                        for t in range(nk // P):
                            transpose(b[:, t * P:(t + 1) * P], Pb[:, i % 3, t * P:(t + 1) * P], ident,
                                      item if t == nk // P - 1 else None)
                    else:
                        evacuated(pe, (st, "T", i))
                        PT = att1_PT if st == "att1" else att2_PT
                        r0 = 64 * (s["o"].start_partition() // 64)
                        for t in range(nk // P):
                            mm(b[r0:r0 + 64, 0:P], s["v"][t], PT[:, i % 3, t, :], t == 0, t == nk // P - 1,
                               item if t == nk // P - 1 else None)

            def norm_sums(which, n):
                z, sq = ln_bufs(n)
                for what, src in (("mean", z), ("var", sq)):
                    b = open_((what, which))
                    for k in range(KC):
                        pe.wait_ge(sem(f"{what}_in"), nth(which) + k + 1)
                        mm(b[:, 0:n], c_("ones"), src[:, k, :], k == 0, k == KC - 1,
                           (what, which) if k == KC - 1 else None)

            pe.wait_ge(sem("params_in"), 16)
            pe.wait_ge(sem("consts_in"), 16)
            b = open_("t5")
            mm(b[0:8, :], p_("rpb_rows")[0:34, :], c_("buckets")[0:34, :], done="t5")
            pe.wait_ge(sem("x_in"), 16)
            for n, name in enumerate(IN_BLOCKS):
                if name in ("iw", "cv0", "cv1", "av0", "av1"):
                    w = 8 if name == "iw" else P
                    b = open_(("in", n))
                    for t in range(2):
                        for k in range(KC):
                            mm(b[:, t * w:(t + 1) * w], X1[:, k, t * P:(t + 1) * P], wblk("in", n * KC + k)[:, 0:w],
                               k == 0, k == KC - 1, ("in", n) if t == 1 and k == KC - 1 else None)
                else:
                    b = open_(("in", n))
                    linear(("in", n), "in", n * KC, KC, lambda k: X1[:, k, :], b[:, 0:S])
            b = open_("ckvms")
            pe.wait_ge(sem("ckv_sq"), 1)
            mm(b[:, 0:S], c_("blockones"), rel[:, 0, 0, :], done="ckvms")
            b = open_("vb")
            pe.wait_ge(sem("ckv_normed"), 1)
            for t in range(2):
                mm(b[:, t * 256:(t + 1) * 256], F["ckv"][0:64, 0, t * P:(t + 1) * P], p_("w_uv")[0:64, :],
                   done="vb" if t else None)
            for i in range(2):
                for q in range(4):
                    b = open_(("ix", i, q))
                    r = slice(32 * q, 32 * q + 32)
                    for m in range(2):
                        mm(b[:, m * S:(m + 1) * S], F["iq"][r, m, i * P:(i + 1) * P], F["ik"][r, 0, :],
                           done=("ix", i, q) if m else None)
            pe.wait_ge(sem("small_act"), 4)
            for name, r0, k in (("dw", R_W, 16), ("da", R_A, 16), ("dg", R_G, 32)):
                b = open_(name)
                for m in range(2):
                    mm(b[:, m * S:(m + 1) * S], p_("lora")[r0:r0 + k, m * P:(m + 1) * P], small_act[r0:r0 + k, :],
                       done=name if m else None)
            b = open_("ca")
            mm(b[:, 0:S], p_("lora")[R_C:R_C + 16, 0:P], small_act[R_C:R_C + 16, :], done="ca",
               tile_position=(96, 0))
            pe.wait_ge(sem("cond_silu"), 1)
            cond = p_("cond").rearrange("p (k s) -> p k s", k=KC)
            for l in range(2):
                for g in range(ADA // 1024):
                    bs = [open_(("ada", l, g, q)) for q in range(2)]
                    for k in range(KC):
                        for q in range(2):
                            mm(bs[q][0:2, :], cond[:, k, :], tile(f"ada{l}", g * KC + k)[:, q * 512:(q + 1) * 512],
                               k == 0, k == KC - 1, ("ada", l, g, q) if k == KC - 1 else None)
            for i in (24, 25):
                evacuated(pe, ("in", i))
            evacuated(pe, "vb")
            attention("att1", att1, lambda i: None)
            if upto <= 1:
                return
            b = open_("ckd")
            pe.wait_ge(sem("c_feat"), 1)
            for t in range(2):
                transpose(b[:, t * P:(t + 1) * P], C["kd"][:, t * P:(t + 1) * P], ident, "ckd" if t else None)
            for h in range(4):
                b = open_(("catt", h))
                r = slice(32 * h, 32 * h + 32)
                for c in range(NCH):
                    o = b[64 * (c % 2):64 * (c % 2) + 64, (c // 2) * CH:(c // 2 + 1) * CH]
                    mm(o, C["ki"][r, c * CH:(c + 1) * CH], C["qd"][r, c * CH:(c + 1) * CH],
                       done=("catt", h) if c == NCH - 1 else None, tile_position=(32 * h, 64 * (c % 2)))
            evacuated(pe, "ckd")
            for c in range(3):
                b = open_(("cupd", c))
                r = slice(64 * (c % 2), 64 * (c % 2) + 64)
                mm(b[:, 0:S], c_kdt[r, c // 2, :], cv[r, c // 2, :], done=("cupd", c))
            for h in range(4):
                evacuated(pe, ("catt", h))
            pe.wait_ge(sem("c_states"), 3)
            for hp in range(2):
                for par_ in range(2):
                    b = open_(("co", hp, par_))
                    r = slice(64 * par_, 64 * par_ + 64)
                    for n in range(2):
                        c = 2 * n + par_
                        for q in range(2):
                            h = 2 * hp + q
                            mm(b[64 * q:64 * q + 64, n * CH:(n + 1) * CH], cv[r, n, h * 64:(h + 1) * 64],
                               c_att[r, h, n, :], True, c == 0, skip_group_check=True)
                        if c:
                            mm(b[:, n * CH:(n + 1) * CH], c_sm[:, c - 1, hp * P:(hp + 1) * P],
                               C["qd"][:, c * CH:(c + 1) * CH], False, True, ("co", hp, par_) if n else None,
                               skip_group_check=True)
            b = open_("coms")
            pe.wait_ge(sem("c_sq"), 1)
            mm(b, c_("blockones"), c_sq.rearrange("p a b -> p (a b)"), done="coms")
            if upto <= 2:
                return
            b = open_("kkn")
            pe.wait_ge(sem("d_kk_sq"), 1)
            mm(b, c_("blockones"), DD["t"].rearrange("p a b -> p (a b)"), done="kkn")
            pe.wait_ge(sem("d_feat"), 1)

            def family(name, f):
                for p in range(2):
                    b = open_((name, p))
                    r = slice(64 * p, 64 * p + 64)
                    for u in range(8):
                        lhsT, rhs = f(r, u)
                        mm(b[r, u * CH:(u + 1) * CH], lhsT, rhs, done=(name, p) if u == 7 else None)

            def tok(x):
                return lambda r, u: x[r, u // NCH, (u % NCH) * CH:(u % NCH + 1) * CH]

            def unit(x):
                return lambda r, u: U[x][r, u, :]

            def pair(a, b2):
                return lambda r, u: (a(r, u), b2(r, u))

            eye = lambda r, u: ident[r, r.start:r.start + 64]
            family("N", pair(tok(DD["Bh"]), tok(Ah)))
            family("A", pair(tok(Ah), tok(DD["Bh"])))
            family("GRB", pair(tok(DD["Bh"]), tok(Rh)))
            family("GAK", pair(tok(DD["Kh"]), tok(Ah)))
            family("GRK", pair(tok(DD["Kh"]), tok(Rh)))
            family("Vt", pair(lambda r, u: dS[r, 5 + u // NCH, (u % NCH) * CH:(u % NCH + 1) * CH], eye))
            family("Bt", pair(tok(DD["Bh"]), eye))
            family("Kt", pair(tok(DD["Kh"]), eye))
            pe.wait_ge(sem("d_split"), 5)
            steps = [("D2", "Dt", "D"), ("D2t", "D", "Dt"), ("Z1", "D2t", "Z"), ("W1", "D2", "W"),
                     ("D4", "D2t", "D2"), ("D4t", "D2", "D2t"), ("Z2", "D4t", "Z"), ("W2", "D4", "W"),
                     ("D8", "D4t", "D4"), ("D8t", "D4", "D4t"), ("Z3", "D8t", "Z"), ("W3", "D8", "W"),
                     ("Pm", "W", "Lo"), ("Pt", "Lo", "W"), ("P2t", "Pm", "Pt"), ("Y1", "P2t", "Z"), ("T", "Pt", "Y1")]
            wrote = {"D": None, "Dt": None, "Z": None, "W": None, "Lo": None}
            for name, l, r_ in steps:
                for src in (l, r_):
                    if wrote.get(src):
                        for p in range(2):
                            evacuated(pe, (wrote[src], p))
                family(name, pair(unit(l), unit(r_)))
                wrote[{"Z1": "Z", "Z2": "Z", "Z3": "Z", "W1": "W", "W2": "W", "W3": "W"}.get(name, name)] = name
            for p in range(2):
                evacuated(pe, ("T", p))
            for c in range(NCH):
                def per_pair(what, terms):
                    for p in range(2):
                        b = open_((what, c, p))
                        r = slice(64 * p, 64 * p + 64)
                        for m in range(2):
                            ts = terms(r, m)
                            for n, (l, r_) in enumerate(ts):
                                mm(b[r, m * CH:(m + 1) * CH], l, r_, n == 0, n == len(ts) - 1,
                                   (what, c, p) if m == 1 and n == len(ts) - 1 else None)
                cs = slice(c * CH, (c + 1) * CH)
                if c:
                    pe.wait_ge(sem("d_state"), 2 * c)
                per_pair("X", lambda r, m: ([(Ah[r, m, cs], m_st[r, c, m, :])] if c else [])
                         + [(U["GAK"][r, 4 * m + c, :], U["Vt"][r, 4 * m + c, :])])
                for p in range(2):
                    evacuated(pe, ("X", c, p))
                per_pair("U", lambda r, m: [(U["T"][r, 4 * m + c, :], x_u[r, 0, m, :])])
                for p in range(2):
                    evacuated(pe, ("U", c, p))
                per_pair("Yc", lambda r, m: ([(m_st[r, c, m, :], Rh[r, m, cs])] if c else [])
                         + [(x_u[r, 1, m, :], U["GRB"][r, 4 * m + c, :]), (U["Vt"][r, 4 * m + c, :], U["GRK"][r, 4 * m + c, :])])
                if c < NCH - 1:
                    per_pair("M", lambda r, m: [(U["Bt"][r, 4 * m + c, :], x_u[r, 1, m, :]),
                                                (U["Kt"][r, 4 * m + c, :], U["Vt"][r, 4 * m + c, :])])
            for name, src, s_ in (("bonus", bn, "d_bonus_in"), ("ymean", yT, "d_y"), ("yvar", DD["t"], "d_ysq")):
                b = open_(name)
                pe.wait_ge(sem(s_), 1)
                mm(b, c_("blockones"), src.rearrange("p a b -> p (a b)"), done=name)
            for l in range(2):
                b = open_(("adaT", l))
                pe.wait_ge(sem(f"ada_mat{l}"), 16)
                transpose(b[:, 0:96], ada_mat[0:96, l, :], ident[0:96, 0:96], ("adaT", l))
            if upto <= 3:
                return
            pe.wait_ge(sem("ys_ready"), 4)
            for m in range(KC):
                for half in range(2):
                    b = open_(("gt", m, half))
                    for n in (2 * half, 2 * half + 1):
                        for k in range(KC):
                            mm(b[:, (n % 2) * S:(n % 2 + 1) * S], wblk("merge", m * 40 + n * KC + k), X1[:, k, :],
                               k == 0, k == KC - 1, ("gt", m, half) if n % 2 and k == KC - 1 else None)
                for half in range(2):
                    b = open_(("br", m, half))
                    for n in (2 * half, 2 * half + 1):
                        for k in range(2):
                            mm(b[:, (n % 2) * S:(n % 2 + 1) * S], wblk("merge", m * 40 + 32 + n * 2 + k),
                               ysT[:, n, k, :], k == 0, k == 1, ("br", m, half) if n % 2 and k == 1 else None)
            pe.wait_ge(sem("merged"), KC)
            for m in range(KC):
                b = open_(("out1", m))
                linear(("out1", m), "out", m * KC, KC, lambda k: mergedT[:, k, :], b[:, 0:S])
            norm_sums("a", S)
            pe.wait_ge(sem("ln_out"), KC)
            router = p_("router").rearrange("p (k n) -> p k n", k=KC)
            for t in range(2):
                b = open_(("rt", t))
                for k in range(KC):
                    mm(b[:, 0:36], X1[:, k, t * P:(t + 1) * P], router[:, k, :], k == 0, k == KC - 1,
                       ("rt", t) if k == KC - 1 else None)
            b = open_("gateT")
            for t in range(2):
                pe.wait_ge(sem("gate_ready"), t + 1)
                transpose(b[0:EXPERTS, t * P:(t + 1) * P], rt[:, t, 11, :], ident, "gateT" if t else None)
            if upto <= 4:
                return
            for bb in range(NBANK):
                pe.wait_ge(bank_free[bb], moe_uses[bb])
            for bb in range(4):
                mm(ps[4 + bb][:, :], c_("zeros"), con[:, 0:512], True, False, skip_group_check=True)

            pe.wait_ge(sem("x_split"), KC)

            def split_tile(n, r=None, last=False):
                pe.wait_ge(w_split, n + 1 if r is None else r * 12 + (n + 1))
                state["pending"] = (w_used, 1)
                return w_hi[:, n % SPLIT_RING, :], w_lo[:, n % SPLIT_RING, :]

            def hidden(e_par, base, r=None):
                for part in range(2):
                    b = ps[2 * e_par + part]
                    for m in range(2):
                        n = base + 2 * part + m
                        w = split_tile(n, r)
                        if n == 0:
                            state["pending"] = (w_free, 1)
                        for k in range(KC):
                            split_product(b[:, m * S:(m + 1) * S], w, k, mx_hi[:, k, :], mx_lo[:, k, :],
                                          k == 0, k == KC - 1,
                                          sem("moe_gate" if part == 0 else "moe_up") if m == 1 and k == KC - 1 else None)

            def down(e_par, base, r=None, last=False):
                for k in range(2):
                    w = split_tile(base + k, r)
                    for m in range(KC):
                        split_product(ps[4 + m // 2][:, (m % 2) * S:(m % 2 + 1) * S], w, m, mh_hi[:, e_par, k, :],
                                      mh_lo[:, e_par, k, :], False, last and k == 1 and m % 2 == 1,
                                      sem("moe_down") if k == 1 and m == KC - 1 else None, skip_group_check=True)

            hidden(0, 0)
            with pe.Fori(0, (EXPERTS - 2) // 2) as r:
                for s in range(2):
                    hidden((1 + s) % 2, 4 + 6 * s, r)
                    pe.wait_ge(sem("moe_hidden"), r * 2 + (s + 1))
                    down(s % 2, 8 + 6 * s, r)
            end = 4 + 6 * (EXPERTS - 2)
            hidden(1, end)
            pe.wait_ge(sem("moe_hidden"), EXPERTS - 1)
            down(0, end + 4)
            pe.wait_ge(sem("moe_hidden"), EXPERTS)
            down(1, end + 6, last=True)
            state["tile"] = first["moe"] + stage_tiles["moe"] - 1
            pe.wait_ge(sem("z_written"), KC)
            norm_sums("b", S)
            if upto <= 5:
                return
            pe.wait_ge(sem("h_ready"), 2 * KC)
            for n in range(18):
                b = open_(("l0in", n))
                if n == 5 or n >= 14:
                    for t in range(4):
                        for k in range(KC):
                            mm(b[:, t * P:(t + 1) * P], H[:, k, t * P:(t + 1) * P], wblk("l0in", n * KC + k),
                               k == 0, k == KC - 1, ("l0in", n) if t == 3 and k == KC - 1 else None)
                else:
                    linear(("l0in", n), "l0in", n * KC, KC, lambda k: H[:, k, :], b)
            for m in range(5):
                b = open_(("qms", m))
                pe.wait_ge(sem("q0_sq"), m + 1)
                mm(b, c_("blockones"), tq2[:, m, :], done=("qms", m))
            for m in range(5):
                b = open_(("rope0", m))
                pe.wait_ge(sem("q0_normed"), m + 1)
                mm(b[:, 0:S], c_("rot"), Q0[:, m, 0:S], done=("rope0", m))
            pe.wait_ge(sem("q0_roped"), 5)
            for n in range(17, 5, -1):
                evacuated(pe, ("l0in", n))
            evacuated(pe, ("l0in", 5))
            attention("att2", att2, lambda i: None)
            evacuated(pe, ("att2", "O", 63))
            for m in range(KC):
                b = open_(("l0out", m))
                linear(("l0out", m), "l0out", m * KC, KC, lambda k: yT0[:, k, :], b)
            norm_sums("c", 512)

            def ffn(l, n):
                pe.wait_ge(sem("h_split"), KC * (l + 1))
                x = in_split(n)
                u = [u_hi[:, :, 0:n], u_lo[:, :, 0:n]]
                for half, part in enumerate("AB"):
                    chunks = range(UP_A) if half == 0 else range(UP_A, FF)
                    for j in chunks:
                        for q, nm in enumerate((f"l{l}g", f"l{l}v")):
                            b = open_((nm, j))
                            split_linear((nm, j), f"l{l}up{part}", (j - chunks[0]) * 16 + q * KC, KC, x, b[:, 0:n])
                    pe.wait_ge(sem("ff_split"), l * FF + (half + 1) * HF)
                    for m in range(KC):
                        b = open_((f"l{l}down", half, m))
                        split_linear((f"l{l}down", half, m), f"l{l}down{part}", m * HF, HF, u, b[:, 0:n])

            ffn(0, 512)
            norm_sums("d", 512)
            if upto <= 6:
                return
            pe.wait_ge(sem("h_ready"), 4 * KC)
            for n in range(9):
                b = open_(("l1in", n))
                w = 512 if n < 3 else S
                linear(("l1in", n), "l1in", n * KC, KC, lambda k: H[:, k, 0:w], b[:, 0:w])
            b = open_("cqms")
            pe.wait_ge(sem("cq_sq"), 1)
            for k in range(6):
                mm(b[:, 0:S], c_("ones"), sq1[:, k, 0:S], k == 0, k == 5, "cqms" if k == 5 else None)
            b = open_("ckvms1")
            for k in range(2):
                mm(b, c_("ones"), sq1[:, 6 + k, :], k == 0, k == 1, "ckvms1" if k == 1 else None)
            b = open_("krope")
            evacuated(pe, ("l1in", 2))
            mm(b[64:96, 0:S], c_("rot")[64:96, 64:96], kr1[64:96, 0:S], done="krope")
            pe.wait_ge(sem("cq_normed"), 6)
            for m in range(8):
                b = open_(("uq", m))
                for q in range(2):
                    for k in range(6):
                        mm(b[:, q * S:(q + 1) * S], wblk("l1uq", (2 * m + q) * 6 + k), cq1[:, k, :], k == 0, k == 5,
                           ("uq", m) if q and k == 5 else None)
            for m in range(8):
                b = open_(("qrope", m))
                evacuated(pe, ("uq", m))
                mm(b[0:96, :], c_("rot")[0:96, 0:96], q1[0:96, 2 * m:2 * m + 2, :].rearrange("p a b -> p (a b)"),
                   done=("qrope", m))
            pe.wait_ge(sem("ckv_normed1"), 2)
            ukv = hold("l1ukv", 0, 4)
            for hf in range(2):
                for t in range(4):
                    b = open_(("v1", t, hf))
                    for k in range(2):
                        mm(b, ckv1[:, k, t * P:(t + 1) * P],
                           ukv[k][:, hf * 512:(hf + 1) * 512], k == 0, k == 1,
                           ("v1", t, hf) if k else None)
            pe.wait_ge(sem("q1_roped"), 8)
            pe.wait_ge(sem("kr_placed"), 2)

            def before3(i):
                evacuated(pe, ("kT", i // 2))

            for hf in range(2):
                for t in range(4):
                    evacuated(pe, ("v1", t, hf))
            attention("att3", att3, before3, ukv)
            evacuated(pe, ("att3", "O", 31))
            for m in range(KC):
                b = open_(("l1out", m))
                linear(("l1out", m), "l1out", m * KC, KC, lambda k: yT1[:, k, :], b[:, 0:S])
            norm_sums("e", S)
            ffn(1, S)
            norm_sums("f", S)

        @block.scalar
        def _(act):
            seq = [0]
            chain = sem("act_seq")

            def step(ins, name=None):
                if name is None:
                    seq[0] += 1
                    ins.then_inc(chain, 1)
                    act.wait_ge(chain, seq[0])
                else:
                    counts[name] = counts.get(name, 0) + 1
                    ins.then_inc(sem(name), 1)
                    act.wait_ge(sem(name), counts[name])

            counts = {}

            def tell(ins, name):
                counts[name] = counts.get(name, 0) + 1
                ins.then_inc(sem(name), 1)

            f = nc.scalar.activation
            fed = [0]

            def feed(stage, n):
                t = first[stage] + n
                upto_ = split_at[min(t + SPLIT_RING, run_end(t + 1)) - 1] + 1
                for i in range(fed[0], upto_):
                    t = split_order[i]
                    act.wait_ge(w_ready[t % RING], 16 * (t // RING + 1))
                    if i >= SPLIT_RING:
                        act.wait_ge(w_used, i - SPLIT_RING + 1)
                    f(w_hi[:, i % SPLIT_RING, :], ring[:, t % RING, :], ACT.Copy).then_inc(w_high, 1)
                fed[0] = max(fed[0], upto_)

            def attention(st, specs, Pb, PT, L):
                n = len(specs)
                for i in range(n + 3):
                    if i < n:
                        s = specs[i]
                        nk = s["nk"]
                        act.wait_ge(sem("att_negmax"), before_[st] + i + 1)
                        if i >= 3:
                            act.wait_ge(bank_ready[job[(st, "T", i - 3)][0]], job[(st, "T", i - 3)][1])
                        den = SV[:, 8 + i % 4:9 + i % 4]
                        nm = SV[:, i % 4:i % 4 + 1]
                        if s["bias"] is not None:
                            tell(f(Pb[:, i % 3, 0:nk], L[:, i % 3, 0:nk], ACT.Exp, bias=nm, accum_out=den), "att_exp")
                        else:
                            ins = f(Pb[:, i % 3, 0:nk], bank(act, (st, "S", i))[:, 0:nk], ACT.Exp, bias=nm,
                                    scale=s["scale"], accum_out=den)
                            frees(ins, (st, "S", i))
                    j = i - 2
                    if 0 <= j < n:
                        nk = specs[j]["nk"]
                        b = bank(act, (st, "T", j))
                        if j >= 3:
                            act.wait_ge(bank_ready[job[(st, "O", j - 3)][0]], job[(st, "O", j - 3)][1])
                        frees(f(PT[:, j % 3, 0:nk // P, :], b[:, 0:nk].rearrange("p (a b) -> p a b", b=P), ACT.Copy),
                              (st, "T", j))

            def layer_norm(which, n, gname, bname, dst, eps=None):
                z, sq = ln_bufs(n)
                for k in range(KC):
                    act.wait_ge(sem("centred"), nth(which) + k + 1)
                    tell(f(sq[:, k, :], z[:, k, :], ACT.Square), "var_in")
                act.wait_ge(sem("var_eps"), nth(which) // KC + 1)
                tell(f(lnst[:, 2, 0:n], lnst[:, 1, 0:n], ACT.Sqrt), "ln_std")
                for k in range(KC):
                    act.wait_ge(sem("scaled"), nth(which) + k + 1)
                    tell(f(dst(k), z[:, k, :], ACT.Identity, bias=p_(bname)[:, k:k + 1], scale=p_(gname)[:, k:k + 1]),
                         "ln_out")

            act.dma_start(X1, xin.rearrange("k p t -> p k t")).then_inc(sem("x_in"), 16)
            act.dma_start(par[:, :], params).then_inc(sem("params_in"), 16)
            act.dma_start(con[:, :], consts).then_inc(sem("consts_in"), 16)
            act.dma_start(XC[:, :, S:2 * S], ctxin.rearrange("k p t -> p k t")).then_inc(sem("ctx_in"), 16)
            act.wait_ge(sem("params_in"), 16)
            tell(f(p_("cond"), p_("cond"), ACT.Silu), "cond_silu")
            dst = {"ik": F["ik"][:, 0, :], "ckv": F["ckv"][:, 0, :], "cq": F["cq"][:, 0, :], "ck": F["ck"][:, 0, :],
                   "small": dF[:, 0, 1:]}
            for m in range(2):
                for nm in ("iq", "bq", "cg", "aq", "ak"):
                    dst[f"{nm}{m}"] = F[nm][:, m, :]
                for q, nm in enumerate(("dr", "dk", "dv")):
                    dst[f"{nm}{m}"] = dF[:, 1 + 2 * q + m, 1:]
            for n, name in enumerate(IN_BLOCKS):
                b = bank(act, ("in", n))
                if name == "iw":
                    o, src = iw[:, :, :], b[:, 0:16].rearrange("p (a b) -> p a b", a=2)
                elif name[:2] in ("cv", "av"):
                    m = int(name[2])
                    o = (cv if name[0] == "c" else av)[:, :, m * P:(m + 1) * P]
                    src = b[:, 0:S].rearrange("p (a b) -> p a b", a=2)
                else:
                    o, src = dst[name], b[:, 0:S]
                frees(f(o, src, ACT.Silu if name[:2] == "cg" else ACT.Copy), ("in", n))
            act.wait_ge(sem("ckv_ms"), 1)
            tell(f(rel[:, 0, 1, :], rel[:, 0, 0, :], ACT.Sqrt), "ckv_rms")
            frees(f(vb, bank(act, "vb").rearrange("p (a b) -> p a b", a=2), ACT.Copy), "vb")
            for i in range(2):
                for q in range(4):
                    n = 4 * i + q
                    if n >= 2:
                        act.wait_ge(sem("rel_used"), n - 1)
                    else:
                        act.wait_ge(sem("ckv_normed"), 1)
                    b = bank(act, ("ix", i, q))
                    frees(f(rel[:, n % 2, :, :], b.rearrange("p (a b) -> p a b", a=2), ACT.Relu, scale=32 ** -0.5),
                          ("ix", i, q))
            act.wait_ge(sem("d_shifted"), 7)
            for r0, fn in ((R_W, ACT.Tanh), (R_A, ACT.Copy), (R_G, ACT.Sigmoid), (R_C, ACT.Copy)):
                tell(f(small_act[r0:r0 + 32, :], dS[r0:r0 + 32, 0, :], fn), "small_act")
            for name in ("dw", "da"):
                b = bank(act, name)
                for m in range(2):
                    ins = f(DZ[name[1]][:, m, :], b[:, m * S:(m + 1) * S], ACT.Sigmoid,
                            bias=p_("d_w0" if name == "dw" else "d_a0")[:, m:m + 1])
                    if m:
                        frees(ins, name)
            frees(f(DZ["g"], bank(act, "dg").rearrange("p (a b) -> p a b", a=2), ACT.Copy), "dg")
            frees(f(c_z, bank(act, "ca")[:, 0:S], ACT.Copy), "ca")
            for l in range(2):
                for g in range(ADA // 512):
                    name = ("ada", l, g // 2, g % 2)
                    b = bank(act, name)
                    n = (l * (ADA // 512) + g) // 4
                    if n:
                        act.wait_ge(sem(f"ada_row_stored{g % 4}"), 16 * n)
                    frees(f(ada_rows[0:2, g % 4, :], b[0:2, :], ACT.Copy), name)
                    evacuated(act, name)
                    tell(f(SV[0:1, 41:42], ada_rows[0:1, g % 4, 0:1], ACT.Copy), "ada_row")
            attention("att1", att1, att1_P, att1_PT, att1_L)
            if upto <= 1:
                return
            act.wait_ge(sem("c_zb"), 1)
            step(f(C["ab"], C["zb"], ACT.Abs))
            step(f(C["ab"], C["ab"], ACT.Exp, scale=-1.0))
            tell(f(C["ln"], C["ab"], ACT.Ln, bias=1.0), "c_softplus")
            act.wait_ge(sem("c_cum"), 1)
            f(C["ec"], C["cum"], ACT.Exp)
            f(C["en"], C["cum"], ACT.Exp, scale=-1.0)
            for c in range(NCH):
                ins = f(C["ed"][:, c * CH:(c + 1) * CH], C["cum"][:, c * CH:(c + 1) * CH], ACT.Exp, scale=-1.0,
                        bias=C["cum"][:, c * CH + CH - 1:c * CH + CH])
            tell(ins, "c_exps")
            frees(f(c_kdt, bank(act, "ckd")[:, 0:S].rearrange("p (a b) -> p a b", a=2), ACT.Copy), "ckd")
            for hp in range(2):
                for q in range(2):
                    o = c_o[:, hp, :].rearrange("p (n q t) -> p n q t", n=2, q=2)[:, :, q, :]
                    frees(f(o, bank(act, ("co", hp, q))[:, 0:P].rearrange("p (a b) -> p a b", a=2), ACT.Copy),
                          ("co", hp, q))
            for hp in range(2):
                for q in range(2):
                    evacuated(act, ("co", hp, q))
            tell(f(c_sq, c_o, ACT.Square), "c_sq")
            act.wait_ge(sem("c_ms"), 1)
            tell(f(c_sq, c_sq, ACT.Sqrt), "c_rms")
            if upto <= 2:
                return
            act.wait_ge(sem("d_kk"), 1)
            tell(f(DD["t"], DD["kk"], ACT.Square), "d_kk_sq")
            tell(f(DD["e1"], bank(act, "kkn").rearrange("p (a b) -> p a b", a=2), ACT.Sqrt), "d_kk_norm")
            frees(f(DD["e2"][:, 0, 0:1], DD["cum"][:, 0, 0:1], ACT.Copy), "kkn") if False else None
            act.wait_ge(sem("d_cum"), 1)
            act.wait_ge(sem("d_kk_unit"), 1)
            f(DD["e1"], DD["cm1"], ACT.Exp)
            f(DD["e2"], DD["cum"], ACT.Exp)
            tell(f(DD["e3"], DD["cum"], ACT.Exp, scale=-1.0), "d_exps")
            for fam in ("Vt", "Bt", "Kt"):
                for p in range(2):
                    r = slice(64 * p, 64 * p + 64)
                    frees(f(U[fam][r, :, :], bank(act, (fam, p))[r, :].rearrange("p (a b) -> p a b", a=8), ACT.Copy),
                          (fam, p))
            for fam in FAM2:
                if fam[0] in "ZW" or fam in ("Y1", "T"):
                    continue
                p = 1
                r = slice(64, P)
                frees(f(U[fam][r, :, :], bank(act, (fam, p))[r, :].rearrange("p (a b) -> p a b", a=8), ACT.Copy),
                      (fam, p))
            for c in range(NCH):
                for what, n in (("X", 0), ("U", 1)):
                    r = slice(64, P)
                    frees(f(x_u[r, n, :, :], bank(act, (what, c, 1))[r, 0:P].rearrange("p (a b) -> p a b", a=2),
                            ACT.Copy), (what, c, 1))
            act.wait_ge(sem("d_centred"), 1)
            tell(f(DD["t"], yT, ACT.Square), "d_ysq")
            act.wait_ge(sem("d_var"), 1)
            tell(f(DD["e1"], DD["e1"], ACT.Sqrt), "d_std")
            if upto <= 3:
                return
            for m in range(KC):
                if m >= 2:
                    act.wait_ge(sem("gates_used"), m - 1)
                for half in range(2):
                    frees(f(gates[:, m % 2, 2 * half:2 * half + 2, :],
                            bank(act, ("gt", m, half)).rearrange("p (a b) -> p a b", a=2), ACT.Sigmoid), ("gt", m, half))
            layer_norm("a", S, "ln1g", "ln1b", lambda k: X1[:, k, :])
            feed("moe", 0)
            for k in range(KC):
                act.wait_ge(sem("ln_out"), k + 1)
                tell(f(mx_hi[:, k, :], X1[:, k, :], ACT.Copy), "x_high")
            for t in range(2):
                act.wait_ge(sem("rt_neg"), t + 1)
                tell(f(rt[:, t, 0, 0:4], lg[:, t, 0:4], ACT.Exp, bias=SV[:, 16 + t:17 + t],
                       accum_out=SV[:, 20 + t:21 + t]), "rt_gexp")
                act.wait_ge(sem("rt_diff"), t + 1)
                tell(f(SV[:, 32 + t:33 + t], SV[:, 28 + t:29 + t], ACT.Exp), "rt_eexp")
            frees(f(gateT[0:EXPERTS, :], bank(act, "gateT")[0:EXPERTS, 0:S], ACT.Copy), "gateT")
            evacuated(act, "gateT")
            tell(f(SV[0:1, 40:41], gateT[0:1, 0:1], ACT.Copy), "gateT_ready")
            if upto <= 4:
                return

            def highs(c, n, r=None):
                for i in range(c, c + n):
                    need = 16 * ((moe0 + i) // RING + 1)
                    act.wait_ge(w_ready[(moe0 + i) % RING], need if r is None else r * (16 * 12 // RING) + need)
                    if i >= SPLIT_RING:
                        act.wait_ge(w_used, i - SPLIT_RING + 1 if r is None else r * 12 + (i - SPLIT_RING + 1))
                    f(w_hi[:, i % SPLIT_RING, :], ring[:, (moe0 + i) % RING, :], ACT.Copy).then_inc(w_high, 1)

            def silu(par_, n):
                act.wait_ge(sem("moe_gate"), n + 1)
                f(m_sg[:, par_, :, :], ps[2 * par_].rearrange("p (a b) -> p a b", a=2), ACT.Silu)\
                    .then_inc(sem("moe_silu"), 1)

            def hidden_high(par_, n):
                act.wait_ge(sem("moe_raw"), n + 1)
                if not isinstance(n, int) or n >= 2:
                    act.wait_ge(sem("moe_down"), n - 1)
                f(mh_hi[:, par_, :, :], m_t[:, par_, :, :], ACT.Copy).then_inc(sem("moe_high"), 1)

            def expert(par_, n, c, r=None, last=False):
                hidden_high(1 - par_, n - 1)
                highs(c + 2, 2, r)
                silu(par_, n)
                highs(c + 4, 2 if last else 4, r)

            highs(3, 1)
            silu(0, 0)
            highs(4, 2)
            for e in (1, 2):
                expert(e % 2, e, 6 * e - 2)
            with act.Fori(0, (EXPERTS - 4) // 2) as r:
                for s in range(2):
                    expert((1 + s) % 2, r * 2 + (3 + s), 16 + 6 * s, r)
            e = EXPERTS - 1
            expert(1, e, 6 * e - 2, last=True)
            hidden_high(1, e)
            highs(6 * EXPERTS - 2, 2)
            fed[0] = 6 * EXPERTS
            layer_norm("b", S, "ln2g", "ln2b", lambda k: X1[:, k, :])
            if upto <= 5:
                return
            for n in range(18):
                b = bank(act, ("l0in", n))
                if n == 5:
                    o = V0[:, :, 0:P]
                elif n >= 14:
                    o = V0[:, :, P + (n - 14) * P:P + (n - 13) * P]
                elif n < 5:
                    o = Q0[:, n, :]
                elif n < 10:
                    o = qb[:, n - 6, :]
                else:
                    o = kb[:, n - 10, :]
                src = b.rearrange("p (a b) -> p a b", a=4) if n == 5 or n >= 14 else b[:, :]
                frees(f(o, src, ACT.Copy), ("l0in", n))
            for m in range(5):
                evacuated(act, ("l0in", m))
                tell(f(tq2[:, m, :], Q0[:, m, :], ACT.Square), "q0_sq")
            for m in range(5):
                act.wait_ge(sem("q0_ms"), m + 1)
                tell(f(tq[:, m, :], tq[:, m, :], ACT.Sqrt), "q0_rms")
            attention("att2", att2, att2_P, att2_PT, att2_L)

            def gated(name, l, n, stage=None):
                for m in range(KC):
                    if stage is not None:
                        feed(stage, (m * HF + HF - 1) // BLOCKS)
                    b = bank(act, name(m))
                    z_n = gated_n[0]
                    gated_n[0] += 1
                    if m >= 2 or stage is not None and stage[-1] == "B":
                        act.wait_ge(sem("z_written"), z_n - 1)
                    g = 16 if stage is None else 40
                    ts = lnst[:, m % 2, 0:n]
                    ins = f(ts[:, 0:S], b[:, 0:S], ACT.Copy, scale=MOD[:, l, g + m, 0:1])
                    if n > S:
                        ins = f(ts[:, S:n], b[:, S:n], ACT.Copy, scale=MOD[:, l, g + m, 1:2])
                    frees(ins, name(m))

            gated_n = [KC]

            gated(lambda m: ("l0out", m), 0, 512)
            feed("l0upA", 0)
            layer_norm("c", 512, "l0ln1g", "l0ln1b", lambda k: XC[:, k, :])

            def ffn(l, n):
                ns = n // S
                z, _ = ln_bufs(n)
                for k in range(KC):
                    act.wait_ge(sem("h_raw"), KC * l + k + 1)
                    tell(f(in_split(n)[0][:, k, :], z[:, k, :], ACT.Copy), "h_high")

                def hidden_high(j):
                    act.wait_ge(sem("ff_raw"), l * FF + j + 1)
                    tell(f(u_hi[:, j % HF, 0:n], u_raw[:, j % 2, 0:n], ACT.Copy), "ff_high")

                done = 0
                for half, part in enumerate("AB"):
                    chunks = range(UP_A) if half == 0 else range(UP_A, FF)
                    for j in chunks:
                        feed(f"l{l}up{part}", 2 * (j - chunks[0]))
                        b = bank(act, (f"l{l}g", j))
                        if j >= 2:
                            act.wait_ge(sem("conv_done"), l * FF + j - 1)
                        else:
                            act.wait_ge(sem("pad_zero"), l + 1)
                        frees(f(gp[:, j % 2, 0:ns, 1:S + 1], b[:, 0:n].rearrange("p (a b) -> p a b", a=ns), ACT.Copy),
                              (f"l{l}g", j))
                        while done <= j - 2:
                            hidden_high(done)
                            done += 1
                        act.wait_ge(sem("conv_done"), l * FF + j + 1)
                        if j >= 2:
                            act.wait_ge(sem("ff_raw"), l * FF + j - 1)
                        tell(f(sg_[:, j % 2, 0:n], cg_[:, j % 2, 0:n], ACT.Silu), "ff_silu")
                    while done < (half + 1) * HF:
                        hidden_high(done)
                        done += 1
                    gated(lambda m: (f"l{l}down", half, m), l, n, f"l{l}down{part}")

            ffn(0, 512)
            layer_norm("d", 512, "l0ln2g", "l0ln2b", lambda k: XC[:, k, :])
            if upto <= 6:
                return
            for n in range(9):
                b = bank(act, ("l1in", n))
                if n < 2:
                    o, src = ckv1[:, n, :], b[:, :]
                elif n == 2:
                    o, src = kr1[64:96, :], b[64:96, :]
                else:
                    o, src = cq1[:, n - 3, :], b[:, 0:S]
                frees(f(o, src, ACT.Copy), ("l1in", n))
            for n in range(9):
                evacuated(act, ("l1in", n))
            f(sq1[:, 0:6, 0:S], cq1, ACT.Square)
            tell(f(sq1[:, 6:8, :], ckv1, ACT.Square), "cq_sq")
            act.wait_ge(sem("cq_ms"), 2)
            f(lnst[:, 0, 0:S], lnst[:, 0, 0:S], ACT.Sqrt)
            tell(f(lnst[:, 1, :], lnst[:, 1, :], ACT.Sqrt), "cq_rms")
            for m in range(8):
                frees(f(q1[0:96, 2 * m:2 * m + 2, :], bank(act, ("uq", m))[0:96, :].rearrange("p (a b) -> p a b", a=2),
                        ACT.Copy), ("uq", m))
            for hf in range(2):
                for t in range(4):
                    frees(f(V1[:, t, hf * 512:(hf + 1) * 512], bank(act, ("v1", t, hf))[:, :], ACT.Copy), ("v1", t, hf))
            attention("att3", att3, att2_P, att2_PT, None)
            gated(lambda m: ("l1out", m), 1, S)
            feed("l1upA", 0)
            layer_norm("e", S, "l1ln1g", "l1ln1b", lambda k: X1[:, k, :])
            ffn(1, S)
            layer_norm("f", S, "l1ln2g", "l1ln2b", lambda k: X1[:, k, :])

        @block.vector
        def _(dve):
            seq = [0]
            chain = sem("dve_seq")
            counts = {}
            V = nc.vector
            fed = [0]

            def low(i, t, r_need):
                dve.wait_ge(w_high, r_need)
                V.tensor_tensor(w_lo[:, i % SPLIT_RING, :], ring[:, t % RING, :],
                                w_hi[:, i % SPLIT_RING, :].bitcast(F32), ALU.subtract).then_inc(w_split, 1)

            def feed(stage, n):
                t = first[stage] + n
                upto_ = split_at[min(t + SPLIT_RING, run_end(t + 1)) - 1] + 1
                for i in range(fed[0], upto_):
                    low(i, split_order[i], i + 1)
                fed[0] = max(fed[0], upto_)

            def rest(o, x, high):
                return V.tensor_tensor(o, x, high.bitcast(F32), ALU.subtract)

            def step(ins, name=None):
                if name is None:
                    seq[0] += 1
                    ins.then_inc(chain, 1)
                    dve.wait_ge(chain, seq[0])
                else:
                    counts[name] = counts.get(name, 0) + 1
                    ins.then_inc(sem(name), 1)
                    dve.wait_ge(sem(name), counts[name])

            def tell(ins, name):
                counts[name] = counts.get(name, 0) + 1
                ins.then_inc(sem(name), 1)

            def attention(st, specs, Pb, L):
                n = len(specs)
                for i in range(n + 4):
                    if st == "att3" and i % 2 == 0 and i < n:
                        h = i // 2
                        b = bank(dve, ("kT", h))
                        if h >= 2:
                            dve.wait_ge(bank_ready[job[(st, "S", i - 3)][0]], job[(st, "S", i - 3)][1])
                        frees(V.tensor_copy(kT1[0:64, h % 2, :], b[0:64, :]), ("kT", h))
                    if i < n:
                        s = specs[i]
                        nk = s["nk"]
                        b = bank(dve, (st, "S", i))
                        nm = SV[:, i % 4:i % 4 + 1]
                        if s["bias"] is not None:
                            if i >= 3 and counts_exp(specs, i - 3):
                                dve.wait_ge(sem("att_exp"), exp_before[st] + counts_exp(specs, i - 3))
                            nb = s["bias"].shape[1]
                            ins = V.scalar_tensor_tensor(L[:, i % 3, 0:nb], b[:, 0:nb], s["scale"], s["bias"],
                                                         ALU.mult, ALU.add)
                            if nk > nb:
                                ins = V.tensor_scalar(L[:, i % 3, nb:nk], b[:, nb:nk], s["scale"], None, ALU.mult)
                            frees(ins, (st, "S", i))
                            evacuated(dve, (st, "S", i))
                            step(V.tensor_reduce(nm, L[:, i % 3, 0:nk], AX.X, ALU.max, negate=True), "att_negmax")
                        else:
                            raw = SV[:, 4 + i % 4:5 + i % 4]
                            step(V.tensor_reduce(raw, b[:, 0:nk], AX.X, ALU.max))
                            step(V.tensor_scalar(nm, raw, -s["scale"], None, ALU.mult), "att_negmax")
                    j = i - 1
                    if 0 <= j < n:
                        s = specs[j]
                        if s["bias"] is not None:
                            dve.wait_ge(sem("att_exp"), exp_before[st] + counts_exp(specs, j))
                        else:
                            evacuated(dve, (st, "S", j))
                        rd = SV[:, 12 + j % 4:13 + j % 4]
                        step(V.reciprocal(rd, SV[:, 8 + j % 4:9 + j % 4]))
                        step(V.tensor_scalar(Pb[:, j % 3, 0:s["nk"]], Pb[:, j % 3, 0:s["nk"]], rd, None, ALU.mult),
                             "att_probs")
                    j = i - 4
                    if 0 <= j < n:
                        o = specs[j]["o"]
                        r0 = 64 * (o.start_partition() // 64)
                        frees(V.tensor_copy(o, bank(dve, (st, "O", j))[r0:r0 + 64, 0:P]), (st, "O", j))

            def counts_exp(specs, i):
                return sum(s["bias"] is not None for s in specs[:i + 1])

            def layer_norm(which, n, eps):
                z, sq = ln_bufs(n)
                b = bank(dve, ("mean", which))
                frees(V.tensor_scalar(lnst[:, 0, 0:n], b[:, 0:n], -1.0 / D, None, ALU.mult), ("mean", which))
                evacuated(dve, ("mean", which))
                for k in range(KC):
                    tell(V.tensor_tensor(z[:, k, :], z[:, k, :], lnst[:, 0, 0:n], ALU.add), "centred")
                b = bank(dve, ("var", which))
                ins = V.tensor_scalar(lnst[:, 1, 0:n], b[:, 0:n], 1.0 / D, eps, ALU.mult, ALU.add)
                frees(ins, ("var", which))
                evacuated(dve, ("var", which))
                step(V.tensor_copy(SV[0:1, 44:45], lnst[0:1, 1, 0:1]), "var_eps")
                dve.wait_ge(sem("ln_std"), nth(which) // KC + 1)
                step(V.reciprocal(lnst[:, 2, 0:n], lnst[:, 2, 0:n]))
                dve.wait_ge(sem("centred"), nth(which) + KC)
                for k in range(KC):
                    tell(V.tensor_tensor(z[:, k, :], z[:, k, :], lnst[:, 2, 0:n], ALU.mult), "scaled")

            step(V.memset(dF[:, :, 0:1], 0.0), "d_pad")
            frees(V.tensor_copy(rows8[0:8, :], bank(dve, "t5")[0:8, :]), "t5")
            evacuated(dve, "t5")
            step(V.tensor_copy(SV[0:1, 45:46], rows8[0:1, 0:1]), "t5_row_ready")
            evacuated(dve, ("in", 4))
            tell(V.tensor_tensor(rel[:, 0, 0, :], F["ckv"][:, 0, :], F["ckv"][:, 0, :], ALU.mult), "ckv_sq")
            b = bank(dve, "ckvms")
            ins = V.tensor_scalar(rel[:, 0, 0, :], b[:, 0:S], 1.0 / 64, 1e-6, ALU.mult, ALU.add)
            frees(ins, "ckvms")
            evacuated(dve, "ckvms")
            step(V.tensor_copy(SV[0:1, 46:47], rel[0:1, 0, 0, 0:1]), "ckv_ms")
            dve.wait_ge(sem("ckv_rms"), 1)
            step(V.reciprocal(rel[:, 0, 1, :], rel[:, 0, 1, :]))
            step(V.scalar_tensor_tensor(F["ckv"][:, 0, :], F["ckv"][:, 0, :], p_("kv_gain"), rel[:, 0, 1, :],
                                        ALU.mult, ALU.mult), "ckv_normed")
            for n in range(7, 14):
                evacuated(dve, ("in", n))
            step(V.tensor_tensor(dS, dF[:, :, 0:S], dF[:, :, 1:S + 1], ALU.subtract))
            for n in range(7):
                step(V.scalar_tensor_tensor(dS[:, n, :], dS[:, n, :], p_("d_mu")[:, n:n + 1], dF[:, n, 1:S + 1],
                                            ALU.mult, ALU.add), "d_shifted")
            evacuated(dve, ("in", 3))
            for i in range(2):
                for q in range(4):
                    n = 4 * i + q
                    evacuated(dve, ("ix", i, q))
                    for m in range(2):
                        h = 4 * m + q
                        if n % 4 == 0 and m == 0:
                            ins = V.tensor_scalar(score[:, i, :], rel[:, n % 2, m, :], iw[:, i, h:h + 1], None, ALU.mult)
                        else:
                            ins = V.scalar_tensor_tensor(score[:, i, :], rel[:, n % 2, m, :], iw[:, i, h:h + 1],
                                                         score[:, i, :], ALU.mult, ALU.add)
                        if m:
                            step(ins, "rel_used")
                        else:
                            step(ins)
                step(V.scalar_tensor_tensor(work[:, i, 0, :], score[:, i, :], 8 ** -0.5,
                                            c_("causal")[:, i * S:(i + 1) * S], ALU.mult, ALU.add))
                for k in range(KEEP // 8):
                    step(V.max(top8[:, i, :], work[:, i, k % 2, :]))
                    step(V.match_replace(work[:, i, (k + 1) % 2, :], top8[:, i, :], work[:, i, k % 2, :], TAKEN))
                step(V.tensor_scalar(selm[:, i, :], work[:, i, 0, :], -2e38, NEG, ALU.is_gt, ALU.mult))
            dve.wait_ge(sem("bias1"), 32)
            for i in range(2):
                step(V.tensor_tensor(bias1[:, 4:8, i, :], bias1[:, 4:8, i, :], bc(selm[:, i, :], 4), ALU.add))
            attention("att1", att1, att1_P, att1_L)
            if upto <= 1:
                return
            evacuated(dve, "ca")
            step(V.tensor_scalar(C["zb"], c_z, p_("c_a_bias"), None, ALU.add), "c_zb")
            dve.wait_ge(sem("c_softplus"), 1)
            step(V.scalar_tensor_tensor(C["la"], C["zb"], 0.0, C["ln"], ALU.min, ALU.subtract))
            step(V.tensor_scalar(C["la"], C["la"], 1.0 / 16, None, ALU.mult))
            for c in range(NCH):
                cs = slice(c * CH, (c + 1) * CH)
                ins = V.tensor_tensor_scan(C["cum"][:, cs], c_("scan_ones"), C["la"][:, cs], 0.0, ALU.mult, ALU.add)
            step(ins, "c_cum")
            dve.wait_ge(sem("c_exps"), 1)
            V.scalar_tensor_tensor(C["qd"], F["cq"][:, 0, :], 32 ** -0.5, C["ec"], ALU.mult, ALU.mult)
            V.tensor_tensor(C["ki"], F["ck"][:, 0, :], C["en"], ALU.mult)
            step(V.tensor_tensor(C["kd"], F["ck"][:, 0, :], C["ed"], ALU.mult), "c_feat")
            for h in range(4):
                b = bank(dve, ("catt", h))
                frees(V.tensor_tensor(c_att[:, h, :, :], b[:, 0:P].rearrange("p (a b) -> p a b", a=2),
                                      bc(c_("upper_incl"), 2), ALU.mult), ("catt", h))
            for c in range(3):
                b = bank(dve, ("cupd", c))
                if c == 0:
                    ins = V.tensor_copy(c_state[:, 0, :], b[:, 0:S])
                else:
                    dec = C["ec"][:, c * CH + CH - 1:c * CH + CH]
                    ins = V.scalar_tensor_tensor(c_state[:, c, :], c_state[:, c - 1, :], dec, b[:, 0:S], ALU.mult,
                                                 ALU.add)
                frees(ins, ("cupd", c))
                evacuated(dve, ("cupd", c))
                step(V.tensor_tensor(c_sm[:, c, :], c_state[:, c, :], c_("heads_c"), ALU.mult), "c_states")
            b = bank(dve, "coms")
            ins = V.tensor_scalar(c_sq, b.rearrange("p (a b) -> p a b", a=2), 1.0 / 64, 1e-6, ALU.mult, ALU.add)
            frees(ins, "coms")
            evacuated(dve, "coms")
            step(V.tensor_copy(SV[0:1, 47:48], c_sq[0:1, 0, 0:1]), "c_ms")
            dve.wait_ge(sem("c_rms"), 1)
            step(V.reciprocal(c_sq, c_sq))
            step(V.tensor_tensor(c_o, c_o, c_sq, ALU.mult))
            for m in range(2):
                ins = V.scalar_tensor_tensor(ysT[:, 2, m, :], c_o[:, m, :], p_("c_norm_gain")[:, m:m + 1],
                                             F["cg"][:, m, :], ALU.mult, ALU.mult)
            step(ins, "ys_ready")
            if upto <= 2:
                return
            r_, k_, v_ = dS[:, 1:3, :], dS[:, 3:5, :], dS[:, 5:7, :]
            evacuated(dve, "dw")
            evacuated(dve, "da")
            evacuated(dve, "dg")
            for m in range(2):
                ins = V.tensor_scalar(DD["kk"][:, m, :], k_[:, m, :], p_("d_k_k")[:, m:m + 1], None, ALU.mult)
            step(ins, "d_kk")
            step(V.tensor_scalar(DD["lw"], DZ["w"], -W_DECAY, None, ALU.mult))
            for m in range(2):
                for c in range(NCH):
                    cs = slice(c * CH, (c + 1) * CH)
                    ins = V.tensor_tensor_scan(DD["cum"][:, m, cs], c_("scan_ones"), DD["lw"][:, m, cs], 0.0,
                                               ALU.mult, ALU.add)
            step(ins)
            step(V.tensor_tensor(DD["cm1"], DD["cum"], DD["lw"], ALU.subtract), "d_cum")
            for m in range(2):
                step(V.tensor_scalar(DD["kp"][:, m, :], DZ["a"][:, m, :], 1.0, p_("d_k_a")[:, m:m + 1], ALU.subtract,
                                     ALU.mult))
            step(V.scalar_tensor_tensor(DD["kp"], DD["kp"], 1.0, k_, ALU.add, ALU.mult))
            dve.wait_ge(sem("d_kk_norm"), 1)
            step(V.tensor_scalar(DD["e1"], DD["e1"], 1e-12, None, ALU.max))
            step(V.reciprocal(DD["e1"], DD["e1"]))
            frees(V.tensor_tensor(DD["kk"], DD["kk"], DD["e1"], ALU.mult), "kkn")
            evacuated(dve, "kkn")
            step(V.tensor_tensor(DD["b"], DD["kk"], DZ["a"], ALU.mult), "d_kk_unit")
            dve.wait_ge(sem("d_exps"), 1)
            V.scalar_tensor_tensor(Ah, DD["kk"], -1.0, DD["e1"], ALU.mult, ALU.mult)
            V.tensor_tensor(Rh, r_, DD["e2"], ALU.mult)
            V.tensor_tensor(DD["Bh"], DD["b"], DD["e3"], ALU.mult)
            step(V.tensor_tensor(DD["Kh"], DD["kp"], DD["e3"], ALU.mult), "d_feat")
            step(V.tensor_tensor(bn, r_, DD["kp"], ALU.mult))
            for m in range(2):
                step(V.tensor_scalar(bn[:, m, :], bn[:, m, :], p_("d_r_k")[:, m:m + 1], None, ALU.mult))
            step(V.tensor_copy(SV[0:1, 48:49], bn[0:1, 0, 0:1]), "d_bonus_in")
            masks = {"N": "upper", "A": "lower", "GRB": "upper_incl", "GAK": "upper", "GRK": "upper_incl"}
            for fam, mask in masks.items():
                for p in range(2):
                    r = slice(64 * p, 64 * p + 64)
                    frees(V.tensor_tensor(U[fam][r, :, :], bank(dve, (fam, p))[r, :].rearrange("p (a b) -> p a b", a=8),
                                          bc(c_(mask)[r, :], 8), ALU.mult), (fam, p))
            for fam in ("N", "A"):
                for p in range(2):
                    evacuated(dve, (fam, p))
            dve.wait_ge(sem("ada_mat1"), 16)
            step(V.tensor_tensor(U["D"], U["N"], bc(c_("diag16"), 8), ALU.mult), "d_split")
            step(V.tensor_tensor(U["Dt"], U["A"], bc(c_("diag16"), 8), ALU.mult), "d_split")
            step(V.tensor_tensor(U["Lo"], U["N"], U["D"], ALU.subtract), "d_split")
            step(V.tensor_tensor(U["Z"], U["D"], bc(c_("eye64"), 8), ALU.add), "d_split")
            step(V.tensor_tensor(U["W"], U["Dt"], bc(c_("eye64"), 8), ALU.add), "d_split")
            for fam in FAM2:
                add_to = "Z" if fam[0] == "Z" else "W" if fam[0] == "W" else {"Y1": "Z", "T": "Y1"}.get(fam)
                for p in range(2):
                    r = slice(64 * p, 64 * p + 64)
                    if add_to is None and p == 1:
                        continue
                    b = bank(dve, (fam, p))[r, :].rearrange("p (a b) -> p a b", a=8)
                    if add_to is None:
                        ins = V.tensor_copy(U[fam][r, :, :], b)
                    else:
                        dst = U[add_to] if fam[0] in "ZW" else U[fam]
                        ins = V.tensor_tensor(dst[r, :, :], U[add_to][r, :, :], b, ALU.add)
                    frees(ins, (fam, p))
                    evacuated(dve, (fam, p))
            for c in range(NCH):
                r = slice(0, 64)
                for what, n in (("X", 0), ("U", 1)):
                    frees(V.tensor_copy(x_u[r, n, :, :], bank(dve, (what, c, 0))[r, 0:P].rearrange("p (a b) -> p a b", a=2)),
                          (what, c, 0))
                for p in range(2):
                    r = slice(64 * p, 64 * p + 64)
                    frees(V.tensor_copy(yT[r, :, c * CH:(c + 1) * CH],
                                        bank(dve, ("Yc", c, p))[r, 0:P].rearrange("p (a b) -> p a b", a=2)), ("Yc", c, p))
                if c < NCH - 1:
                    for p in range(2):
                        r = slice(64 * p, 64 * p + 64)
                        b = bank(dve, ("M", c, p))[r, 0:P].rearrange("p (a b) -> p a b", a=2)
                        if c == 0:
                            ins = V.tensor_copy(m_st[r, 4, :, :], b)
                        else:
                            ins = V.tensor_tensor(m_st[r, 4, :, :], m_st[r, c, :, :], b, ALU.add)
                        frees(ins, ("M", c, p))
                        evacuated(dve, ("M", c, p))
                        for m in range(2):
                            ins = V.tensor_scalar(m_st[r, c + 1, m, :], m_st[r, 4, m, :],
                                                  DD["e2"][r, m, c * CH + CH - 1:c * CH + CH], None, ALU.mult)
                        step(ins, "d_state")
            for p in range(2):
                for c in range(NCH):
                    evacuated(dve, ("Yc", c, p))
            step(V.tensor_copy(SV[0:1, 49:50], yT[0:1, 0, 0:1]), "d_y")
            flat2 = "p (a b) -> p a b"
            frees(V.tensor_tensor(bn, bank(dve, "bonus").rearrange(flat2, a=2), v_, ALU.mult), "bonus")
            b = bank(dve, "ymean").rearrange(flat2, a=2)
            frees(V.scalar_tensor_tensor(yT, b, -1.0 / 64, yT, ALU.mult, ALU.add), "ymean")
            evacuated(dve, "ymean")
            step(V.tensor_copy(SV[0:1, 50:51], yT[0:1, 0, 0:1]), "d_centred")
            b = bank(dve, "yvar").rearrange(flat2, a=2)
            frees(V.tensor_scalar(DD["e1"], b, 1.0 / 64, 64e-5, ALU.mult, ALU.add), "yvar")
            evacuated(dve, "yvar")
            step(V.tensor_copy(SV[0:1, 51:52], DD["e1"][0:1, 0, 0:1]), "d_var")
            dve.wait_ge(sem("d_std"), 1)
            step(V.reciprocal(DD["e1"], DD["e1"]))
            step(V.tensor_tensor(yT, yT, DD["e1"], ALU.mult))
            for m in range(2):
                step(V.tensor_scalar(yT[:, m, :], yT[:, m, :], p_("d_gn_w")[:, m:m + 1], p_("d_gn_b")[:, m:m + 1],
                                     ALU.mult, ALU.add))
            evacuated(dve, "bonus")
            step(V.tensor_tensor(yT, yT, bn, ALU.add))
            step(V.tensor_tensor(ysT[:, 3, :, :], yT, DZ["g"], ALU.mult), "ys_ready")
            for i in (12, 13, 14, 15, 8, 9, 10, 11, 0, 1, 2, 3, 4, 5, 6, 7):
                evacuated(dve, ("att1", "O", i))
            step(V.tensor_copy(SV[0:1, 52:53], ysT[0:1, 0, 0, 0:1]), "ys_ready")
            step(V.tensor_copy(SV[0:1, 53:54], ysT[0:1, 1, 0, 0:1]), "ys_ready")
            if upto <= 3:
                return
            for l in range(2):
                b = bank(dve, ("adaT", l))
                o, n = PARAM[f"bada{l}"]
                ins = V.tensor_tensor(MOD[:, l, :, :], b[:, 0:96].rearrange("p (s m) -> p m s", s=2),
                                      par[:, o:o + n].unsqueeze(2).broadcast_to([P, 48, 2]), ALU.add)
                frees(ins, ("adaT", l))
                evacuated(dve, ("adaT", l))
                for q, g in enumerate((8, 32)):
                    step(V.tensor_scalar(SC1[:, l, q, :, :], MOD[:, l, g:g + 8, :], 1.0, None, ALU.add), "mods")
            z, _ = ln_bufs(S)
            for m in range(KC):
                for half in range(2):
                    evacuated(dve, ("gt", m, half))
                    b = bank(dve, ("br", m, half)).rearrange(flat2, a=2)
                    frees(V.tensor_tensor(tmpm[:, m % 2, half, :, :], b, gates[:, m % 2, 2 * half:2 * half + 2, :],
                                          ALU.mult), ("br", m, half))
                for half in range(2):
                    evacuated(dve, ("br", m, half))
                step(V.tensor_tensor(tmpm[:, m % 2, 0, :, :], tmpm[:, m % 2, 0, :, :], tmpm[:, m % 2, 1, :, :], ALU.add),
                     "gates_used")
                step(V.tensor_tensor(mergedT[:, m, :], tmpm[:, m % 2, 0, 0, :], tmpm[:, m % 2, 0, 1, :], ALU.add),
                     "merged")
            for m in range(KC):
                b = bank(dve, ("out1", m))
                frees(V.scalar_tensor_tensor(z[:, m, :], X1[:, m, :], ALPHA1, b[:, 0:S], ALU.mult, ALU.add),
                      ("out1", m))
                evacuated(dve, ("out1", m))
                step(V.tensor_copy(SV[0:1, 54:55], z[0:1, m, 0:1]), "mean_in")
            layer_norm("a", S, 1e-5)

            def first_max(t, vals, m, eq, incl, oh, w):
                step(V.tensor_scalar(eq, vals, m, None, ALU.is_equal))
                step(V.tensor_tensor_scan(incl, c_("scan_ones")[:, 0:w], eq, 0.0, ALU.mult, ALU.max))
                step(V.tensor_copy(oh[:, 0:1], incl[:, 0:1]))
                step(V.tensor_tensor(oh[:, 1:w], incl[:, 1:w], incl[:, 0:w - 1], ALU.subtract))

            for t in range(2):
                def sv(n):
                    return SV[:, n + t:n + t + 1]

                b = bank(dve, ("rt", t))
                frees(V.tensor_tensor(lg[:, t, :], b[:, 0:36], p_("router_bias"), ALU.add), ("rt", t))
                evacuated(dve, ("rt", t))
                step(V.tensor_reduce(sv(18), lg[:, t, 0:4], AX.X, ALU.max))
                step(V.tensor_scalar(sv(16), sv(18), -1.0, None, ALU.mult), "rt_neg")
                R = [rt[:, t, n, :] for n in range(12)]
                first_max(t, lg[:, t, 0:4], sv(18), R[1][:, 0:4], R[2][:, 0:4], R[3][:, 0:4], 4)
                ohg = R[3][:, 0:4].unsqueeze(2).broadcast_to([P, 4, 8])
                step(V.tensor_scalar(R[4][:, 0:4], R[3][:, 0:4], 1.0, -NEG, ALU.subtract, ALU.mult))
                step(V.tensor_tensor(R[5].rearrange("p (a b) -> p a b", a=4),
                                     lg[:, t, 4:36].rearrange("p (a b) -> p a b", a=4), ohg, ALU.mult))
                step(V.tensor_tensor(R[5].rearrange("p (a b) -> p a b", a=4), R[5].rearrange("p (a b) -> p a b", a=4),
                                     R[4][:, 0:4].unsqueeze(2).broadcast_to([P, 4, 8]), ALU.add))
                step(V.tensor_reduce(sv(22), R[5], AX.X, ALU.max))
                first_max(t, R[5], sv(22), R[6], R[7], R[8], 32)
                step(V.scalar_tensor_tensor(R[5], R[8], 4 * NEG, R[5], ALU.mult, ALU.add))
                step(V.tensor_reduce(sv(24), R[5], AX.X, ALU.max))
                first_max(t, R[5], sv(24), R[6], R[7], R[9], 32)
                step(V.tensor_tensor(sv(28), sv(24), sv(22), ALU.subtract), "rt_diff")
                dve.wait_ge(sem("rt_gexp"), t + 1)
                dve.wait_ge(sem("rt_eexp"), t + 1)
                step(V.tensor_scalar(sv(34), sv(32), 1.0, sv(20), ALU.add, ALU.mult))
                step(V.reciprocal(sv(36), sv(34)))
                step(V.scalar_tensor_tensor(R[10], R[9], sv(32), R[8], ALU.mult, ALU.add))
                step(V.tensor_scalar(R[11], R[10], sv(36), None, ALU.mult), "gate_ready")
            feed("moe", 0)
            for k in range(KC):
                dve.wait_ge(sem("x_high"), k + 1)
                tell(rest(mx_lo[:, k, :], X1[:, k, :], mx_hi[:, k, :]), "x_split")
            if upto <= 4:
                return
            dve.wait_ge(sem("gate_bc"), 16)

            def lows(c, n, r=None):
                for i in range(c, c + n):
                    low(i, moe0 + i, i + 1 if r is None else r * 12 + (i + 1))

            def gated_hidden(par_, n):
                dve.wait_ge(sem("moe_silu"), n + 1)
                V.tensor_tensor(m_t[:, par_, :, :], m_sg[:, par_, :, :], gate_of(n), ALU.mult)\
                    .then_inc(sem("moe_gated"), 1)

            def raw_hidden(par_, n):
                dve.wait_ge(sem("moe_gated"), n + 1)
                dve.wait_ge(sem("moe_up"), n + 1)
                V.tensor_tensor(m_t[:, par_, :, :], m_t[:, par_, :, :],
                                ps[2 * par_ + 1].rearrange("p (a b) -> p a b", a=2), ALU.mult)\
                    .then_inc(sem("moe_raw"), 1)

            def hidden_low(par_, n):
                dve.wait_ge(sem("moe_high"), n + 1)
                rest(mh_lo[:, par_, :, :], m_t[:, par_, :, :], mh_hi[:, par_, :, :]).then_inc(sem("moe_hidden"), 1)

            def gate_of(e):
                rows = gate_bc[:, e:e + 1, :] if isinstance(e, int) else gate_bc[:, bass.ds(e, 1), :]
                return rows.broadcast_to([P, 2, S])

            def expert(par_, n, c, r=None, last=False):
                hidden_low(1 - par_, n - 1)
                lows(c + 2, 2, r)
                gated_hidden(par_, n)
                lows(c + 4, 2, r)
                raw_hidden(par_, n)
                if not last:
                    lows(c + 6, 2, r)

            lows(3, 1)
            gated_hidden(0, 0)
            raw_hidden(0, 0)
            lows(4, 2)
            for e in (1, 2):
                expert(e % 2, e, 6 * e - 2)
            with dve.Fori(0, (EXPERTS - 4) // 2) as r:
                for s in range(2):
                    expert((1 + s) % 2, r * 2 + (3 + s), 16 + 6 * s, r)
            e = EXPERTS - 1
            expert(1, e, 6 * e - 2, last=True)
            hidden_low(1, e)
            lows(6 * EXPERTS - 2, 2)
            fed[0] = 6 * EXPERTS
            dve.wait_ge(sem("moe_down"), EXPERTS)
            for m in range(KC):
                step(V.scalar_tensor_tensor(z[:, m, :], X1[:, m, :], ALPHA1, ps[4 + m // 2][:, (m % 2) * S:(m % 2 + 1) * S],
                                            ALU.mult, ALU.add), "z_written")
                step(V.tensor_copy(SV[0:1, 54:55], z[0:1, m, 0:1]), "mean_in")
            layer_norm("b", S, 1e-5)

            def modulate(l, q, n, which):
                hh = H if n == 512 else HB[:, 0:KC * S].rearrange("p (k t) -> p k t", k=KC)
                sh = 24 * q
                for k in range(KC):
                    dve.wait_ge(sem("ln_out"), nth(which) + k + 1)
                    for s in range(n // S):
                        tell(V.tensor_scalar(hh[:, k, s * S:(s + 1) * S], XC[:, k, s * S:(s + 1) * S],
                                             SC1[:, l, q, k, s:s + 1], MOD[:, l, sh + k, s:s + 1], ALU.mult, ALU.add),
                             "h_ready")

            def modulate_split(l, n, which):
                hi, lo = in_split(n)
                zz, _ = ln_bufs(n)
                for k in range(KC + 1):
                    if k < KC:
                        dve.wait_ge(sem("ln_out"), nth(which) + k + 1)
                        for s in range(n // S):
                            ss = slice(s * S, (s + 1) * S)
                            ins = V.tensor_scalar(zz[:, k, ss], XC[:, k, ss], SC1[:, l, 1, k, s:s + 1],
                                                  MOD[:, l, 24 + k, s:s + 1], ALU.mult, ALU.add)
                        tell(ins, "h_raw")
                    if k:
                        dve.wait_ge(sem("h_high"), KC * l + k)
                        tell(rest(lo[:, k - 1, :], zz[:, k - 1, :], hi[:, k - 1, :]), "h_split")

            if upto <= 5:
                return
            dve.wait_ge(sem("ctx_in"), 16)
            dve.wait_ge(sem("mods"), 4)
            modulate(0, 0, 512, "b")
            for m in range(5):
                b = bank(dve, ("qms", m))
                frees(V.tensor_scalar(tq[:, m, :], b[:, :], 1.0 / 64, 1e-6, ALU.mult, ALU.add), ("qms", m))
                evacuated(dve, ("qms", m))
                step(V.tensor_copy(SV[0:1, 55:56], tq[0:1, m, 0:1]), "q0_ms")
            for m in range(5):
                dve.wait_ge(sem("q0_rms"), m + 1)
                step(V.reciprocal(tq[:, m, :], tq[:, m, :]))
                g = p_("q_gain") if m < 4 else p_("k_gain")
                step(V.scalar_tensor_tensor(Q0[:, m, :], Q0[:, m, :], g, tq[:, m, :], ALU.mult, ALU.mult), "q0_normed")
            for m in range(5):
                b = bank(dve, ("rope0", m))
                frees(V.tensor_tensor(tq[:, m, 0:S], b[:, 0:S], c_("sin64"), ALU.mult), ("rope0", m))
                evacuated(dve, ("rope0", m))
                step(V.tensor_tensor(Q0[:, m, 0:S], Q0[:, m, 0:S], c_("cos64"), ALU.mult))
                step(V.tensor_tensor(Q0[:, m, 0:S], Q0[:, m, 0:S], tq[:, m, 0:S], ALU.add), "q0_roped")
            dve.wait_ge(sem("na_bias"), 16 * 32)
            for h in range(8):
                step(V.tensor_tensor(na_bias[:, h, :, :], na_bias[:, h, :, :], bc(c_("na_mask"), 2), ALU.add))
            attention("att2", att2, att2_P, att2_L)

            def residual(name, n, stage=None):
                zz, _ = ln_bufs(n)
                for m in range(KC):
                    if stage is not None:
                        feed(stage, (m * HF + HF - 1) // BLOCKS)
                    evacuated(dve, name(m))
                    part = lnst[:, m % 2, 0:n]
                    if stage is not None and stage[-1] == "B":
                        step(V.tensor_tensor(zz[:, m, :], zz[:, m, :], part, ALU.add), "z_written")
                    else:
                        step(V.scalar_tensor_tensor(zz[:, m, :], XC[:, m, 0:n], ALPHA2, part, ALU.mult, ALU.add),
                             "z_written")
                    if stage is None or stage[-1] == "B":
                        step(V.tensor_copy(SV[0:1, 54:55], zz[0:1, m, 0:1]), "mean_in")

            residual(lambda m: ("l0out", m), 512)
            feed("l0upA", 0)
            layer_norm("c", 512, 1e-6)
            modulate_split(0, 512, "c")

            def ffn(l, n):
                ns = n // S
                cw = p_(f"l{l}conv").rearrange("p (w j) -> p w j", w=3)
                cb = p_(f"l{l}convb")
                step(V.memset(gp[:, :, :, :], 0.0), "pad_zero")
                raw, split = 0, 0
                for half, part in enumerate("AB"):
                    chunks = range(UP_A) if half == 0 else range(UP_A, FF)
                    for j in chunks:
                        feed(f"l{l}up{part}", 2 * (j - chunks[0]))
                        evacuated(dve, (f"l{l}g", j))
                        if j >= 2:
                            dve.wait_ge(sem("ff_silu"), l * FF + j - 1)
                        g = gp[:, j % 2, 0:ns, :]
                        c = cg_[:, j % 2, 0:n].rearrange("p (a b) -> p a b", a=ns)
                        step(V.tensor_scalar(c, g[:, :, 0:S], cw[:, 0, j:j + 1], cb[:, j:j + 1], ALU.mult, ALU.add))
                        step(V.scalar_tensor_tensor(c, g[:, :, 1:S + 1], cw[:, 1, j:j + 1], c, ALU.mult, ALU.add))
                        step(V.scalar_tensor_tensor(c, g[:, :, 2:S + 2], cw[:, 2, j:j + 1], c, ALU.mult, ALU.add),
                             "conv_done")
                        while raw <= j - 1:
                            hidden(l, raw, n)
                            raw += 1
                        while split <= j - 2:
                            hidden_low(l, split, n)
                            split += 1
                    hidden(l, raw, n)
                    raw += 1
                    while split < (half + 1) * HF:
                        hidden_low(l, split, n)
                        split += 1
                    residual(lambda m: (f"l{l}down", half, m), n, f"l{l}down{part}")

            def hidden(l, j, n):
                dve.wait_ge(sem("ff_silu"), l * FF + j + 1)
                if j >= 2:
                    dve.wait_ge(sem("ff_split"), l * FF + j - 1)
                b = bank(dve, (f"l{l}v", j))
                ins = V.tensor_tensor(u_raw[:, j % 2, 0:n], sg_[:, j % 2, 0:n], b[:, 0:n], ALU.mult)
                frees(ins, (f"l{l}v", j))
                evacuated(dve, (f"l{l}v", j))
                step(V.tensor_copy(SV[0:1, 56:57], u_raw[0:1, j % 2, 0:1]), "ff_raw")

            def hidden_low(l, j, n):
                dve.wait_ge(sem("ff_high"), l * FF + j + 1)
                tell(rest(u_lo[:, j % HF, 0:n], u_raw[:, j % 2, 0:n], u_hi[:, j % HF, 0:n]), "ff_split")

            ffn(0, 512)
            layer_norm("d", 512, 1e-6)
            if upto <= 6:
                return
            modulate(1, 0, 512, "d")
            b = bank(dve, "cqms")
            frees(V.tensor_scalar(lnst[:, 0, 0:S], b[:, 0:S], 1.0 / 768, 1e-6, ALU.mult, ALU.add), "cqms")
            b = bank(dve, "ckvms1")
            frees(V.tensor_scalar(lnst[:, 1, :], b[:, :], 1.0 / 256, 1e-6, ALU.mult, ALU.add), "ckvms1")
            evacuated(dve, "cqms")
            step(V.tensor_copy(SV[0:1, 57:58], lnst[0:1, 0, 0:1]), "cq_ms")
            evacuated(dve, "ckvms1")
            step(V.tensor_copy(SV[0:1, 57:58], lnst[0:1, 1, 0:1]), "cq_ms")
            dve.wait_ge(sem("cq_rms"), 1)
            V.reciprocal(lnst[:, 0, 0:S], lnst[:, 0, 0:S])
            step(V.reciprocal(lnst[:, 1, :], lnst[:, 1, :]))
            for k in range(6):
                tell(V.scalar_tensor_tensor(cq1[:, k, :], cq1[:, k, :], p_("cq_gain")[:, k:k + 1], lnst[:, 0, 0:S],
                                            ALU.mult, ALU.mult), "cq_normed")
            for k in range(2):
                tell(V.scalar_tensor_tensor(ckv1[:, k, :], ckv1[:, k, :], p_("ckv_gain")[:, k:k + 1], lnst[:, 1, :],
                                            ALU.mult, ALU.mult), "ckv_normed1")
            kr = slice(64, 96)
            b = bank(dve, "krope")
            frees(V.tensor_tensor(tq1[kr, 0, 0:S], b[kr, 0:S], c_("sinm")[kr, :], ALU.mult), "krope")
            evacuated(dve, "krope")
            step(V.tensor_tensor(kr1[kr, 0:S], kr1[kr, 0:S], c_("cosm")[kr, :], ALU.mult))
            step(V.tensor_tensor(kr1[kr, 0:S], kr1[kr, 0:S], tq1[kr, 0, 0:S], ALU.add))
            for q in range(2):
                step(V.tensor_copy(kT1[kr, q, :], kr1[kr, :]), "kr_placed")
            for m in range(8):
                b = bank(dve, ("qrope", m))[0:96, :].rearrange(flat2, a=2)
                t = tq1[0:96, m % 2, :].rearrange(flat2, a=2)
                qq = q1[0:96, 2 * m:2 * m + 2, :]
                frees(V.tensor_tensor(t, b, bc(c_("sinm")[0:96, :], 2), ALU.mult), ("qrope", m))
                evacuated(dve, ("qrope", m))
                step(V.tensor_tensor(qq, qq, bc(c_("cosm")[0:96, :], 2), ALU.mult))
                step(V.tensor_tensor(qq, qq, t, ALU.add), "q1_roped")
            attention("att3", att3, att2_P, None)
            residual(lambda m: ("l1out", m), S)
            feed("l1upA", 0)
            layer_norm("e", S, 1e-6)
            modulate_split(1, S, "e")
            ffn(1, S)
            layer_norm("f", S, 1e-6)
            for k in range(KC):
                dve.wait_ge(sem("ln_out"), nth("f") + k + 1)
                step(V.tensor_copy(SV[0:1, 58:59], X1[0:1, k, 0:1]), "result_chunks")


def shape_constants():
    c = np.zeros((P, NCONST), np.float32)

    def put(name, a, rows=P):
        o, n = CONST[name]
        c[:rows, o:o + n] = a

    put("ident", np.eye(P))
    put("ones", np.ones((P, P)))
    half = np.arange(P) // 64
    put("blockones", (half[:, None] == half[None, :]))
    rot = np.zeros((P, P))
    for i in range(0, P, 2):
        rot[i + 1, i] = -1.0
        rot[i, i + 1] = 1.0
    put("rot", rot)
    pos = np.arange(S)

    def rope(dim):
        inv = (np.float32(10000.0) ** (-np.arange(0, dim // 2, 2, dtype=np.float32) / np.float32(dim // 2)))
        ang = np.concatenate([(pos // 64)[:, None].astype(np.float32) * inv,
                              (pos % 64)[:, None].astype(np.float32) * inv], -1).astype(np.float32)
        return np.repeat(np.cos(ang), 2, 1).T, np.repeat(np.sin(ang), 2, 1).T

    co, si = rope(64)
    put("cos64", np.tile(co, (2, 1)))
    put("sin64", np.tile(si, (2, 1)))
    co, si = rope(32)
    a = np.zeros((P, S))
    a[0:64] = 1.0
    a[64:96] = co
    put("cosm", a)
    a = np.zeros((P, S))
    a[64:96] = si
    put("sinm", a)
    dist = 255 - np.arange(512)
    dd = np.maximum(dist, 0)
    df = np.maximum(dd, 1).astype(np.float32)
    large = 16 + (np.log(df / np.float32(16)) / np.float32(math.log(128.0)) * np.float32(16)).astype(np.int32)
    bucket = np.where(dd < 16, dd, np.minimum(large, 31))
    t = np.zeros((34, 512))
    ok = dist >= 0
    t[bucket[ok], np.nonzero(ok)[0]] = 1.0
    count = ok * ((dist <= 128) * 1 + (dist % 4 == 0) + (dist % 16 == 0))
    t[32] = np.where(count > 0, np.log(np.maximum(count, 1)), NEG)
    t[33] = np.where(ok, 0.0, NEG)
    put("buckets", t, 34)
    col = np.arange(64)
    start = np.clip(col - 8, 0, 48)
    inside = (col[None, :] >= start[:, None]) & (col[None, :] < start[:, None] + 16)
    put("na_mask", np.tile(np.where(inside, 0.0, NEG), (2, 4)))
    i, j = np.arange(64)[:, None], np.arange(64)[None, :]
    put("upper", np.tile(i < j, (2, 1)))
    put("upper_incl", np.tile(i <= j, (2, 1)))
    put("lower", np.tile(i > j, (2, 1)))
    put("diag16", np.tile(i // 16 == j // 16, (2, 1)))
    put("eye64", np.tile(i == j, (2, 1)))
    put("heads_c", (np.arange(P) // 32)[:, None] == (np.arange(256) // 64)[None, :])
    q = np.arange(P)[:, None]
    put("causal", np.concatenate([np.where(np.arange(S)[None, :] <= q + P * n, 0.0, NEG) for n in range(2)], 1))
    put("scan_ones", np.ones((P, 64)))
    return c


def lay_out(v):
    f32 = np.float32

    def blocks(w, order="mk"):
        kk, mm = w.shape
        b = w.reshape(kk // P, P, mm // P, P)
        b = b.transpose(2, 0, 1, 3) if order == "mk" else b.transpose(0, 2, 1, 3)
        return b.reshape(-1, P, P)

    def tiles(bl):
        n = -(-len(bl) // BLOCKS)
        if len(bl) < n * BLOCKS:
            bl = np.concatenate([bl, np.zeros((n * BLOCKS - len(bl), P, P), f32)])
        return bl.reshape(n, BLOCKS, P, P).transpose(0, 2, 1, 3).reshape(n, P, TILE)

    wi = v["w_in"][0]

    def cols(name, a=0, b=None):
        o = IN_OFF[name]
        return wi[:, o + a:o + (b if b is not None else dict(IN_NAMES)[name])]

    small = np.zeros((D, P), f32)
    small[:, R_W:R_W + 16] = cols("d", 768, 784)
    small[:, R_A:R_A + 16] = cols("d", 784, 800)
    small[:, R_G:R_G + 32] = cols("d", 800, 832)
    small[:, R_C:R_C + 16] = cols("c_a")
    iwp = np.zeros((D, P), f32)
    iwp[:, 0:8] = cols("b_iw")
    w1 = np.concatenate([cols("b_iq"), np.tile(cols("b_ik"), (1, 4)), iwp, np.tile(cols("b_ckv"), (1, 2)),
                         cols("b_q"), small, cols("d", 0, 768), cols("c_q"), cols("c_k"), cols("c_v"), cols("c_g"),
                         cols("a_q"), cols("a_k"), cols("a_v")], 1)
    parts = [tiles(blocks(w1))]
    for l in range(2):
        parts.append(v[f"l{l}_w_ada_2"].reshape(KC, P, ADA // 1024, 1024).transpose(2, 0, 1, 3).reshape(-1, P, TILE))
    gt = blocks(cols("gate")).reshape(4, KC, KC, P, P)
    br = np.stack([blocks(v["w_branch"][0, n]).reshape(KC, 2, P, P) for n in range(4)])
    mg = np.concatenate([gt.transpose(1, 0, 2, 3, 4).reshape(KC, 32, P, P),
                         br.transpose(1, 0, 2, 3, 4).reshape(KC, 8, P, P)], 1).reshape(-1, P, P)
    parts.append(tiles(mg))
    parts.append(tiles(blocks(v["w_out"][0])))
    moe = {"gate": v["moe_w_gate"][0], "up": v["moe_w_up"][0], "down": v["moe_w_down"][0]}
    parts.append(np.concatenate([tiles(blocks(moe[kind][e], "km" if kind == "down" else "mk"))
                                 for kind, e in moe_tiles()]))
    w = v["l0_w_in_2"]
    qa = w[:, 0:512].reshape(D, 2, 4, 64).transpose(0, 2, 1, 3).reshape(D, 512)
    parts.append(tiles(blocks(np.concatenate([qa, w[:, 512:]], 1))))
    w = v["l0_w_out_2"]
    wa = w[0:512].reshape(2, 4, 64, D).transpose(1, 0, 2, 3).reshape(512, D)
    parts.append(tiles(blocks(np.concatenate([wa, w[512:]], 0))))

    def ff(l):
        up = tiles(blocks(v[f"l{l}_w_up_2"]).reshape(2, FF, KC, P, P).transpose(1, 0, 2, 3, 4).reshape(-1, P, P))
        down = v[f"l{l}_w_down_2"]
        return [up[:2 * UP_A], tiles(blocks(down[:HF * P])), up[2 * UP_A:], tiles(blocks(down[HF * P:]))]

    parts += ff(0)
    w = v["l1_w_in_2"]
    krp = np.zeros((D, P), f32)
    krp[:, 64:96] = w[:, 1024:1056]
    parts.append(tiles(blocks(np.concatenate([w[:, 768:1024], krp, w[:, 0:768]], 1))))
    uq = np.zeros((768, 16, P), f32)
    uq[:, :, 0:96] = v["l1_w_uq_2"].reshape(768, 16, 96)
    parts.append(tiles(blocks(uq.reshape(768, 2048))))
    ukv = v["l1_w_ukv_2"].reshape(2, P, 16, 2, 64)
    for which in (1, 0):
        parts.append(ukv[:, :, :, which, :].reshape(2, P, TILE))
    parts.append(tiles(blocks(v["l1_w_out_2"])))
    parts += ff(1)
    wall = np.concatenate(parts)
    assert wall.shape[0] == stream_plan()[1], (wall.shape, stream_plan()[1], [x.shape[0] for x in parts])

    par = np.zeros((P, NPARAM), f32)

    def put(name, a, r0=0):
        o, n = PARAM[name]
        a = np.asarray(a, f32)
        par[r0:r0 + a.shape[0], o:o + a.shape[1]] = a

    def col(a):
        return np.asarray(a, f32).reshape(-1, P).T

    put("kv_gain", np.tile(v["b_kv_gain"][0], 2)[:, None])
    put("c_a_bias", col(v["c_a_bias"][0]))
    put("c_norm_gain", col(v["c_norm_gain"][0]))
    mu = v["d_mu"][0]
    o = PARAM["d_mu"][0]
    par[R_W:R_W + 16, o] = mu[768:784]
    par[R_A:R_A + 16, o] = mu[784:800]
    par[R_G:R_G + 32, o] = mu[800:832]
    par[:, o + 1:o + 7] = col(mu[:768])
    for nm in ("d_w0", "d_a0", "d_k_k", "d_k_a", "d_r_k", "d_gn_w", "d_gn_b"):
        put(nm, col(v[nm][0]))
    for n in range(2):
        put(f"ln{n + 1}g", col(v["ln_g"][0, n]))
        put(f"ln{n + 1}b", col(v["ln_b"][0, n]))
    for l in range(2):
        put(f"bada{l}", col(v[f"l{l}_b_ada_2"]))
        for n in range(1, 3):
            for s in "gb":
                put(f"l{l}ln{n}{s}", col(v[f"l{l}_ln{n}_{s}_2"]))
        put(f"l{l}conv", np.concatenate([col(v[f"l{l}_conv_w_2"][n]) for n in range(3)], 1))
        put(f"l{l}convb", col(v[f"l{l}_conv_b_2"]))
    put("q_gain", np.tile(v["l0_q_gain_2"], 2)[:, None])
    put("k_gain", np.tile(v["l0_k_gain_2"], 2)[:, None])
    put("cq_gain", col(v["l1_cq_gain_2"]))
    put("ckv_gain", col(v["l1_ckv_gain_2"]))
    put("cond", np.stack([col(v["c_2"][0]), col(v["c_ctx_2"])], 2).reshape(P, 16))
    put("lora", v["d_w2"][0], R_W)
    put("lora", v["d_a2"][0], R_A)
    put("lora", v["d_g2"][0], R_G)
    put("lora", v["c_a_up"][0], R_C)
    put("w_uv", v["b_w_uv"][0].transpose(1, 0, 2).reshape(64, 256))
    r = np.concatenate([v["router_g"][0], v["router_e"][0]], 1)
    put("router", r.reshape(KC, P, 36).transpose(1, 0, 2).reshape(P, 288))
    put("router_bias", np.tile(np.concatenate([v["router_g_bias"][0], v["router_e_bias"][0]])[None], (P, 1)))
    rows = np.zeros((34, 8), f32)
    rows[0:32] = v["rpb_table"]
    rows[32, 0:4] = 1.0
    rows[33, 4:8] = 1.0
    put("rpb_rows", rows)
    rpb = np.zeros((8, 7, P), f32)
    rpb[:, :, 48:79] = v["l0_rpb_2"][:, 4:11, :]
    xt = np.ascontiguousarray(v["x"][0].T).reshape(KC, P, S)
    ct = np.ascontiguousarray(v["ctx_2"][0].T).reshape(KC, P, S)
    return {"wall": wall, "consts": shape_constants(), "params": par, "xin": xt, "ctxin": ct,
            "rpb_pad": rpb.reshape(8, 896)}


def kernel(**inputs):
    import concourse.bacc as bacc
    from concourse.bass_utils import run_bass_kernel_spmd

    nc = bacc.Bacc("TRN2", target_bir_lowering=False, num_devices=1)
    arrays = {k: np.ascontiguousarray(a) for k, a in lay_out({k: np.asarray(a) for k, a in inputs.items()}).items()}
    aps = [nc.dram_tensor(k, a.shape, F32, kind="ExternalInput").ap() for k, a in arrays.items()]
    out = nc.dram_tensor("out", [KC, P, S], F32, kind="ExternalOutput").ap()
    build(nc, *aps, out)
    r = run_bass_kernel_spmd(nc, [arrays], core_ids=[0])
    return np.ascontiguousarray(r.results[0]["out"].reshape(D, S).T[None])
```

```python
import math
from contextlib import ExitStack

import numpy as np

import concourse.bass as bass
from concourse import mybir

F32 = mybir.dt.float32
F32R = mybir.dt.float32r
ALU = mybir.AluOpType
ACT = mybir.ActivationFunctionType
AX = mybir.AxisListType

P = 128
D = 1024
KC = D // P
S = 256
NBANK = 8
RING = 6
SPLIT_RING = 3
BLOCKS = 8
TILE = BLOCKS * P
NP = 3
NEG = -1e30
HEAD_SCALE = 64 ** -0.5
MLA_SCALE = 96 ** -0.5
TAKEN = -3e38
ALPHA1 = 2.0 ** 0.25
ALPHA2 = 4.0 ** 0.25
EXPERTS = 32
FF = 22
HF = FF // 2
ADA = 6 * D
CH = 64
NCH = S // CH
KEEP = 64
W_DECAY = math.exp(-0.5)

IN_NAMES = (("a_q", 256), ("a_k", 256), ("a_v", 256), ("b_q", 256), ("b_ckv", 64), ("b_iq", 256), ("b_ik", 32),
            ("b_iw", 8), ("c_q", 128), ("c_k", 128), ("c_v", 256), ("c_a", 16), ("c_g", 256), ("d", 832),
            ("gate", 4096))
IN_OFF = {}
_o = 0
for _n, _w in IN_NAMES:
    IN_OFF[_n] = _o
    _o += _w
IN_BLOCKS = ["iq0", "iq1", "ik", "iw", "ckv", "bq0", "bq1", "small", "dr0", "dr1", "dk0", "dk1", "dv0", "dv1",
             "cq", "ck", "cv0", "cv1", "cg0", "cg1", "aq0", "aq1", "ak0", "ak1", "av0", "av1"]
R_W, R_A, R_G, R_C = 0, 32, 64, 96


def stream_plan():
    order = [("in", 26), ("ada0", ADA // 128), ("ada1", ADA // 128), ("merge", 40), ("out", 8)]
    order += [("moe", 6 * EXPERTS)]
    order += [("l0in", 18), ("l0out", 8), ("l0upA", 24), ("l0downA", HF), ("l0upB", 20), ("l0downB", HF)]
    order += [("l1in", 9), ("l1uq", 12), ("l1ukv", 4), ("l1out", 8), ("l1upA", 24), ("l1downA", HF), ("l1upB", 20),
              ("l1downB", HF)]
    first, at = {}, 0
    for name, n in order:
        first[name] = at
        at += n
    return first, at, dict(order)


SPLIT = ("in", "ada0", "ada1", "merge", "out", "moe", "l0in", "l0out", "l0upA", "l0downA", "l0upB", "l0downB", "l1in", "l1uq", "l1out", "l1upA", "l1downA", "l1upB", "l1downB")
UP_A = HF + 1


def moe_tiles():
    tiles = []
    for e in range(EXPERTS):
        tiles += [("gate", e), ("up", e)]
        if e:
            tiles.append(("down", e - 1))
    return tiles + [("down", EXPERTS - 1)]


def columns(items):
    at, out = 0, {}
    for name, n in items:
        out[name] = (at, n)
        at += n
    return out, at


CONST_ITEMS = [("ident", 128), ("ones", 128), ("blockones", 128), ("zeros", 128), ("rot", 128),
               ("cos64", 256), ("sin64", 256), ("cosm", 256), ("sinm", 256), ("buckets", 512),
               ("na_mask", 256), ("upper", 64), ("upper_incl", 64), ("lower", 64), ("diag16", 64), ("eye64", 64),
               ("heads_c", 256), ("causal", 512), ("scan_ones", 64)]
PARAM_ITEMS = [("kv_gain", 1), ("c_a_bias", 1), ("c_norm_gain", 2), ("d_mu", 7), ("d_w0", 2), ("d_a0", 2),
               ("d_k_k", 2), ("d_k_a", 2), ("d_r_k", 2), ("d_gn_w", 2), ("d_gn_b", 2),
               ("ln1g", 8), ("ln2g", 8), ("ln1b", 8), ("ln2b", 8),
               ("bada0", 48), ("bada1", 48), ("q_gain", 1), ("k_gain", 1),
               ("l0ln1g", 8), ("l0ln1b", 8), ("l0ln2g", 8), ("l0ln2b", 8),
               ("l1ln1g", 8), ("l1ln1b", 8), ("l1ln2g", 8), ("l1ln2b", 8),
               ("l0conv", 66), ("l0convb", 22), ("l1conv", 66), ("l1convb", 22),
               ("cq_gain", 6), ("ckv_gain", 2), ("cond", 16),
               ("lora", 256), ("w_uv", 256), ("router", 288), ("router_bias", 36), ("rpb_rows", 8)]
CONST, NCONST = columns(CONST_ITEMS)
PARAM, NPARAM = columns(PARAM_ITEMS)


def build(nc, wall, consts, params, xin, ctxin, rpb_pad, out):
    first, n_tiles, stage_tiles = stream_plan()
    split_order = [first[st] + n for st in SPLIT for n in range(stage_tiles[st])]
    split_at = {t: i for i, t in enumerate(split_order)}
    whole_at = {t: i for i, t in enumerate(t for t in range(n_tiles) if t not in split_at)}
    moe0 = first["moe"]
    split0 = split_at[moe0]

    def run_end(t):
        while t < n_tiles and (t in split_at) == ((t - 1) in split_at or t == 0):
            t += 1
        return t
    with ExitStack() as ctx:
        def sb(name, shape, dtype=F32):
            return ctx.enter_context(nc.sbuf_tensor(name, shape, dtype))

        def as_f32r(name, cols):
            return nc.alloc_sbuf_tensor_at(name, [P, cols], F32R, offset=nc.sbuf_base - 4 * cols)

        sems = {}

        def sem(name):
            if name not in sems:
                sems[name] = ctx.enter_context(nc.semaphore(name))
            return sems[name]

        ring = sb("ring", [P, RING, TILE])
        w_hi = sb("w_hi", [P, SPLIT_RING, TILE], F32R)
        w_lo = sb("w_lo", [P, SPLIT_RING, TILE], F32R)
        con = sb("con", [P, NCONST])
        par = sb("par", [P, NPARAM])
        XC = sb("XC", [P, KC, 2 * S])
        XCR = nc.alloc_sbuf_tensor_at("XC_f32r", [P, KC, 2 * S], F32R, offset=nc.sbuf_base - 4 * KC * 2 * S)
        x_hi = XCR[:, :, S:2 * S]
        BIG = sb("BIG", [P, 3 * 4096])
        BIGR = as_f32r("BIG_f32r", 3 * 4096)
        lnst = sb("lnst", [P, 3, 512])
        lnst_f32r = as_f32r("lnst_f32r", 1536)
        MOD = sb("MOD", [P, 2, 48, 2])
        SC1 = sb("SC1", [P, 2, 2, 8, 2])
        SV = sb("SV", [P, 96])
        arena_n = 17472
        AR = sb("AR", [P, arena_n])
        ARR = as_f32r("AR_f32r", arena_n)
        ada_mat = sb("ada_mat", [P, 2, P])
        ps = [ctx.enter_context(nc.psum_tensor(f"bank{b}", [P, 512], F32))[:, :] for b in range(NBANK)]

        def c_(name):
            o, n = CONST[name]
            return con[:, o:o + n]

        def p_(name):
            o, n = PARAM[name]
            return par[:, o:o + n]

        class Arena:

            def __init__(self, region, size, start=0, region_f32r=None):
                self.region, self.size, self.at, self.region_f32r = region, size, start, region_f32r

            def take_f32r(self, *shape):
                return self.take(*shape, region=self.region_f32r)

            def take(self, *shape, region=None):
                n = int(np.prod(shape))
                a = (self.region if region is None else region)[:, self.at:self.at + n]
                self.at += n
                assert self.at <= self.size, (self.at, self.size)
                if len(shape) == 1:
                    return a
                names = "abcde"[:len(shape)]
                return a.rearrange(f"p ({' '.join(names)}) -> p {' '.join(names)}",
                                   **{k: v for k, v in zip(names[1:], shape[1:])})

        Z = BIG[:, 0:4096]
        SQ = BIG[:, 4096:8192]
        HB = BIG[:, 8192:12288]
        X1 = XC[:, :, 0:S]

        a1 = Arena(AR, arena_n, 0, ARR)
        F = {}
        for name, n in (("iq", 2), ("ik", 1), ("ckv", 1), ("bq", 2), ("cq", 1), ("ck", 1), ("cg", 2), ("aq", 2),
                        ("ak", 2)):
            F[name] = a1.take(n, S)
        cv = a1.take(2, 256)
        av = a1.take(2, 256)
        vb = a1.take(2, 256)
        iw = a1.take(2, 8)
        dS = a1.take(7, S)
        ysT = a1.take(4, 2, S)
        small_act = a1.take(S)
        x_lo = [lnst_f32r[:, k * S:(k + 1) * S] for k in range(6)] + [a1.take_f32r(S) for k in range(2)]
        DZ = {n: a1.take(2, S) for n in ("w", "a", "g")}
        c_z = a1.take(S)
        a1_common = a1.at
        dF = a1.take(7, S + 1)
        dF_end = a1.at
        bA = Arena(BIG, 12288)
        bias1 = bA.take(8, 2, S)
        att1_L = bA.take(3, S)
        att1_P = bA.take(NP, S)
        att1_PT = bA.take(NP, 2, P)
        rel = bA.take(2, 2, S)
        score = bA.take(2, S)
        work = bA.take(2, 2, S)
        top8 = bA.take(2, 8)
        selm = bA.take(2, S)
        rows8 = bA.take(512)

        cC = Arena(BIG, 12288)
        C = {n: cC.take(S) for n in ("zb", "ab", "ln", "la", "cum", "ec", "en", "ed", "qd", "ki", "kd")}
        c_kdt = cC.take(2, P)
        c_att = cC.take(4, 2, CH)
        c_state = cC.take(3, S)
        c_sm = cC.take(3, S)
        c_o = cC.take(2, S)
        c_sq = cC.take(2, S)
        bD = Arena(BIG, 12288)
        DD = {n: bD.take(2, S) for n in ("lw", "cum", "cm1", "e1", "e2", "e3", "kk", "kp", "b", "Bh", "Kh", "t")}
        Ah = bD.take(2, S)
        Rh = bD.take(2, S)
        yT = bD.take(2, S)
        bn = bD.take(2, S)
        dU = Arena(BIG, 12288, bD.at)
        cU = Arena(AR, arena_n, a1_common)
        U = {n: dU.take(8, CH) for n in ("N", "A", "GRB", "GAK", "GRK", "Vt", "Bt", "Kt")}
        U |= {n: cU.take(8, CH) for n in ("D", "Dt", "D2", "D2t", "D4", "D4t", "Z", "W", "Lo")}
        U["D8"], U["D8t"] = U["D"], U["Dt"]
        U["Pm"], U["Pt"], U["P2t"], U["Y1"], U["T"] = U["D2"], U["D2t"], U["D4"], U["D4t"], U["Lo"]
        x_u = cU.take(2, 2, CH)
        m_st = cU.take(5, 2, CH)
        aA = Arena(AR, arena_n, dF_end, ARR)
        ada_rows = aA.take(4, 512)
        cond_st = aA.take_f32r(KC, P)
        ada_mat_lo = Arena(AR, arena_n, arena_n - 2 * P).take(2, P)
        assert max(aA.at, cU.at) <= arena_n - 2 * P
        cM = Arena(AR, arena_n, a1_common)
        tmpm = cM.take(2, 2, 2, S)
        gates = cM.take(2, 4, S)
        mergedT = HB[:, 0:2048].rearrange("p (k t) -> p k t", k=KC)
        mg_hi, mg_lo = [BIGR[:, o:o + 2048].rearrange("p (k t) -> p k t", k=KC) for o in (4096, 6144)]
        ys_hi, ys_lo = [BIGR[:, o:o + 2048].rearrange("p (n k t) -> p n k t", n=4, k=2) for o in (0, 2048)]

        def ln_bufs(n):
            z = Z[:, 0:KC * n].rearrange("p (k t) -> p k t", k=KC)
            sq = SQ[:, 0:KC * n].rearrange("p (k t) -> p k t", k=KC)
            return z, sq

        aM = Arena(AR, arena_n, 0, ARR)
        gate_bc = aM.take(EXPERTS, S)
        m_sg = aM.take(2, 2, S)
        m_t = aM.take(2, 2, S)
        mh_hi = aM.take_f32r(2, 2, S)
        mh_lo = aM.take_f32r(2, 2, S)
        lg = aM.take(2, 36)
        rt = aM.take(2, 12, 32)
        gateT = aM.take(S)

        def in_split(n):
            return [BIGR[:, o:o + KC * n].rearrange("p (k t) -> p k t", k=KC) for o in (8192, 4096)]

        mx_hi = BIGR[:, 8192:10240].rearrange("p (k t) -> p k t", k=KC)
        mx_lo = BIGR[:, 10240:12288].rearrange("p (k t) -> p k t", k=KC)

        a2 = Arena(AR, arena_n, 0, ARR)
        Q0 = a2.take(5, 512)
        qb = a2.take(4, 512)
        kb = a2.take(4, 512)
        V0 = a2.take(4, 640)
        yT0 = a2.take(8, 512)
        na_bias = a2.take(8, 2, S)
        y0_hi = BIGR[:, 8192:12288].rearrange("p (k t) -> p k t", k=KC)
        y0_lo = ARR[:, 0:4096].rearrange("p (k t) -> p k t", k=KC)
        aP = Arena(SQ, 4096)
        att2_P = aP.take(NP, 512)
        att2_PT = aP.take(NP, 4, P)
        aL = Arena(Z, 4096)
        att2_L = aL.take(3, 512)
        tq = aL.take(5, 512)
        tq2 = yT0[:, 0:5, :]

        aF = Arena(AR, arena_n, 0, ARR)
        u_hi = aF.take_f32r(HF, 512)
        u_lo = aF.take_f32r(HF, 512)
        u_raw = aF.take(2, 512)
        gp = aF.take(2, 2, S + 2)
        cg_ = aF.take(2, 512)
        sg_ = aF.take(2, 512)

        a3 = Arena(AR, arena_n, 0, ARR)
        cq1 = a3.take(6, S)
        ckv1 = a3.take(2, 512)
        kr1 = a3.take(512)
        cq_hi, cq_lo = [ARR[:, a3.at + o:a3.at + o + 6 * S].rearrange("p (k t) -> p k t", k=6) for o in (0, 6 * S)]
        sq1 = a3.take(8, 512)
        q1 = a3.take(16, S)
        V1 = a3.take(4, 1024)
        kT1 = a3.take(2, 512)
        yT1 = Z[:, 2048:4096].rearrange("p (k t) -> p k t", k=KC)
        y1_hi, y1_lo = [BIGR[:, o:o + 2048].rearrange("p (k t) -> p k t", k=KC) for o in (8192, 10240)]
        tq1 = SQ[:, 3072:4096].rearrange("p (a b) -> p a b", a=2)

        scr_t5 = nc.dram_tensor("t5_rows", [8, P, 512], F32, kind="Internal").ap()
        scr_na = nc.dram_tensor("na_rows", [8, CH, 896], F32, kind="Internal").ap()
        scr_ada = nc.dram_tensor("ada_results", [2, 4, ADA], F32, kind="Internal").ap()
        scr_gate = nc.dram_tensor("gate_rows", [EXPERTS, S], F32, kind="Internal").ap()

        bank_ready = [sem(f"bank_ready{b}") for b in range(NBANK)]
        bank_free = [sem(f"bank_free{b}") for b in range(NBANK)]
        w_ready = [sem(f"weights_in_slot{s}") for s in range(RING)]
        w_free = sem("ring_slots_freed")
        w_high = sem("weight_high_parts")
        w_split = sem("weight_tiles_split")
        w_used = sem("split_tiles_used")

        def spec(q, k, v, o, bias=None, nk=S):
            return dict(q=q, k=k, v=v, o=o, bias=bias, nk=nk)

        att1, att2, att3 = [], [], []
        for br, (fq, fk, fv) in enumerate(((F["aq"], F["ak"], av), (F["bq"], None, vb))):
            for h in range(4):
                r = slice(64 * (h % 2), 64 * (h % 2) + 64)
                for i in range(2):
                    k = fk[r, h // 2, :] if br == 0 else F["ckv"][r, 0, :]
                    att1.append(spec(fq[r, h // 2, i * P:(i + 1) * P], k,
                                     [fv[:, t, h * 64:(h + 1) * 64] for t in range(2)],
                                     ysT[r, br, h // 2, i * P:(i + 1) * P], bias=bias1[:, 4 * br + h, i, :]))
        units = [(2 * hp + q, 2 * part + i) for hp in range(8) for part in range(2) for q in range(2) for i in range(2)]
        for h, i in units:
            r = slice(64 * (h % 2), 64 * (h % 2) + 64)
            if h < 8:
                j, g = h // 2, h % 2
                q, kk, v0 = Q0[r, j, :], Q0[r, 4, :], 64 * g
            else:
                j = (h - 8) // 2
                q, kk, v0 = qb[r, j, :], kb[r, j, :], P + 64 * (h - 8)
            y = yT0[r, h // 2, i * P:(i + 1) * P]
            if i < 2:
                b = na_bias[:, h - 8, i, :] if h >= 8 else None
                att2.append(spec(q[:, i * P:(i + 1) * P], kk, [V0[:, t, v0:v0 + 64] for t in range(4)], y, b, 512))
            else:
                att2.append(spec(q[:, i * P:(i + 1) * P], kk[:, S:2 * S],
                                 [V0[:, t, v0:v0 + 64] for t in (2, 3)], y, None, S))
        for h in range(16):
            for i in range(2):
                att3.append(spec(q1[0:96, h, i * P:(i + 1) * P], kT1[0:96, h % 2, :],
                                 [V1[:, t, h * 64:(h + 1) * 64] for t in range(4)],
                                 yT1[64 * (h % 2):64 * (h % 2) + 64, h // 2, i * P:(i + 1) * P],
                                 None, 512))

        def att_order(st, n):
            for i in range(n + NP):
                if st == "att3" and i == 0:
                    yield ("kT", 0)
                if i < n:
                    yield (st, "S", i)
                if st == "att3" and i % 2 == 0 and i < n - 2:
                    yield ("kT", i // 2 + 1)
                if 0 <= i - NP + 1 < n:
                    yield (st, "T", i - NP + 1)
                if 0 <= i - NP < n:
                    yield (st, "O", i - NP)

        before_ = {"att1": 0, "att2": len(att1), "att3": len(att1) + len(att2)}
        exp_before = {"att1": 0, "att2": len(att1), "att3": len(att1) + 16}

        def nth(which):
            return KC * "abcdef".index(which)

        FAM1 = ["N", "A", "GRB", "GAK", "GRK", "Vt", "Bt", "Kt"]
        FAM2 = ["D2", "D2t", "Z1", "W1", "D4", "D4t", "Z2", "W2", "D8", "D8t", "Z3", "W3", "Pm", "Pt", "P2t", "Y1", "T"]
        plan = []

        def add(*names):
            plan.extend(names)

        add(*[("in", b) for b in range(11)], "ckvms")
        add(*[("in", b) for b in range(11, 16)], "vb")
        add(*[("in", b) for b in range(16, 26)])
        add("t5")
        add(*[("ix", i, b) for i in range(2) for b in range(4)])
        add(*[("ada", l, g, q) for l in range(2) for g in range(ADA // 1024) for q in range(2)])
        add("dw", "da", "dg", "ca")
        add(*att_order("att1", 16))
        add("ckd", *[("catt", h) for h in range(4)], *[("cupd", c) for c in range(3)], *[("co", hp, q) for hp in range(2) for q in range(2)], "coms")
        add("kkn")
        for fam in FAM1 + FAM2:
            add((fam, 0), (fam, 1))
        for c in range(NCH):
            for what in ("X", "U", "Yc", "M"):
                if what == "M" and c == NCH - 1:
                    continue
                add((what, c, 0), (what, c, 1))
        add("bonus", "ymean", "yvar")
        add(("adaT", 0), ("adaT", 1))
        for m in range(KC):
            add(("gt", m, 0), ("gt", m, 1), ("br", m, 0), ("br", m, 1))
        add(*[("out1", m) for m in range(KC)], ("mean", "a"), ("var", "a"))
        add(("rt", 0), ("rt", 1), "BANK4", "gateT")
        plan.append("MOE")
        add(("mean", "b"), ("var", "b"))
        L0_ORDER = [("l0in", m) for m in range(7)] + [("qms", m) for m in range(5)] \
            + [("l0in", m) for m in range(7, 13)] + [("rope0", m) for m in range(5)] \
            + [("l0in", 13)] + [("l0vals", t) for t in range(4)]
        add(*L0_ORDER)
        add(*att_order("att2", 64))
        add(*[("l0out", m) for m in range(KC)], ("mean", "c"), ("var", "c"))
        for half, chunks in enumerate((range(UP_A), range(UP_A, FF))):
            for j in chunks:
                add(("l0g", j), ("l0v", j))
            add(*[("l0down", half, m) for m in range(KC)])
        add(("mean", "d"), ("var", "d"))
        add(*[("l1in", m) for m in range(9)], "cqms", "ckvms1")
        add("krope", *[("uq", m) for m in range(8)], *[("qrope", m) for m in range(8)])
        add(*[("v1", t, hf) for hf in range(2) for t in range(4)])
        add(*att_order("att3", 32))
        add(*[("l1out", m) for m in range(KC)], ("mean", "e"), ("var", "e"))
        for half, chunks in enumerate((range(UP_A), range(UP_A, FF))):
            for j in chunks:
                add(("l1g", j), ("l1v", j))
            add(*[("l1down", half, m) for m in range(KC)])
        add(("mean", "f"), ("var", "f"))
        job, at, uses = {}, 0, [0] * NBANK
        moe_uses = None
        for name in plan:
            if name == "MOE":
                moe_uses = list(uses)
                continue
            if name == "BANK4":
                at += -(at - 4) % NBANK
                continue
            b = at % NBANK
            uses[b] += 1
            job[name] = (b, uses[b])
            at += 1

        def bank(eng, name):
            b, use = job[name]
            eng.wait_ge(bank_ready[b], use)
            return ps[b]

        def evacuated(eng, name):
            b, use = job[name]
            eng.wait_ge(bank_free[b], use)

        def frees(ins, name):
            ins.then_inc(bank_free[job[name][0]], 1)

        def bc(ap, n):
            return ap.unsqueeze(1).broadcast_to([ap.shape[0], n, ap.shape[1]])

        block = ctx.enter_context(nc.Block())

        @block.sync
        def _(sp):
            for t in range(RING):
                if t == 1:
                    sp.wait_ge(sem("x_in"), 16)
                sp.dma_start(ring[:, t, :], wall[t]).then_inc(w_ready[t], 16)
            t = RING
            while t < n_tiles:
                old = t - RING
                place = split_at if old in split_at else whole_at
                freed = w_split if old in split_at else w_free
                end = min(run_end(old + 1) + RING, n_tiles)
                rounds = (end - t) // RING
                if rounds > 1:
                    with sp.Fori(0, rounds) as r:
                        for q in range(RING):
                            sp.wait_ge(freed, r * RING + (place[old] + q + 1))
                            sp.dma_start(ring[:, (t + q) % RING, :], wall[r * RING + (t + q)])\
                                .then_inc(w_ready[(t + q) % RING], 16)
                    t += rounds * RING
                while t < end:
                    sp.wait_ge(freed, place[t - RING] + 1)
                    sp.dma_start(ring[:, t % RING, :], wall[t]).then_inc(w_ready[t % RING], 16)
                    t += 1
            for k in range(KC):
                sp.wait_ge(sem("result_chunks"), k + 1)
                sp.dma_start(out[k], X1[:, k, :]).then_inc(sem("stored"), 16)
            sp.wait_ge(sem("stored"), 16 * KC)

        @block.gpsimd
        def _(gp_):
            gp_.wait_ge(w_ready[3], 16)
            gp_.dma_start(scr_na, bass.AP(rpb_pad.tensor, 0, [[896, 8], [0, CH], [1, 896]])).then_inc(sem("na_rows"), 16)
            gp_.wait_ge(sem("t5_row_ready"), 1)
            for h in range(8):
                gp_.dma_start(bass.AP(scr_t5.tensor, h * P * 512, [[P * 512, 1], [512, P], [1, 512]]),
                              rows8[h:h + 1, :].unsqueeze(1).broadcast_to([1, P, 512])).then_inc(sem("t5_rows"), 16)
            gp_.wait_ge(sem("t5_rows"), 16 * 8)
            for i in range(2):
                src = bass.AP(scr_t5.tensor, 255 - P * i, [[511, P], [P * 512, 8], [1, S]])
                gp_.dma_start(bias1[:, :, i, :], src).then_inc(sem("bias1"), 16)
            for l in range(2):
                for g in range(ADA // 512):
                    evacuated(gp_, ("ada", l, g // 2, g % 2))
                    gp_.dma_start(scr_ada[l, :, g * 512:(g + 1) * 512], ada_rows[0:4, g % 4, :])\
                        .then_inc(sem(f"ada_row_stored{g % 4}"), 16)
                for q in range(4):
                    gp_.wait_ge(sem(f"ada_row_stored{q}"), 16 * 3 * (l + 1))
                for part, mat in enumerate((ada_mat, ada_mat_lo)):
                    gp_.dma_start(mat[0:96, l, :], scr_ada[l, 2 * part:2 * part + 2].rearrange("s (m p) -> (s m) p", p=P))\
                        .then_inc(sem(f"ada_mat{l}"), 16)
            gp_.wait_ge(sem("merged"), KC)
            gp_.dma_start(XC[:, :, S:2 * S], ctxin.rearrange("k p t -> p k t")).then_inc(sem("ctx_in"), 16)
            gp_.wait_ge(sem("gateT_ready"), 1)
            gp_.dma_start(scr_gate, gateT[0:EXPERTS, :]).then_inc(sem("gate_rows"), 16)
            gp_.wait_ge(sem("gate_rows"), 16)
            gp_.dma_start(gate_bc, bass.AP(scr_gate.tensor, 0, [[0, P], [S, EXPERTS], [1, S]])).then_inc(sem("gate_bc"), 16)
            gp_.wait_ge(sem("na_rows"), 16)
            gp_.wait_ge(sem("moe_hidden"), EXPERTS)
            for h in range(8):
                for i in range(2):
                    for r in range(2):
                        src = bass.AP(scr_na.tensor, h * CH * 896 + (3 - 2 * i - r) * P + 63,
                                      [[895, CH], [P, 4], [1, CH]])
                        dst = na_bias[64 * r:64 * r + 64, h, i, :].rearrange("p (a b) -> p a b", a=4)
                        gp_.dma_start(dst, src).then_inc(sem("na_bias"), 16)

        @block.tensor
        def _(pe):
            state = {"tile": None, "held": 1, "pending": None, "at": 0}

            def open_(name):
                b, use = job[name]
                while plan[state["at"]] in ("MOE", "BANK4"):
                    state["at"] += 1
                assert plan[state["at"]] == name, (plan[state["at"]], name)
                state["at"] += 1
                if use > 1:
                    pe.wait_ge(bank_free[b], use - 1)
                return ps[b]

            def mm(o, lhsT, rhs, start=True, stop=True, done=None, **kw):
                ins = nc.tensor.matmul(o, lhsT, rhs, start=start, stop=stop, **kw)
                note(ins, done)

            def note(ins, done):
                if done is not None:
                    ins.then_inc(bank_ready[job[done][0]], 1)
                elif state["pending"] is not None:
                    ins.then_inc(*state["pending"])
                    state["pending"] = None

            def release():
                if state["held"]:
                    free = w_used if state["tile"] in split_at else w_free
                    more = 0
                    if state["pending"] is not None:
                        assert state["pending"][0] is free
                        more = state["pending"][1]
                    state["pending"] = (free, state["held"] + more)
                    state["held"] = 0

            def tile(stage, n):
                t = first[stage] + n
                if t != state["tile"]:
                    if state["tile"] is not None:
                        assert t == state["tile"] + 1, (stage, n, state)
                        release()
                    if t in split_at:
                        pe.wait_ge(w_split, split_at[t] + 1)
                    else:
                        pe.wait_ge(w_ready[t % RING], 16 * (t // RING + 1))
                    state["tile"], state["held"] = t, 1
                if t in split_at:
                    return w_hi[:, split_at[t] % SPLIT_RING, :], w_lo[:, split_at[t] % SPLIT_RING, :]
                return ring[:, t % RING, :]

            def hold(stage, n0, n):
                ws = [tile(stage, n0)]
                for q in range(1, n):
                    t = first[stage] + n0 + q
                    if q < n - 1:
                        pe.wait_ge(w_ready[t % RING], 16 * (t // RING + 1))
                    ws.append(ring[:, t % RING, :])
                state["tile"], state["held"] = first[stage] + n0 + n - 1, n
                return ws

            def held_last():
                pe.wait_ge(w_ready[state["tile"] % RING], 16 * (state["tile"] // RING + 1))

            def split_sum(o, a, b_, start, stop, done=None, **kw):
                for n, (l, r) in enumerate(((a[0], b_[1]), (a[1], b_[0]), (a[0], b_[0]))):
                    ins = nc.tensor.matmul(o, l, r, start=start and n == 0, stop=stop and n == 2, **kw)
                    if n == 2 and done is not None:
                        ins.then_inc(done, 1)
                    elif n == 0:
                        note(ins, None)

            def split_product(o, w, blk, x_hi, x_lo, start, stop, done=None, **kw):
                cs = slice(blk * P, (blk + 1) * P)
                split_sum(o, (w[0][:, cs], w[1][:, cs]), (x_hi, x_lo), start, stop, done, **kw)

            def split_linear(name, stage, n0, nk, x, o, each=None):
                for k in range(nk):
                    if each is not None:
                        pe.wait_ge(each[0], each[1] + k + 1)
                    w = tile(stage, (n0 + k) // BLOCKS)
                    split_product(o, w, (n0 + k) % BLOCKS, x[0][:, k, :],
                                  x[1][k] if isinstance(x[1], list) else x[1][:, k, :], k == 0, k == nk - 1,
                                  bank_ready[job[name][0]] if k == nk - 1 else None)

            def transpose(o, i, ident, done=None):
                note(nc.tensor.transpose(o, i, ident), done)

            ident = c_("ident")

            def attention(st, specs, before, ukv=None):
                for item in att_order(st, len(specs)):
                    if item[0] == "kT":
                        h = item[1]
                        b = open_(item)
                        for k in range(2):
                            mm(b[0:64, :], ukv[2 + k][:, h * 64:h * 64 + 64],
                               ckv1[:, k, :], k == 0, k == 1, item if k == 1 else None)
                        if h == 15:
                            release()
                        continue
                    _, what, i = item
                    s = specs[i]
                    b = open_(item)
                    nk = s["nk"]
                    if what == "S":
                        before(i)
                        mm(b[:, 0:nk], s["q"], s["k"], done=item)
                    elif what == "T":
                        pe.wait_ge(sem("att_probs"), before_[st] + i + 1)
                        Pb = att1_P if st == "att1" else att2_P
                        for t in range(nk // P):
                            transpose(b[:, t * P:(t + 1) * P], Pb[:, i % NP, t * P:(t + 1) * P], ident,
                                      item if t == nk // P - 1 else None)
                    else:
                        evacuated(pe, (st, "T", i))
                        PT = att1_PT if st == "att1" else att2_PT
                        r0 = 64 * (s["o"].start_partition() // 64)
                        for t in range(nk // P):
                            mm(b[r0:r0 + 64, 0:P], s["v"][t], PT[:, i % NP, t, :], t == 0, t == nk // P - 1,
                               item if t == nk // P - 1 else None)

            def norm_sums(which, n):
                z, sq = ln_bufs(n)
                release()
                for what, src in (("mean", z), ("var", sq)):
                    b = open_((what, which))
                    for k in range(KC):
                        pe.wait_ge(sem(f"{what}_in"), nth(which) + k + 1)
                        mm(b[:, 0:n], c_("ones"), src[:, k, :], k == 0, k == KC - 1,
                           (what, which) if k == KC - 1 else None)

            for n, name in enumerate(IN_BLOCKS):
                if n == 11:
                    pe.wait_ge(sem("params_in"), 16)
                    pe.wait_ge(sem("consts_in"), 16)
                    b = open_("ckvms")
                    pe.wait_ge(sem("ckv_sq"), 1)
                    mm(b[:, 0:S], c_("blockones"), rel[:, 0, 0, :], done="ckvms")
                if n == 16:
                    b = open_("vb")
                    pe.wait_ge(sem("ckv_normed"), 1)
                    for t in range(2):
                        mm(b[:, t * 256:(t + 1) * 256], F["ckv"][0:64, 0, t * P:(t + 1) * P], p_("w_uv")[0:64, :],
                           done="vb" if t else None)
                if name == "iw":
                    b = open_(("in", n))
                    w = tile("in", n)
                    for t in range(2):
                        ts = slice(t * P, (t + 1) * P)
                        for k in range(KC):
                            cs = slice(k * P, k * P + 8)
                            split_sum(b[:, t * 8:(t + 1) * 8], (x_hi[:, k, ts], x_lo[k][:, ts]), (w[0][:, cs], w[1][:, cs]),
                                      k == 0, k == KC - 1,
                                      bank_ready[job[("in", n)][0]] if t == 1 and k == KC - 1 else None)
                elif name in ("cv0", "av0"):
                    bs = [open_(("in", n + t)) for t in range(2)]
                    for k in range(KC):
                        w = tile("in", n + k // 4)
                        cs = slice((k % 4) * S, (k % 4 + 1) * S)
                        for t in range(2):
                            ts = slice(t * P, (t + 1) * P)
                            split_sum(bs[t][:, 0:S], (x_hi[:, k, ts], x_lo[k][:, ts]), (w[0][:, cs], w[1][:, cs]),
                                      k == 0, k == KC - 1, bank_ready[job[("in", n + t)][0]] if k == KC - 1 else None)
                elif name not in ("cv1", "av1"):
                    split_linear(("in", n), "in", n * KC, KC, (x_hi, x_lo), open_(("in", n))[:, 0:S],
                                 None if n else (sem("x_in_split"), 0))
            b = open_("t5")
            mm(b[0:8, :], p_("rpb_rows")[0:34, :], c_("buckets")[0:34, :], done="t5")
            for i in range(2):
                for q in range(4):
                    b = open_(("ix", i, q))
                    r = slice(32 * q, 32 * q + 32)
                    for m in range(2):
                        mm(b[:, m * S:(m + 1) * S], F["iq"][r, m, i * P:(i + 1) * P], F["ik"][r, 0, :],
                           done=("ix", i, q) if m else None)
            pe.wait_ge(sem("cond_split"), 1)
            for l in range(2):
                for g in range(ADA // 1024):
                    bs = [open_(("ada", l, g, q)) for q in range(2)]
                    for k in range(KC):
                        w = tile(f"ada{l}", g * KC + k)
                        for q in range(2):
                            cs = slice(q * 512, (q + 1) * 512)
                            mm(bs[q], cond_st[:, k, :], w[1][:, cs], k == 0, False)
                            mm(bs[q], cond_st[:, k, :], w[0][:, cs], False, k == KC - 1,
                               ("ada", l, g, q) if k == KC - 1 else None)
            pe.wait_ge(sem("small_act"), 4)
            for name, r0, k in (("dw", R_W, 16), ("da", R_A, 16), ("dg", R_G, 32)):
                b = open_(name)
                for m in range(2):
                    mm(b[:, m * S:(m + 1) * S], p_("lora")[r0:r0 + k, m * P:(m + 1) * P], small_act[r0:r0 + k, :],
                       done=name if m else None)
            b = open_("ca")
            mm(b[:, 0:S], p_("lora")[R_C:R_C + 16, 0:P], small_act[R_C:R_C + 16, :], done="ca",
               tile_position=(96, 0))
            for i in (24, 25):
                evacuated(pe, ("in", i))
            evacuated(pe, "vb")
            attention("att1", att1, lambda i: None)
            b = open_("ckd")
            pe.wait_ge(sem("c_feat"), 1)
            for t in range(2):
                transpose(b[:, t * P:(t + 1) * P], C["kd"][:, t * P:(t + 1) * P], ident, "ckd" if t else None)
            for h in range(4):
                b = open_(("catt", h))
                r = slice(32 * h, 32 * h + 32)
                for c in range(NCH):
                    o = b[64 * (c % 2):64 * (c % 2) + 64, (c // 2) * CH:(c // 2 + 1) * CH]
                    mm(o, C["ki"][r, c * CH:(c + 1) * CH], C["qd"][r, c * CH:(c + 1) * CH],
                       done=("catt", h) if c == NCH - 1 else None, tile_position=(32 * h, 64 * (c % 2)))
            evacuated(pe, "ckd")
            for c in range(3):
                b = open_(("cupd", c))
                r = slice(64 * (c % 2), 64 * (c % 2) + 64)
                mm(b[:, 0:S], c_kdt[r, c // 2, :], cv[r, c // 2, :], done=("cupd", c))
            for h in range(4):
                evacuated(pe, ("catt", h))
            pe.wait_ge(sem("c_states"), 3)
            for hp in range(2):
                for par_ in range(2):
                    b = open_(("co", hp, par_))
                    r = slice(64 * par_, 64 * par_ + 64)
                    for n in range(2):
                        c = 2 * n + par_
                        for q in range(2):
                            h = 2 * hp + q
                            mm(b[64 * q:64 * q + 64, n * CH:(n + 1) * CH], cv[r, n, h * 64:(h + 1) * 64],
                               c_att[r, h, n, :], True, c == 0, skip_group_check=True)
                        if c:
                            mm(b[:, n * CH:(n + 1) * CH], c_sm[:, c - 1, hp * P:(hp + 1) * P],
                               C["qd"][:, c * CH:(c + 1) * CH], False, True, ("co", hp, par_) if n else None,
                               skip_group_check=True)
            b = open_("coms")
            pe.wait_ge(sem("c_sq"), 1)
            mm(b, c_("blockones"), c_sq.rearrange("p a b -> p (a b)"), done="coms")
            b = open_("kkn")
            pe.wait_ge(sem("d_kk_sq"), 1)
            mm(b, c_("blockones"), DD["t"].rearrange("p a b -> p (a b)"), done="kkn")
            pe.wait_ge(sem("d_feat"), 1)

            def family(name, f):
                for p in range(2):
                    b = open_((name, p))
                    r = slice(64 * p, 64 * p + 64)
                    for u in range(8):
                        lhsT, rhs = f(r, u)
                        mm(b[r, u * CH:(u + 1) * CH], lhsT, rhs, done=(name, p) if u == 7 else None)

            def tok(x):
                return lambda r, u: x[r, u // NCH, (u % NCH) * CH:(u % NCH + 1) * CH]

            def unit(x):
                return lambda r, u: U[x][r, u, :]

            def pair(a, b2):
                return lambda r, u: (a(r, u), b2(r, u))

            eye = lambda r, u: ident[r, r.start:r.start + 64]
            family("N", pair(tok(DD["Bh"]), tok(Ah)))
            family("A", pair(tok(Ah), tok(DD["Bh"])))
            family("GRB", pair(tok(DD["Bh"]), tok(Rh)))
            family("GAK", pair(tok(DD["Kh"]), tok(Ah)))
            family("GRK", pair(tok(DD["Kh"]), tok(Rh)))
            family("Vt", pair(lambda r, u: dS[r, 5 + u // NCH, (u % NCH) * CH:(u % NCH + 1) * CH], eye))
            family("Bt", pair(tok(DD["Bh"]), eye))
            family("Kt", pair(tok(DD["Kh"]), eye))
            pe.wait_ge(sem("d_split"), 5)
            steps = [("D2", "Dt", "D"), ("D2t", "D", "Dt"), ("Z1", "D2t", "Z"), ("W1", "D2", "W"),
                     ("D4", "D2t", "D2"), ("D4t", "D2", "D2t"), ("Z2", "D4t", "Z"), ("W2", "D4", "W"),
                     ("D8", "D4t", "D4"), ("D8t", "D4", "D4t"), ("Z3", "D8t", "Z"), ("W3", "D8", "W"),
                     ("Pm", "W", "Lo"), ("Pt", "Lo", "W"), ("P2t", "Pm", "Pt"), ("Y1", "P2t", "Z"), ("T", "Pt", "Y1")]
            wrote = {"D": None, "Dt": None, "Z": None, "W": None, "Lo": None}
            for name, l, r_ in steps:
                for src in (l, r_):
                    if wrote.get(src):
                        for p in range(2):
                            evacuated(pe, (wrote[src], p))
                family(name, pair(unit(l), unit(r_)))
                wrote[{"Z1": "Z", "Z2": "Z", "Z3": "Z", "W1": "W", "W2": "W", "W3": "W"}.get(name, name)] = name
            for p in range(2):
                evacuated(pe, ("T", p))
            for c in range(NCH):
                def per_pair(what, terms):
                    for p in range(2):
                        b = open_((what, c, p))
                        r = slice(64 * p, 64 * p + 64)
                        for m in range(2):
                            ts = terms(r, m)
                            for n, (l, r_) in enumerate(ts):
                                mm(b[r, m * CH:(m + 1) * CH], l, r_, n == 0, n == len(ts) - 1,
                                   (what, c, p) if m == 1 and n == len(ts) - 1 else None)
                cs = slice(c * CH, (c + 1) * CH)
                if c:
                    pe.wait_ge(sem("d_state"), 2 * c)
                per_pair("X", lambda r, m: ([(Ah[r, m, cs], m_st[r, c, m, :])] if c else [])
                         + [(U["GAK"][r, 4 * m + c, :], U["Vt"][r, 4 * m + c, :])])
                for p in range(2):
                    evacuated(pe, ("X", c, p))
                per_pair("U", lambda r, m: [(U["T"][r, 4 * m + c, :], x_u[r, 0, m, :])])
                for p in range(2):
                    evacuated(pe, ("U", c, p))
                per_pair("Yc", lambda r, m: ([(m_st[r, c, m, :], Rh[r, m, cs])] if c else [])
                         + [(x_u[r, 1, m, :], U["GRB"][r, 4 * m + c, :]), (U["Vt"][r, 4 * m + c, :], U["GRK"][r, 4 * m + c, :])])
                if c < NCH - 1:
                    per_pair("M", lambda r, m: [(U["Bt"][r, 4 * m + c, :], x_u[r, 1, m, :]),
                                                (U["Kt"][r, 4 * m + c, :], U["Vt"][r, 4 * m + c, :])])
            for name, src, s_ in (("bonus", bn, "d_bonus_in"), ("ymean", yT, "d_y"), ("yvar", DD["t"], "d_ysq")):
                b = open_(name)
                pe.wait_ge(sem(s_), 1)
                mm(b, c_("blockones"), src.rearrange("p a b -> p (a b)"), done=name)
            for l in range(2):
                b = open_(("adaT", l))
                pe.wait_ge(sem(f"ada_mat{l}"), 32)
                mm(b[:, 0:96], ada_mat_lo[0:96, l, :], ident[0:96, 0:96], True, False)
                mm(b[:, 0:96], ada_mat[0:96, l, :], ident[0:96, 0:96], False, True, ("adaT", l))
            for m in range(KC):
                for half in range(2):
                    b = open_(("gt", m, half))
                    for n in (2 * half, 2 * half + 1):
                        w = tile("merge", m * 5 + n)
                        for k in range(KC):
                            split_product(b[:, (n % 2) * S:(n % 2 + 1) * S], w, k, x_hi[:, k, :], x_lo[k], k == 0,
                                          k == KC - 1,
                                          bank_ready[job[("gt", m, half)][0]] if n % 2 and k == KC - 1 else None)
                for half in range(2):
                    b = open_(("br", m, half))
                    w = tile("merge", m * 5 + 4)
                    for n in (2 * half, 2 * half + 1):
                        if m == 0:
                            pe.wait_ge(sem("ys_split"), n + 1)
                        for k in range(2):
                            split_product(b[:, (n % 2) * S:(n % 2 + 1) * S], w, n * 2 + k, ys_hi[:, n, k, :],
                                          ys_lo[:, n, k, :], k == 0, k == 1,
                                          bank_ready[job[("br", m, half)][0]] if n % 2 and k == 1 else None)
            for m in range(KC):
                b = open_(("out1", m))
                split_linear(("out1", m), "out", m * KC, KC, (mg_hi, mg_lo), b[:, 0:S],
                             None if m else (sem("merged_split"), 0))
            norm_sums("a", S)
            pe.wait_ge(sem("ln_out"), KC)
            router = p_("router").rearrange("p (k n) -> p k n", k=KC)
            for t in range(2):
                b = open_(("rt", t))
                for k in range(KC):
                    mm(b[:, 0:36], X1[:, k, t * P:(t + 1) * P], router[:, k, :], k == 0, k == KC - 1,
                       ("rt", t) if k == KC - 1 else None)
            release()
            pe.wait_ge(sem("x_split"), KC)

            def split_tile(n, r=None, last=False):
                i = split0 + n
                pe.wait_ge(w_split, i + 1 if r is None else r * 12 + (i + 1))
                state["pending"] = (w_used, 1)
                return w_hi[:, i % SPLIT_RING, :], w_lo[:, i % SPLIT_RING, :]

            def hidden(e_par, base, r=None):
                for part in range(2):
                    b = ps[2 * e_par + part]
                    for m in range(2):
                        n = base + 2 * part + m
                        w = split_tile(n, r)
                        if n == 0:
                            state["pending"] = None
                        for k in range(KC):
                            split_product(b[:, m * S:(m + 1) * S], w, k, mx_hi[:, k, :], mx_lo[:, k, :],
                                          k == 0, k == KC - 1,
                                          sem("moe_gate" if part == 0 else "moe_up") if m == 1 and k == KC - 1 else None)

            def down(e_par, base, r=None, last=False):
                for k in range(2):
                    w = split_tile(base + k, r)
                    for m in range(KC):
                        split_product(ps[4 + m // 2][:, (m % 2) * S:(m % 2 + 1) * S], w, m, mh_hi[:, e_par, k, :],
                                      mh_lo[:, e_par, k, :], False, last and k == 1 and m % 2 == 1,
                                      sem("moe_down") if k == 1 and m == KC - 1 else None, skip_group_check=True)

            assert job["gateT"][0] >= 4 and len({job[("rt", t)][0] for t in range(2)} & {0, 1}) == 0
            for bb in range(2):
                pe.wait_ge(bank_free[bb], moe_uses[bb])
            hidden(0, 0)
            b = open_("gateT")
            for t in range(2):
                pe.wait_ge(sem("gate_ready"), t + 1)
                transpose(b[0:EXPERTS, t * P:(t + 1) * P], rt[:, t, 11, :], ident, "gateT" if t else None)
            for bb in range(2, NBANK):
                pe.wait_ge(bank_free[bb], moe_uses[bb])
            for bb in range(4):
                mm(ps[4 + bb][:, :], c_("zeros"), con[:, 0:512], True, False, skip_group_check=True)
            with pe.Fori(0, (EXPERTS - 2) // 2) as r:
                for s in range(2):
                    hidden((1 + s) % 2, 4 + 6 * s, r)
                    pe.wait_ge(sem("moe_hidden"), r * 2 + (s + 1))
                    down(s % 2, 8 + 6 * s, r)
            end = 4 + 6 * (EXPERTS - 2)
            hidden(1, end)
            pe.wait_ge(sem("moe_hidden"), EXPERTS - 1)
            down(0, end + 4)
            pe.wait_ge(sem("moe_hidden"), EXPERTS)
            down(1, end + 6, last=True)
            state["tile"], state["held"] = first["moe"] + stage_tiles["moe"] - 1, 1
            pe.wait_ge(sem("z_written"), KC)
            norm_sums("b", S)
            x = in_split(512)
            for kind, n in L0_ORDER:
                if kind == "l0vals":
                    continue
                if kind == "qms":
                    b = open_(("qms", n))
                    pe.wait_ge(sem("q0_sq"), n + 1)
                    mm(b, c_("blockones"), tq2[:, n, :], done=("qms", n))
                elif kind == "rope0":
                    b = open_(("rope0", n))
                    pe.wait_ge(sem("q0_normed"), n + 1)
                    mm(b[:, 0:S], c_("rot"), Q0[:, n, 0:S], done=("rope0", n))
                elif n == 5:
                    b = open_(("l0in", n))
                    w = tile("l0in", n)
                    for t in range(4):
                        ts = slice(t * P, (t + 1) * P)
                        for k in range(KC):
                            cs = slice(k * P, (k + 1) * P)
                            last = t == 3 and k == KC - 1
                            split_sum(b[:, ts], (x[0][:, k, ts], x[1][:, k, ts]), (w[0][:, cs], w[1][:, cs]),
                                      k == 0, k == KC - 1, bank_ready[job[("l0in", n)][0]] if last else None)
                else:
                    split_linear(("l0in", n), "l0in", n * KC, KC, x, open_(("l0in", n)),
                                 None if n else (sem("h_split"), 0))
            bs = [open_(("l0vals", t)) for t in range(4)]
            for k in range(KC):
                w = tile("l0in", 14 + k // 2)
                cs = slice((k % 2) * 512, (k % 2 + 1) * 512)
                for t in range(4):
                    ts = slice(t * P, (t + 1) * P)
                    split_sum(bs[t], (x[0][:, k, ts], x[1][:, k, ts]), (w[0][:, cs], w[1][:, cs]), k == 0,
                              k == KC - 1, bank_ready[job[("l0vals", t)][0]] if k == KC - 1 else None)
            pe.wait_ge(sem("q0_roped"), 5)
            for t in range(4):
                evacuated(pe, ("l0vals", t))
            for n in range(13, 5, -1):
                evacuated(pe, ("l0in", n))
            evacuated(pe, ("l0in", 5))
            attention("att2", att2, lambda i: None)
            for m in range(KC):
                b = open_(("l0out", m))
                split_linear(("l0out", m), "l0out", m * KC, KC, (y0_hi, y0_lo), b, None if m else (sem("y_split"), 0))
            norm_sums("c", 512)

            def ffn(l, n):
                x = in_split(n)
                u = [u_hi[:, :, 0:n], u_lo[:, :, 0:n]]
                for half, part in enumerate("AB"):
                    chunks = range(UP_A) if half == 0 else range(UP_A, FF)
                    for j in chunks:
                        for q, nm in enumerate((f"l{l}g", f"l{l}v")):
                            b = open_((nm, j))
                            split_linear((nm, j), f"l{l}up{part}", (j - chunks[0]) * 16 + q * KC, KC, x, b[:, 0:n],
                                         None if j or q else (sem("h_split"), KC * (2 * l + 1)))
                    pe.wait_ge(sem("ff_split"), l * FF + (half + 1) * HF)
                    for m in range(KC):
                        b = open_((f"l{l}down", half, m))
                        split_linear((f"l{l}down", half, m), f"l{l}down{part}", m * HF, HF, u, b[:, 0:n])

            ffn(0, 512)
            norm_sums("d", 512)
            x = in_split(512)
            for n in range(9):
                b = open_(("l1in", n))
                w = 512 if n < 3 else S
                split_linear(("l1in", n), "l1in", n * KC, KC, [q[:, :, 0:w] for q in x], b[:, 0:w],
                             None if n else (sem("h_split"), 2 * KC))
            b = open_("cqms")
            pe.wait_ge(sem("cq_sq"), 1)
            for k in range(6):
                mm(b[:, 0:S], c_("ones"), sq1[:, k, 0:S], k == 0, k == 5, "cqms" if k == 5 else None)
            b = open_("ckvms1")
            for k in range(2):
                mm(b, c_("ones"), sq1[:, 6 + k, :], k == 0, k == 1, "ckvms1" if k == 1 else None)
            b = open_("krope")
            evacuated(pe, ("l1in", 2))
            mm(b[64:96, 0:S], c_("rot")[64:96, 64:96], kr1[64:96, 0:S], done="krope")
            for m in range(8):
                b = open_(("uq", m))
                for q in range(2):
                    for k in range(6):
                        n = (2 * m + q) * 6 + k
                        if n < 6:
                            pe.wait_ge(sem("cq_split"), k + 1)
                        split_product(b[:, q * S:(q + 1) * S], tile("l1uq", n // BLOCKS), n % BLOCKS, cq_hi[:, k, :],
                                      cq_lo[:, k, :], k == 0, k == 5,
                                      bank_ready[job[("uq", m)][0]] if q and k == 5 else None)
            for m in range(8):
                b = open_(("qrope", m))
                evacuated(pe, ("uq", m))
                mm(b[0:96, :], c_("rot")[0:96, 0:96], q1[0:96, 2 * m:2 * m + 2, :].rearrange("p a b -> p (a b)"),
                   done=("qrope", m))
            pe.wait_ge(sem("ckv_normed1"), 2)
            ukv = hold("l1ukv", 0, 4)
            for hf in range(2):
                for t in range(4):
                    b = open_(("v1", t, hf))
                    for k in range(2):
                        mm(b, ckv1[:, k, t * P:(t + 1) * P],
                           ukv[k][:, hf * 512:(hf + 1) * 512], k == 0, k == 1,
                           ("v1", t, hf) if k else None)
            pe.wait_ge(sem("q1_roped"), 8)
            pe.wait_ge(sem("kr_placed"), 2)

            def before3(i):
                evacuated(pe, ("kT", i // 2))

            for hf in range(2):
                for t in range(4):
                    evacuated(pe, ("v1", t, hf))
            held_last()
            attention("att3", att3, before3, ukv)
            for m in range(KC):
                b = open_(("l1out", m))
                split_linear(("l1out", m), "l1out", m * KC, KC, (y1_hi, y1_lo), b[:, 0:S],
                             None if m else (sem("y_split"), KC))
            norm_sums("e", S)
            ffn(1, S)
            norm_sums("f", S)

        @block.scalar
        def _(act):
            seq = [0]
            chain = sem("act_seq")

            def step(ins, name=None):
                if name is None:
                    seq[0] += 1
                    ins.then_inc(chain, 1)
                    act.wait_ge(chain, seq[0])
                else:
                    counts[name] = counts.get(name, 0) + 1
                    ins.then_inc(sem(name), 1)
                    act.wait_ge(sem(name), counts[name])

            counts = {}

            def tell(ins, name):
                counts[name] = counts.get(name, 0) + 1
                ins.then_inc(sem(name), 1)

            f = nc.scalar.activation
            fed = [0]

            def feed(stage, n):
                t = first[stage] + n
                end = split_at[min(t + SPLIT_RING, run_end(t + 1 if t >= 0 else 1)) - 1] + 1
                for i in range(fed[0], end):
                    t = split_order[i]
                    act.wait_ge(w_ready[t % RING], 16 * (t // RING + 1))
                    if i >= SPLIT_RING:
                        act.wait_ge(w_used, i - SPLIT_RING + 1)
                    f(w_hi[:, i % SPLIT_RING, :], ring[:, t % RING, :], ACT.Copy).then_inc(w_high, 1)
                fed[0] = max(fed[0], end)

            def attention(st, specs, Pb, PT, L):
                n = len(specs)
                for i in range(n + NP):
                    if i < n:
                        s = specs[i]
                        nk = s["nk"]
                        act.wait_ge(sem("att_negmax"), before_[st] + i + 1)
                        if i >= NP:
                            b, use = job[(st, "T", i - NP)]
                            act.wait_ge(bank_ready[b], use)
                        den = SV[:, 8 + i % 4:9 + i % 4]
                        nm = SV[:, i % 4:i % 4 + 1]
                        if s["bias"] is not None:
                            tell(f(Pb[:, i % NP, 0:nk], L[:, i % 3, 0:nk], ACT.Exp, bias=nm, accum_out=den), "att_exp")
                        else:
                            ins = f(Pb[:, i % NP, 0:nk], bank(act, (st, "S", i))[:, 0:nk], ACT.Exp, bias=nm,
                                    accum_out=den)
                            frees(ins, (st, "S", i))
                    j = i - NP + 1
                    if 0 <= j < n:
                        nk = specs[j]["nk"]
                        if j >= NP:
                            b, use = job[(st, "O", j - NP)]
                            act.wait_ge(bank_ready[b], use)
                        b = bank(act, (st, "T", j))
                        frees(f(PT[:, j % NP, 0:nk // P, :], b[:, 0:nk].rearrange("p (a b) -> p a b", b=P), ACT.Copy),
                              (st, "T", j))

            def layer_norm(which, n, gname, bname, dst, then=None):
                z, sq = ln_bufs(n)
                for k in range(KC):
                    act.wait_ge(sem("centred"), nth(which) + k + 1)
                    tell(f(sq[:, k, :], z[:, k, :], ACT.Square), "var_in")
                act.wait_ge(sem("var_eps"), nth(which) // KC + 1)
                tell(f(lnst[:, 2, 0:n], lnst[:, 1, 0:n], ACT.Sqrt), "ln_std")
                for k in range(KC):
                    act.wait_ge(sem("scaled"), nth(which) + k + 1)
                    tell(f(dst(k), z[:, k, :], ACT.Identity, bias=p_(bname)[:, k:k + 1], scale=p_(gname)[:, k:k + 1]),
                         "ln_out")
                    if then is not None and k >= 2:
                        then(k - 2)
                if then is not None:
                    then(KC - 2)
                    then(KC - 1)

            def h_high(n, which):
                z, _ = ln_bufs(n)

                def chunk(k):
                    act.wait_ge(sem("h_raw"), KC * which + k + 1)
                    tell(f(in_split(n)[0][:, k, :], z[:, k, :], ACT.Copy), "h_high")

                return chunk

            act.dma_start(X1, xin.rearrange("k p t -> p k t")).then_inc(sem("x_in"), 16)
            dst = {"ik": F["ik"][:, 0, :], "ckv": F["ckv"][:, 0, :], "cq": F["cq"][:, 0, :], "ck": F["ck"][:, 0, :],
                   "small": dF[:, 0, 1:]}
            for m in range(2):
                for nm in ("iq", "bq", "cg", "aq", "ak"):
                    dst[f"{nm}{m}"] = F[nm][:, m, :]
                for q, nm in enumerate(("dr", "dk", "dv")):
                    dst[f"{nm}{m}"] = dF[:, 1 + 2 * q + m, 1:]
            for k in range(KC):
                if k == 0:
                    act.wait_ge(sem("x_in"), 16)
                tell(f(x_hi[:, k, :], X1[:, k, :], ACT.Copy), "x_in_high")
                if k < 3:
                    feed("in", k - 2)
            act.wait_ge(w_ready[3], 16)
            act.dma_start(par[:, :], params).then_inc(sem("params_in"), 16)
            act.dma_start(con[:, :], consts).then_inc(sem("consts_in"), 16)
            for n, name in enumerate(IN_BLOCKS):
                if n == 8:
                    act.wait_ge(sem("params_in"), 16)
                    tell(f(p_("cond"), p_("cond"), ACT.Silu), "cond_silu")
                    act.wait_ge(sem("cond_silu"), 1)
                    act.wait_ge(sem("cond_zero"), 1)
                    tell(f(cond_st[:, :, 0:2], p_("cond").rearrange("p (k s) -> p k s", k=KC), ACT.Copy), "cond_high")
                if n == 12:
                    act.wait_ge(sem("ckv_ms"), 1)
                    tell(f(rel[:, 0, 1, :], rel[:, 0, 0, :], ACT.Sqrt), "ckv_rms")
                if n == 17:
                    frees(f(vb, bank(act, "vb").rearrange("p (a b) -> p a b", a=2), ACT.Copy), "vb")
                feed("in", n)
                b = bank(act, ("in", n))
                if name == "iw":
                    o, src = iw[:, :, :], b[:, 0:16].rearrange("p (a b) -> p a b", a=2)
                elif name[:2] in ("cv", "av"):
                    o, src = (cv if name[0] == "c" else av)[:, int(name[2]), :], b[:, 0:S]
                else:
                    o, src = dst[name], b[:, 0:S]
                scale = HEAD_SCALE if name[:2] in ("aq", "bq") else 1.0
                frees(f(o, src, ACT.Silu if name[:2] == "cg" else ACT.Copy, scale=scale), ("in", n))
            for i in range(2):
                for q in range(4):
                    n = 4 * i + q
                    if n >= 2:
                        act.wait_ge(sem("rel_used"), n - 1)
                    else:
                        act.wait_ge(sem("ckv_normed"), 1)
                    b = bank(act, ("ix", i, q))
                    frees(f(rel[:, n % 2, :, :], b.rearrange("p (a b) -> p a b", a=2), ACT.Relu, scale=32 ** -0.5),
                          ("ix", i, q))
            act.wait_ge(sem("d_shifted"), 7)
            for r0, fn in ((R_W, ACT.Tanh), (R_A, ACT.Copy), (R_G, ACT.Sigmoid), (R_C, ACT.Copy)):
                tell(f(small_act[r0:r0 + 32, :], dS[r0:r0 + 32, 0, :], fn), "small_act")
            def ada_rows_out(t):
                for q in range(2):
                    name = ("ada", t // (ADA // 1024), t % (ADA // 1024), q)
                    n = 2 * t + q
                    if n >= 4:
                        act.wait_ge(sem(f"ada_row_stored{n % 4}"), 16 * (n // 4))
                    frees(f(ada_rows[0:4, n % 4, :], bank(act, name)[0:4, :], ACT.Copy), name)

            for t in range(2 * (ADA // 1024)):
                feed("ada0", t * KC + 3)
                if t:
                    ada_rows_out(t - 1)
                feed("ada0", t * KC + KC - 1)
            ada_rows_out(2 * (ADA // 1024) - 1)
            for name in ("dw", "da"):
                b = bank(act, name)
                for m in range(2):
                    ins = f(DZ[name[1]][:, m, :], b[:, m * S:(m + 1) * S], ACT.Sigmoid,
                            bias=p_("d_w0" if name == "dw" else "d_a0")[:, m:m + 1])
                    if m:
                        frees(ins, name)
            frees(f(DZ["g"], bank(act, "dg").rearrange("p (a b) -> p a b", a=2), ACT.Copy), "dg")
            frees(f(c_z, bank(act, "ca")[:, 0:S], ACT.Copy), "ca")
            attention("att1", att1, att1_P, att1_PT, att1_L)
            act.wait_ge(sem("c_zb"), 1)
            step(f(C["ab"], C["zb"], ACT.Abs))
            step(f(C["ab"], C["ab"], ACT.Exp, scale=-1.0))
            tell(f(C["ln"], C["ab"], ACT.Ln, bias=1.0), "c_softplus")
            act.wait_ge(sem("c_cum"), 1)
            f(C["ec"], C["cum"], ACT.Exp)
            f(C["en"], C["cum"], ACT.Exp, scale=-1.0)
            for c in range(NCH):
                ins = f(C["ed"][:, c * CH:(c + 1) * CH], C["cum"][:, c * CH:(c + 1) * CH], ACT.Exp, scale=-1.0,
                        bias=C["cum"][:, c * CH + CH - 1:c * CH + CH])
            tell(ins, "c_exps")
            frees(f(c_kdt, bank(act, "ckd")[:, 0:S].rearrange("p (a b) -> p a b", a=2), ACT.Copy), "ckd")
            for hp in range(2):
                for q in range(2):
                    o = c_o[:, hp, :].rearrange("p (n q t) -> p n q t", n=2, q=2)[:, :, q, :]
                    frees(f(o, bank(act, ("co", hp, q))[:, 0:P].rearrange("p (a b) -> p a b", a=2), ACT.Copy),
                          ("co", hp, q))
            for hp in range(2):
                for q in range(2):
                    evacuated(act, ("co", hp, q))
            tell(f(c_sq, c_o, ACT.Square), "c_sq")
            act.wait_ge(sem("c_ms"), 1)
            tell(f(c_sq, c_sq, ACT.Sqrt), "c_rms")
            act.wait_ge(sem("d_kk"), 1)
            tell(f(DD["t"], DD["kk"], ACT.Square), "d_kk_sq")
            tell(f(DD["e1"], bank(act, "kkn").rearrange("p (a b) -> p a b", a=2), ACT.Sqrt), "d_kk_norm")
            act.wait_ge(sem("d_cum"), 1)
            act.wait_ge(sem("d_kk_unit"), 1)
            f(DD["e1"], DD["cm1"], ACT.Exp)
            f(DD["e2"], DD["cum"], ACT.Exp)
            tell(f(DD["e3"], DD["cum"], ACT.Exp, scale=-1.0), "d_exps")
            for fam in ("Vt", "Bt", "Kt"):
                for p in range(2):
                    r = slice(64 * p, 64 * p + 64)
                    frees(f(U[fam][r, :, :], bank(act, (fam, p))[r, :].rearrange("p (a b) -> p a b", a=8), ACT.Copy),
                          (fam, p))
            for fam in FAM2:
                if fam[0] in "ZW" or fam in ("Y1", "T"):
                    continue
                p = 1
                r = slice(64, P)
                frees(f(U[fam][r, :, :], bank(act, (fam, p))[r, :].rearrange("p (a b) -> p a b", a=8), ACT.Copy),
                      (fam, p))
            for c in range(NCH):
                for what, n in (("X", 0), ("U", 1)):
                    r = slice(64, P)
                    frees(f(x_u[r, n, :, :], bank(act, (what, c, 1))[r, 0:P].rearrange("p (a b) -> p a b", a=2),
                            ACT.Copy), (what, c, 1))
            act.wait_ge(sem("d_centred"), 1)
            tell(f(DD["t"], yT, ACT.Square), "d_ysq")
            act.wait_ge(sem("d_var"), 1)
            tell(f(DD["e1"], DD["e1"], ACT.Sqrt), "d_std")
            for m in range(KC):
                if m >= 2:
                    act.wait_ge(sem("gates_used"), m - 1)
                for half in range(2):
                    feed("merge", m * 5 + 2 * half + 1)
                    frees(f(gates[:, m % 2, 2 * half:2 * half + 2, :],
                            bank(act, ("gt", m, half)).rearrange("p (a b) -> p a b", a=2), ACT.Sigmoid), ("gt", m, half))
                if m == 0:
                    act.wait_ge(sem("ys_ready"), 4)
                    for n in range(4):
                        tell(f(ys_hi[:, n, :, :], ysT[:, n, :, :], ACT.Copy), "ys_high")
                else:
                    act.wait_ge(sem("merged"), m)
                    tell(f(mg_hi[:, m - 1, :], mergedT[:, m - 1, :], ACT.Copy), "merged_high")
            feed("out", 0)
            act.wait_ge(sem("merged"), KC)
            tell(f(mg_hi[:, KC - 1, :], mergedT[:, KC - 1, :], ACT.Copy), "merged_high")
            for m in range(KC):
                feed("out", m)
            layer_norm("a", S, "ln1g", "ln1b", lambda k: X1[:, k, :])
            feed("moe", 0)
            for k in range(KC):
                act.wait_ge(sem("ln_out"), k + 1)
                tell(f(mx_hi[:, k, :], X1[:, k, :], ACT.Copy), "x_high")
            def highs(c, n, r=None):
                for i in range(c, c + n):
                    need = 16 * ((moe0 + i) // RING + 1)
                    act.wait_ge(w_ready[(moe0 + i) % RING], need if r is None else r * (16 * 12 // RING) + need)
                    q = split0 + i
                    if q >= SPLIT_RING:
                        act.wait_ge(w_used, q - SPLIT_RING + 1 if r is None else r * 12 + (q - SPLIT_RING + 1))
                    f(w_hi[:, q % SPLIT_RING, :], ring[:, (moe0 + i) % RING, :], ACT.Copy).then_inc(w_high, 1)

            for t in range(2):
                if t:
                    highs(3, 1)
                act.wait_ge(sem("rt_neg"), t + 1)
                tell(f(rt[:, t, 0, 0:4], lg[:, t, 0:4], ACT.Exp, bias=SV[:, 16 + t:17 + t],
                       accum_out=SV[:, 20 + t:21 + t]), "rt_gexp")
                act.wait_ge(sem("rt_diff"), t + 1)
                tell(f(SV[:, 32 + t:33 + t], SV[:, 28 + t:29 + t], ACT.Exp), "rt_eexp")
            frees(f(gateT[0:EXPERTS, :], bank(act, "gateT")[0:EXPERTS, 0:S], ACT.Copy), "gateT")
            evacuated(act, "gateT")
            tell(f(SV[0:1, 40:41], gateT[0:1, 0:1], ACT.Copy), "gateT_ready")

            def silu(par_, n):
                act.wait_ge(sem("moe_gate"), n + 1)
                f(m_sg[:, par_, :, :], ps[2 * par_].rearrange("p (a b) -> p a b", a=2), ACT.Silu)\
                    .then_inc(sem("moe_silu"), 1)

            def hidden_high(par_, n):
                act.wait_ge(sem("moe_raw"), n + 1)
                if not isinstance(n, int) or n >= 2:
                    act.wait_ge(sem("moe_down"), n - 1)
                f(mh_hi[:, par_, :, :], m_t[:, par_, :, :], ACT.Copy).then_inc(sem("moe_high"), 1)

            def expert(par_, n, c, r=None, last=False):
                hidden_high(1 - par_, n - 1)
                if c > 4:
                    highs(c + 2, 2, r)
                silu(par_, n)
                highs(c + 4, 2 if last else 4, r)

            silu(0, 0)
            highs(4, 4)
            for e in (1, 2):
                expert(e % 2, e, 6 * e - 2)
            with act.Fori(0, (EXPERTS - 4) // 2) as r:
                for s in range(2):
                    expert((1 + s) % 2, r * 2 + (3 + s), 16 + 6 * s, r)
            e = EXPERTS - 1
            expert(1, e, 6 * e - 2, last=True)
            hidden_high(1, e)
            highs(6 * EXPERTS - 2, 2)
            fed[0] = split0 + 6 * EXPERTS
            feed("l0in", 0)
            layer_norm("b", S, "ln2g", "ln2b", lambda k: X1[:, k, :])
            for k in range(KC):
                h_high(512, 0)(k)
            for n in range(18):
                if n == 9:
                    for m in range(5):
                        act.wait_ge(sem("q0_ms"), m + 1)
                        tell(f(tq[:, m, :], tq[:, m, :], ACT.Sqrt, scale=HEAD_SCALE ** -2 if m < 4 else 1.0), "q0_rms")
                if n >= 14:
                    feed("l0in", 17)
                    frees(f(V0[:, n - 14, P:], bank(act, ("l0vals", n - 14))[:, :], ACT.Copy), ("l0vals", n - 14))
                    continue
                feed("l0in", n)
                b = bank(act, ("l0in", n))
                if n == 5:
                    o = V0[:, :, 0:P]
                elif n < 5:
                    o = Q0[:, n, :]
                elif n < 10:
                    o = qb[:, n - 6, :]
                else:
                    o = kb[:, n - 10, :]
                src = b.rearrange("p (a b) -> p a b", a=4) if n == 5 else b[:, :]
                frees(f(o, src, ACT.Copy, scale=HEAD_SCALE if 6 <= n < 10 else 1.0), ("l0in", n))
                if n < 5:
                    evacuated(act, ("l0in", n))
                    tell(f(tq2[:, n, :], Q0[:, n, :], ACT.Square), "q0_sq")
            attention("att2", att2, att2_P, att2_PT, att2_L)

            def y_high(st, per, y, hi):
                for k in range(KC):
                    evacuated(act, (st, "O", per * (k + 1) - 1))
                    tell(f(hi[:, k, :], y[:, k, :], ACT.Copy), "y_high")

            def gated(name, l, n, stage=None):
                for m in range(KC):
                    if stage is not None:
                        feed(stage, (m * HF + HF - 1) // BLOCKS)
                    else:
                        feed(f"l{l}out", m)
                    b = bank(act, name(m))
                    z_n = gated_n[0]
                    gated_n[0] += 1
                    if m >= 2 or stage is not None and stage[-1] == "B":
                        act.wait_ge(sem("z_written"), z_n - 1)
                    g = 16 if stage is None else 40
                    ts = lnst[:, m % 2, 0:n]
                    ins = f(ts[:, 0:S], b[:, 0:S], ACT.Copy, scale=MOD[:, l, g + m, 0:1])
                    if n > S:
                        ins = f(ts[:, S:n], b[:, S:n], ACT.Copy, scale=MOD[:, l, g + m, 1:2])
                    frees(ins, name(m))

            gated_n = [KC]

            y_high("att2", 8, yT0, y0_hi)
            gated(lambda m: ("l0out", m), 0, 512)
            feed("l0upA", 0)
            layer_norm("c", 512, "l0ln1g", "l0ln1b", lambda k: XC[:, k, :], h_high(512, 1))

            def ffn(l, n):
                ns = n // S
                def hidden_high(j):
                    act.wait_ge(sem("ff_raw"), l * FF + j + 1)
                    tell(f(u_hi[:, j % HF, 0:n], u_raw[:, j % 2, 0:n], ACT.Copy), "ff_high")

                done = 0
                for half, part in enumerate("AB"):
                    chunks = range(UP_A) if half == 0 else range(UP_A, FF)
                    for j in chunks:
                        feed(f"l{l}up{part}", 2 * (j - chunks[0]))
                        b = bank(act, (f"l{l}g", j))
                        if j >= 2:
                            act.wait_ge(sem("conv_done"), l * FF + j - 1)
                        else:
                            act.wait_ge(sem("pad_zero"), l + 1)
                        frees(f(gp[:, j % 2, 0:ns, 1:S + 1], b[:, 0:n].rearrange("p (a b) -> p a b", a=ns), ACT.Copy),
                              (f"l{l}g", j))
                        while done <= j - 2:
                            hidden_high(done)
                            done += 1
                        act.wait_ge(sem("conv_done"), l * FF + j + 1)
                        if j >= 2:
                            act.wait_ge(sem("ff_raw"), l * FF + j - 1)
                        tell(f(sg_[:, j % 2, 0:n], cg_[:, j % 2, 0:n], ACT.Silu), "ff_silu")
                    while done < (half + 1) * HF:
                        hidden_high(done)
                        done += 1
                    gated(lambda m: (f"l{l}down", half, m), l, n, f"l{l}down{part}")

            ffn(0, 512)
            feed("l1in", 0)
            layer_norm("d", 512, "l0ln2g", "l0ln2b", lambda k: XC[:, k, :], h_high(512, 2))
            for n in range(9):
                feed("l1in", n)
                b = bank(act, ("l1in", n))
                if n < 2:
                    o, src = ckv1[:, n, :], b[:, :]
                elif n == 2:
                    o, src = kr1[64:96, :], b[64:96, :]
                else:
                    o, src = cq1[:, n - 3, :], b[:, 0:S]
                frees(f(o, src, ACT.Copy), ("l1in", n))
            for n in range(9):
                evacuated(act, ("l1in", n))
            f(sq1[:, 0:6, 0:S], cq1, ACT.Square)
            tell(f(sq1[:, 6:8, :], ckv1, ACT.Square), "cq_sq")
            act.wait_ge(sem("cq_ms"), 2)
            f(lnst[:, 0, 0:S], lnst[:, 0, 0:S], ACT.Sqrt)
            tell(f(lnst[:, 1, :], lnst[:, 1, :], ACT.Sqrt), "cq_rms")
            for k in range(6):
                act.wait_ge(sem("cq_normed"), k + 1)
                tell(f(cq_hi[:, k, :], cq1[:, k, :], ACT.Copy), "cq_high")
            for m in range(8):
                feed("l1uq", ((2 * m + 1) * 6 + 5) // BLOCKS)
                frees(f(q1[0:96, 2 * m:2 * m + 2, :], bank(act, ("uq", m))[0:96, :].rearrange("p (a b) -> p a b", a=2),
                        ACT.Copy, scale=MLA_SCALE), ("uq", m))
            for hf in range(2):
                for t in range(4):
                    frees(f(V1[:, t, hf * 512:(hf + 1) * 512], bank(act, ("v1", t, hf))[:, :], ACT.Copy), ("v1", t, hf))
            attention("att3", att3, att2_P, att2_PT, None)
            y_high("att3", 4, yT1, y1_hi)
            gated(lambda m: ("l1out", m), 1, S)
            feed("l1upA", 0)
            layer_norm("e", S, "l1ln1g", "l1ln1b", lambda k: X1[:, k, :], h_high(S, 3))
            ffn(1, S)
            layer_norm("f", S, "l1ln2g", "l1ln2b", lambda k: X1[:, k, :])

        @block.vector
        def _(dve):
            seq = [0]
            chain = sem("dve_seq")
            counts = {}
            V = nc.vector
            fed = [0]

            def low(i, t, r_need):
                dve.wait_ge(w_high, r_need)
                V.tensor_tensor(w_lo[:, i % SPLIT_RING, :], ring[:, t % RING, :],
                                w_hi[:, i % SPLIT_RING, :].bitcast(F32), ALU.subtract).then_inc(w_split, 1)

            def feed(stage, n):
                t = first[stage] + n
                end = split_at[min(t + SPLIT_RING, run_end(t + 1 if t >= 0 else 1)) - 1] + 1
                for i in range(fed[0], end):
                    low(i, split_order[i], i + 1)
                fed[0] = max(fed[0], end)

            def rest(o, x, high):
                return V.tensor_tensor(o, x, high.bitcast(F32), ALU.subtract)

            def step(ins, name=None):
                if name is None:
                    seq[0] += 1
                    ins.then_inc(chain, 1)
                    dve.wait_ge(chain, seq[0])
                else:
                    counts[name] = counts.get(name, 0) + 1
                    ins.then_inc(sem(name), 1)
                    dve.wait_ge(sem(name), counts[name])

            def tell(ins, name):
                counts[name] = counts.get(name, 0) + 1
                ins.then_inc(sem(name), 1)

            def keys(h):
                b = bank(dve, ("kT", h))
                if h >= 2:
                    s_bank, use = job[("att3", "S", 2 * h - 3)]
                    dve.wait_ge(bank_ready[s_bank], use)
                frees(V.tensor_copy(kT1[0:64, h % 2, :], b[0:64, :]), ("kT", h))

            def attention(st, specs, Pb, L):
                n = len(specs)
                for i in range(n + NP + 1):
                    if st == "att3" and i == 0:
                        keys(0)
                    if i < n:
                        s = specs[i]
                        nk = s["nk"]
                        b = bank(dve, (st, "S", i))
                        nm = SV[:, i % 4:i % 4 + 1]
                        if s["bias"] is not None:
                            if i >= 3 and counts_exp(specs, i - 3):
                                dve.wait_ge(sem("att_exp"), exp_before[st] + counts_exp(specs, i - 3))
                            nb = s["bias"].shape[1]
                            ins = V.tensor_tensor(L[:, i % 3, 0:nb], b[:, 0:nb], s["bias"], ALU.add)
                            if nk > nb:
                                ins = V.tensor_copy(L[:, i % 3, nb:nk], b[:, nb:nk])
                            frees(ins, (st, "S", i))
                            evacuated(dve, (st, "S", i))
                            tell(V.tensor_reduce(nm, L[:, i % 3, 0:nk], AX.X, ALU.max, negate=True), "att_negmax")
                        else:
                            tell(V.tensor_reduce(nm, b[:, 0:nk], AX.X, ALU.max, negate=True), "att_negmax")
                    if st == "att3" and i % 2 == 0 and i < n - 2:
                        keys(i // 2 + 1)
                    j = i - 1
                    if 0 <= j < n:
                        s = specs[j]
                        if s["bias"] is not None:
                            dve.wait_ge(sem("att_exp"), exp_before[st] + counts_exp(specs, j))
                        else:
                            evacuated(dve, (st, "S", j))
                        rd = SV[:, 12 + j % 4:13 + j % 4]
                        tell(V.reciprocal(rd, SV[:, 8 + j % 4:9 + j % 4]), "att_recip")
                    j = i - NP - 1
                    if 0 <= j < n:
                        o = specs[j]["o"]
                        r0 = 64 * (o.start_partition() // 64)
                        frees(V.tensor_copy(o, bank(dve, (st, "O", j))[r0:r0 + 64, 0:P]), (st, "O", j))
                    j = i - 1
                    if 0 <= j < n:
                        s = specs[j]
                        dve.wait_ge(sem("att_recip"), counts["att_recip"])
                        tell(V.tensor_scalar(Pb[:, j % NP, 0:s["nk"]], Pb[:, j % NP, 0:s["nk"]], rd, None, ALU.mult),
                             "att_probs")

            def counts_exp(specs, i):
                return sum(s["bias"] is not None for s in specs[:i + 1])

            def layer_norm(which, n, eps, then=None):
                z, sq = ln_bufs(n)
                b = bank(dve, ("mean", which))
                frees(V.tensor_scalar(lnst[:, 0, 0:n], b[:, 0:n], -1.0 / D, None, ALU.mult), ("mean", which))
                evacuated(dve, ("mean", which))
                for k in range(KC):
                    tell(V.tensor_tensor(z[:, k, :], z[:, k, :], lnst[:, 0, 0:n], ALU.add), "centred")
                b = bank(dve, ("var", which))
                ins = V.tensor_scalar(lnst[:, 1, 0:n], b[:, 0:n], 1.0 / D, eps, ALU.mult, ALU.add)
                frees(ins, ("var", which))
                evacuated(dve, ("var", which))
                step(V.tensor_copy(SV[0:1, 44:45], lnst[0:1, 1, 0:1]), "var_eps")
                dve.wait_ge(sem("ln_std"), nth(which) // KC + 1)
                step(V.reciprocal(lnst[:, 2, 0:n], lnst[:, 2, 0:n]))
                dve.wait_ge(sem("centred"), nth(which) + KC)
                for k in range(KC):
                    tell(V.tensor_tensor(z[:, k, :], z[:, k, :], lnst[:, 2, 0:n], ALU.mult), "scaled")
                    if then is not None and k:
                        then(k - 1)
                if then is not None:
                    then(KC - 1)
                    then(KC)

            step(V.memset(dF[:, :, 0:1], 0.0), "d_pad")
            step(V.memset(cond_st.bitcast(F32), 0.0), "cond_zero")
            for k in range(KC):
                dve.wait_ge(sem("x_in_high"), k + 1)
                tell(rest(x_lo[k], X1[:, k, :], x_hi[:, k, :]), "x_in_split")
                if k < 3:
                    feed("in", k - 2)
            feed("in", 4)
            evacuated(dve, ("in", 4))
            tell(V.tensor_tensor(rel[:, 0, 0, :], F["ckv"][:, 0, :], F["ckv"][:, 0, :], ALU.mult), "ckv_sq")
            feed("in", 8)
            dve.wait_ge(sem("cond_high"), 1)
            tell(rest(cond_st[:, :, 2:4], p_("cond").rearrange("p (k s) -> p k s", k=KC), cond_st[:, :, 0:2]),
                 "cond_split")
            feed("in", 11)
            b = bank(dve, "ckvms")
            ins = V.tensor_scalar(rel[:, 0, 0, :], b[:, 0:S], 1.0 / 64, 1e-6, ALU.mult, ALU.add)
            frees(ins, "ckvms")
            evacuated(dve, "ckvms")
            step(V.tensor_copy(SV[0:1, 46:47], rel[0:1, 0, 0, 0:1]), "ckv_ms")
            dve.wait_ge(sem("ckv_rms"), 1)
            step(V.reciprocal(rel[:, 0, 1, :], rel[:, 0, 1, :]))
            step(V.scalar_tensor_tensor(F["ckv"][:, 0, :], F["ckv"][:, 0, :], p_("kv_gain"), rel[:, 0, 1, :],
                                        ALU.mult, ALU.mult), "ckv_normed")
            feed("in", 13)
            for n in range(7, 14):
                evacuated(dve, ("in", n))
            step(V.tensor_tensor(dS, dF[:, :, 0:S], dF[:, :, 1:S + 1], ALU.subtract))
            for n in range(7):
                step(V.scalar_tensor_tensor(dS[:, n, :], dS[:, n, :], p_("d_mu")[:, n:n + 1], dF[:, n, 1:S + 1],
                                            ALU.mult, ALU.add), "d_shifted")
            feed("in", 25)
            frees(V.tensor_copy(rows8[0:8, :], bank(dve, "t5")[0:8, :]), "t5")
            evacuated(dve, "t5")
            step(V.tensor_copy(SV[0:1, 45:46], rows8[0:1, 0:1]), "t5_row_ready")
            evacuated(dve, ("in", 3))
            for i in range(2):
                for q in range(4):
                    n = 4 * i + q
                    evacuated(dve, ("ix", i, q))
                    for m in range(2):
                        h = 4 * m + q
                        if n % 4 == 0 and m == 0:
                            ins = V.tensor_scalar(score[:, i, :], rel[:, n % 2, m, :], iw[:, i, h:h + 1], None, ALU.mult)
                        else:
                            ins = V.scalar_tensor_tensor(score[:, i, :], rel[:, n % 2, m, :], iw[:, i, h:h + 1],
                                                         score[:, i, :], ALU.mult, ALU.add)
                        if m:
                            step(ins, "rel_used")
                        else:
                            step(ins)
                step(V.scalar_tensor_tensor(work[:, i, 0, :], score[:, i, :], 8 ** -0.5,
                                            c_("causal")[:, i * S:(i + 1) * S], ALU.mult, ALU.add))
            for k in range(KEEP // 8):
                for i in range(2):
                    tell(V.max(top8[:, i, :], work[:, i, k % 2, :]), "top8")
                feed("ada0", 2 * k - 1)
                for i in range(2):
                    dve.wait_ge(sem("top8"), 2 * k + i + 1)
                    tell(V.match_replace(work[:, i, (k + 1) % 2, :], top8[:, i, :], work[:, i, k % 2, :], TAKEN),
                         "replaced")
                feed("ada0", 2 * k)
                dve.wait_ge(sem("replaced"), 2 * k + 2)
            for i in range(2):
                step(V.tensor_scalar(selm[:, i, :], work[:, i, 0, :], -2e38, NEG, ALU.is_gt, ALU.mult))
            feed("ada0", 2 * (KEEP // 8))
            dve.wait_ge(sem("bias1"), 32)
            for i in range(2):
                step(V.tensor_tensor(bias1[:, 4:8, i, :], bias1[:, 4:8, i, :], bc(selm[:, i, :], 4), ALU.add))
            feed("ada1", stage_tiles["ada1"] - 1)
            attention("att1", att1, att1_P, att1_L)
            evacuated(dve, "ca")
            step(V.tensor_scalar(C["zb"], c_z, p_("c_a_bias"), None, ALU.add), "c_zb")
            dve.wait_ge(sem("c_softplus"), 1)
            step(V.scalar_tensor_tensor(C["la"], C["zb"], 0.0, C["ln"], ALU.min, ALU.subtract))
            step(V.tensor_scalar(C["la"], C["la"], 1.0 / 16, None, ALU.mult))
            for c in range(NCH):
                cs = slice(c * CH, (c + 1) * CH)
                ins = V.tensor_tensor_scan(C["cum"][:, cs], c_("scan_ones"), C["la"][:, cs], 0.0, ALU.mult, ALU.add)
            step(ins, "c_cum")
            dve.wait_ge(sem("c_exps"), 1)
            V.scalar_tensor_tensor(C["qd"], F["cq"][:, 0, :], 32 ** -0.5, C["ec"], ALU.mult, ALU.mult)
            V.tensor_tensor(C["ki"], F["ck"][:, 0, :], C["en"], ALU.mult)
            step(V.tensor_tensor(C["kd"], F["ck"][:, 0, :], C["ed"], ALU.mult), "c_feat")
            for h in range(4):
                b = bank(dve, ("catt", h))
                frees(V.tensor_tensor(c_att[:, h, :, :], b[:, 0:P].rearrange("p (a b) -> p a b", a=2),
                                      bc(c_("upper_incl"), 2), ALU.mult), ("catt", h))
            for c in range(3):
                b = bank(dve, ("cupd", c))
                if c == 0:
                    ins = V.tensor_copy(c_state[:, 0, :], b[:, 0:S])
                else:
                    dec = C["ec"][:, c * CH + CH - 1:c * CH + CH]
                    ins = V.scalar_tensor_tensor(c_state[:, c, :], c_state[:, c - 1, :], dec, b[:, 0:S], ALU.mult,
                                                 ALU.add)
                frees(ins, ("cupd", c))
                evacuated(dve, ("cupd", c))
                step(V.tensor_tensor(c_sm[:, c, :], c_state[:, c, :], c_("heads_c"), ALU.mult), "c_states")
            b = bank(dve, "coms")
            ins = V.tensor_scalar(c_sq, b.rearrange("p (a b) -> p a b", a=2), 1.0 / 64, 1e-6, ALU.mult, ALU.add)
            frees(ins, "coms")
            evacuated(dve, "coms")
            step(V.tensor_copy(SV[0:1, 47:48], c_sq[0:1, 0, 0:1]), "c_ms")
            dve.wait_ge(sem("c_rms"), 1)
            step(V.reciprocal(c_sq, c_sq))
            step(V.tensor_tensor(c_o, c_o, c_sq, ALU.mult))
            for m in range(2):
                ins = V.scalar_tensor_tensor(ysT[:, 2, m, :], c_o[:, m, :], p_("c_norm_gain")[:, m:m + 1],
                                             F["cg"][:, m, :], ALU.mult, ALU.mult)
            step(ins, "ys_ready")
            r_, k_, v_ = dS[:, 1:3, :], dS[:, 3:5, :], dS[:, 5:7, :]
            evacuated(dve, "dw")
            evacuated(dve, "da")
            evacuated(dve, "dg")
            for m in range(2):
                ins = V.tensor_scalar(DD["kk"][:, m, :], k_[:, m, :], p_("d_k_k")[:, m:m + 1], None, ALU.mult)
            step(ins, "d_kk")
            step(V.tensor_scalar(DD["lw"], DZ["w"], -W_DECAY, None, ALU.mult))
            for m in range(2):
                for c in range(NCH):
                    cs = slice(c * CH, (c + 1) * CH)
                    ins = V.tensor_tensor_scan(DD["cum"][:, m, cs], c_("scan_ones"), DD["lw"][:, m, cs], 0.0,
                                               ALU.mult, ALU.add)
            step(ins)
            step(V.tensor_tensor(DD["cm1"], DD["cum"], DD["lw"], ALU.subtract), "d_cum")
            for m in range(2):
                step(V.tensor_scalar(DD["kp"][:, m, :], DZ["a"][:, m, :], 1.0, p_("d_k_a")[:, m:m + 1], ALU.subtract,
                                     ALU.mult))
            step(V.scalar_tensor_tensor(DD["kp"], DD["kp"], 1.0, k_, ALU.add, ALU.mult))
            dve.wait_ge(sem("d_kk_norm"), 1)
            step(V.tensor_scalar(DD["e1"], DD["e1"], 1e-12, None, ALU.max))
            step(V.reciprocal(DD["e1"], DD["e1"]))
            frees(V.tensor_tensor(DD["kk"], DD["kk"], DD["e1"], ALU.mult), "kkn")
            evacuated(dve, "kkn")
            step(V.tensor_tensor(DD["b"], DD["kk"], DZ["a"], ALU.mult), "d_kk_unit")
            dve.wait_ge(sem("d_exps"), 1)
            V.scalar_tensor_tensor(Ah, DD["kk"], -1.0, DD["e1"], ALU.mult, ALU.mult)
            V.tensor_tensor(Rh, r_, DD["e2"], ALU.mult)
            V.tensor_tensor(DD["Bh"], DD["b"], DD["e3"], ALU.mult)
            step(V.tensor_tensor(DD["Kh"], DD["kp"], DD["e3"], ALU.mult), "d_feat")
            step(V.tensor_tensor(bn, r_, DD["kp"], ALU.mult))
            for m in range(2):
                step(V.tensor_scalar(bn[:, m, :], bn[:, m, :], p_("d_r_k")[:, m:m + 1], None, ALU.mult))
            step(V.tensor_copy(SV[0:1, 48:49], bn[0:1, 0, 0:1]), "d_bonus_in")
            masks = {"N": "upper", "A": "lower", "GRB": "upper_incl", "GAK": "upper", "GRK": "upper_incl"}
            for fam, mask in masks.items():
                for p in range(2):
                    r = slice(64 * p, 64 * p + 64)
                    frees(V.tensor_tensor(U[fam][r, :, :], bank(dve, (fam, p))[r, :].rearrange("p (a b) -> p a b", a=8),
                                          bc(c_(mask)[r, :], 8), ALU.mult), (fam, p))
            for fam in ("N", "A"):
                for p in range(2):
                    evacuated(dve, (fam, p))
            dve.wait_ge(sem("ada_mat1"), 32)
            step(V.tensor_tensor(U["D"], U["N"], bc(c_("diag16"), 8), ALU.mult), "d_split")
            step(V.tensor_tensor(U["Dt"], U["A"], bc(c_("diag16"), 8), ALU.mult), "d_split")
            step(V.tensor_tensor(U["Lo"], U["N"], U["D"], ALU.subtract), "d_split")
            step(V.tensor_tensor(U["Z"], U["D"], bc(c_("eye64"), 8), ALU.add), "d_split")
            step(V.tensor_tensor(U["W"], U["Dt"], bc(c_("eye64"), 8), ALU.add), "d_split")
            for fam in FAM2:
                add_to = "Z" if fam[0] == "Z" else "W" if fam[0] == "W" else {"Y1": "Z", "T": "Y1"}.get(fam)
                for p in range(2):
                    r = slice(64 * p, 64 * p + 64)
                    if add_to is None and p == 1:
                        continue
                    b = bank(dve, (fam, p))[r, :].rearrange("p (a b) -> p a b", a=8)
                    if add_to is None:
                        ins = V.tensor_copy(U[fam][r, :, :], b)
                    else:
                        dst = U[add_to] if fam[0] in "ZW" else U[fam]
                        ins = V.tensor_tensor(dst[r, :, :], U[add_to][r, :, :], b, ALU.add)
                    frees(ins, (fam, p))
                    evacuated(dve, (fam, p))
            for c in range(NCH):
                r = slice(0, 64)
                for what, n in (("X", 0), ("U", 1)):
                    frees(V.tensor_copy(x_u[r, n, :, :], bank(dve, (what, c, 0))[r, 0:P].rearrange("p (a b) -> p a b", a=2)),
                          (what, c, 0))
                for p in range(2):
                    r = slice(64 * p, 64 * p + 64)
                    frees(V.tensor_copy(yT[r, :, c * CH:(c + 1) * CH],
                                        bank(dve, ("Yc", c, p))[r, 0:P].rearrange("p (a b) -> p a b", a=2)), ("Yc", c, p))
                if c < NCH - 1:
                    for p in range(2):
                        r = slice(64 * p, 64 * p + 64)
                        b = bank(dve, ("M", c, p))[r, 0:P].rearrange("p (a b) -> p a b", a=2)
                        if c == 0:
                            ins = V.tensor_copy(m_st[r, 4, :, :], b)
                        else:
                            ins = V.tensor_tensor(m_st[r, 4, :, :], m_st[r, c, :, :], b, ALU.add)
                        frees(ins, ("M", c, p))
                        evacuated(dve, ("M", c, p))
                        for m in range(2):
                            ins = V.tensor_scalar(m_st[r, c + 1, m, :], m_st[r, 4, m, :],
                                                  DD["e2"][r, m, c * CH + CH - 1:c * CH + CH], None, ALU.mult)
                        step(ins, "d_state")
            for p in range(2):
                for c in range(NCH):
                    evacuated(dve, ("Yc", c, p))
            step(V.tensor_copy(SV[0:1, 49:50], yT[0:1, 0, 0:1]), "d_y")
            flat2 = "p (a b) -> p a b"
            frees(V.tensor_tensor(bn, bank(dve, "bonus").rearrange(flat2, a=2), v_, ALU.mult), "bonus")
            b = bank(dve, "ymean").rearrange(flat2, a=2)
            frees(V.scalar_tensor_tensor(yT, b, -1.0 / 64, yT, ALU.mult, ALU.add), "ymean")
            evacuated(dve, "ymean")
            step(V.tensor_copy(SV[0:1, 50:51], yT[0:1, 0, 0:1]), "d_centred")
            b = bank(dve, "yvar").rearrange(flat2, a=2)
            frees(V.tensor_scalar(DD["e1"], b, 1.0 / 64, 64e-5, ALU.mult, ALU.add), "yvar")
            evacuated(dve, "yvar")
            step(V.tensor_copy(SV[0:1, 51:52], DD["e1"][0:1, 0, 0:1]), "d_var")
            dve.wait_ge(sem("d_std"), 1)
            step(V.reciprocal(DD["e1"], DD["e1"]))
            step(V.tensor_tensor(yT, yT, DD["e1"], ALU.mult))
            for m in range(2):
                step(V.tensor_scalar(yT[:, m, :], yT[:, m, :], p_("d_gn_w")[:, m:m + 1], p_("d_gn_b")[:, m:m + 1],
                                     ALU.mult, ALU.add))
            evacuated(dve, "bonus")
            step(V.tensor_tensor(yT, yT, bn, ALU.add))
            step(V.tensor_tensor(ysT[:, 3, :, :], yT, DZ["g"], ALU.mult), "ys_ready")
            for i in (12, 13, 14, 15, 8, 9, 10, 11, 0, 1, 2, 3, 4, 5, 6, 7):
                evacuated(dve, ("att1", "O", i))
            step(V.tensor_copy(SV[0:1, 52:53], ysT[0:1, 0, 0, 0:1]), "ys_ready")
            step(V.tensor_copy(SV[0:1, 53:54], ysT[0:1, 1, 0, 0:1]), "ys_ready")
            for l in range(2):
                b = bank(dve, ("adaT", l))
                o, n = PARAM[f"bada{l}"]
                ins = V.tensor_tensor(MOD[:, l, :, :], b[:, 0:96].rearrange("p (s m) -> p m s", s=2),
                                      par[:, o:o + n].unsqueeze(2).broadcast_to([P, 48, 2]), ALU.add)
                frees(ins, ("adaT", l))
                evacuated(dve, ("adaT", l))
                for q, g in enumerate((8, 32)):
                    step(V.tensor_scalar(SC1[:, l, q, :, :], MOD[:, l, g:g + 8, :], 1.0, None, ALU.add), "mods")
            z, _ = ln_bufs(S)
            def merged_low(m):
                dve.wait_ge(sem("merged_high"), m + 1)
                tell(rest(mg_lo[:, m, :], mergedT[:, m, :], mg_hi[:, m, :]), "merged_split")

            for m in range(KC):
                for half in range(2):
                    feed("merge", m * 5 + 2 * half + 1)
                    evacuated(dve, ("gt", m, half))
                    if half == 1 and m:
                        merged_low(m - 1)
                if m == 0:
                    for n in range(4):
                        dve.wait_ge(sem("ys_high"), n + 1)
                        tell(rest(ys_lo[:, n, :, :], ysT[:, n, :, :], ys_hi[:, n, :, :]), "ys_split")
                feed("merge", m * 5 + 4)
                for half in range(2):
                    b = bank(dve, ("br", m, half)).rearrange(flat2, a=2)
                    frees(V.tensor_tensor(tmpm[:, m % 2, half, :, :], b, gates[:, m % 2, 2 * half:2 * half + 2, :],
                                          ALU.mult), ("br", m, half))
                for half in range(2):
                    evacuated(dve, ("br", m, half))
                step(V.tensor_tensor(tmpm[:, m % 2, 0, :, :], tmpm[:, m % 2, 0, :, :], tmpm[:, m % 2, 1, :, :], ALU.add),
                     "gates_used")
                step(V.tensor_tensor(mergedT[:, m, :], tmpm[:, m % 2, 0, 0, :], tmpm[:, m % 2, 0, 1, :], ALU.add),
                     "merged")
            merged_low(KC - 1)
            for m in range(KC):
                feed("out", m)
                b = bank(dve, ("out1", m))
                frees(V.scalar_tensor_tensor(z[:, m, :], X1[:, m, :], ALPHA1, b[:, 0:S], ALU.mult, ALU.add),
                      ("out1", m))
                evacuated(dve, ("out1", m))
                step(V.tensor_copy(SV[0:1, 54:55], z[0:1, m, 0:1]), "mean_in")
            layer_norm("a", S, 1e-5)

            def first_max(t, vals, m, eq, incl, oh, w):
                step(V.tensor_scalar(eq, vals, m, None, ALU.is_equal))
                step(V.tensor_tensor_scan(incl, c_("scan_ones")[:, 0:w], eq, 0.0, ALU.mult, ALU.max))
                step(V.tensor_copy(oh[:, 0:1], incl[:, 0:1]))
                step(V.tensor_tensor(oh[:, 1:w], incl[:, 1:w], incl[:, 0:w - 1], ALU.subtract))

            feed("moe", 0)
            for k in range(KC):
                dve.wait_ge(sem("x_high"), k + 1)
                tell(rest(mx_lo[:, k, :], X1[:, k, :], mx_hi[:, k, :]), "x_split")
            def lows(c, n, r=None):
                for i in range(c, c + n):
                    q = split0 + i
                    low(q, moe0 + i, q + 1 if r is None else r * 12 + (q + 1))

            for t in range(2):
                if t:
                    lows(3, 1)

                def sv(n):
                    return SV[:, n + t:n + t + 1]

                b = bank(dve, ("rt", t))
                frees(V.tensor_tensor(lg[:, t, :], b[:, 0:36], p_("router_bias"), ALU.add), ("rt", t))
                evacuated(dve, ("rt", t))
                step(V.tensor_reduce(sv(18), lg[:, t, 0:4], AX.X, ALU.max))
                step(V.tensor_scalar(sv(16), sv(18), -1.0, None, ALU.mult), "rt_neg")
                R = [rt[:, t, n, :] for n in range(12)]
                first_max(t, lg[:, t, 0:4], sv(18), R[1][:, 0:4], R[2][:, 0:4], R[3][:, 0:4], 4)
                ohg = R[3][:, 0:4].unsqueeze(2).broadcast_to([P, 4, 8])
                step(V.tensor_scalar(R[4][:, 0:4], R[3][:, 0:4], 1.0, -NEG, ALU.subtract, ALU.mult))
                step(V.tensor_tensor(R[5].rearrange("p (a b) -> p a b", a=4),
                                     lg[:, t, 4:36].rearrange("p (a b) -> p a b", a=4), ohg, ALU.mult))
                step(V.tensor_tensor(R[5].rearrange("p (a b) -> p a b", a=4), R[5].rearrange("p (a b) -> p a b", a=4),
                                     R[4][:, 0:4].unsqueeze(2).broadcast_to([P, 4, 8]), ALU.add))
                step(V.tensor_reduce(sv(22), R[5], AX.X, ALU.max))
                first_max(t, R[5], sv(22), R[6], R[7], R[8], 32)
                step(V.scalar_tensor_tensor(R[5], R[8], 4 * NEG, R[5], ALU.mult, ALU.add))
                step(V.tensor_reduce(sv(24), R[5], AX.X, ALU.max))
                first_max(t, R[5], sv(24), R[6], R[7], R[9], 32)
                step(V.tensor_tensor(sv(28), sv(24), sv(22), ALU.subtract), "rt_diff")
                dve.wait_ge(sem("rt_gexp"), t + 1)
                dve.wait_ge(sem("rt_eexp"), t + 1)
                step(V.tensor_scalar(sv(34), sv(32), 1.0, sv(20), ALU.add, ALU.mult))
                step(V.reciprocal(sv(36), sv(34)))
                step(V.scalar_tensor_tensor(R[10], R[9], sv(32), R[8], ALU.mult, ALU.add))
                step(V.tensor_scalar(R[11], R[10], sv(36), None, ALU.mult), "gate_ready")

            def gated_hidden(par_, n):
                dve.wait_ge(sem("moe_silu"), n + 1)
                V.tensor_tensor(m_t[:, par_, :, :], m_sg[:, par_, :, :], gate_of(n), ALU.mult)\
                    .then_inc(sem("moe_gated"), 1)

            def raw_hidden(par_, n):
                dve.wait_ge(sem("moe_gated"), n + 1)
                dve.wait_ge(sem("moe_up"), n + 1)
                V.tensor_tensor(m_t[:, par_, :, :], m_t[:, par_, :, :],
                                ps[2 * par_ + 1].rearrange("p (a b) -> p a b", a=2), ALU.mult)\
                    .then_inc(sem("moe_raw"), 1)

            def hidden_low(par_, n):
                dve.wait_ge(sem("moe_high"), n + 1)
                rest(mh_lo[:, par_, :, :], m_t[:, par_, :, :], mh_hi[:, par_, :, :]).then_inc(sem("moe_hidden"), 1)

            def gate_of(e):
                rows = gate_bc[:, e:e + 1, :] if isinstance(e, int) else gate_bc[:, bass.ds(e, 1), :]
                return rows.broadcast_to([P, 2, S])

            def expert(par_, n, c, r=None, last=False):
                hidden_low(1 - par_, n - 1)
                if c > 4:
                    lows(c + 2, 2, r)
                gated_hidden(par_, n)
                lows(c + 4, 2, r)
                raw_hidden(par_, n)
                if not last:
                    lows(c + 6, 2, r)

            lows(4, 4)
            dve.wait_ge(sem("gate_bc"), 16)
            gated_hidden(0, 0)
            raw_hidden(0, 0)
            for e in (1, 2):
                expert(e % 2, e, 6 * e - 2)
            with dve.Fori(0, (EXPERTS - 4) // 2) as r:
                for s in range(2):
                    expert((1 + s) % 2, r * 2 + (3 + s), 16 + 6 * s, r)
            e = EXPERTS - 1
            expert(1, e, 6 * e - 2, last=True)
            hidden_low(1, e)
            lows(6 * EXPERTS - 2, 2)
            fed[0] = split0 + 6 * EXPERTS
            dve.wait_ge(sem("moe_down"), EXPERTS)
            for m in range(KC):
                step(V.scalar_tensor_tensor(z[:, m, :], X1[:, m, :], ALPHA1, ps[4 + m // 2][:, (m % 2) * S:(m % 2 + 1) * S],
                                            ALU.mult, ALU.add), "z_written")
                step(V.tensor_copy(SV[0:1, 54:55], z[0:1, m, 0:1]), "mean_in")
            feed("l0in", 0)
            layer_norm("b", S, 1e-5)

            def modulate(l, q, n, which):
                before = KC * (2 * l + q)
                hi, lo = in_split(n)
                zz, _ = ln_bufs(n)

                def chunk(k):
                    if k < KC:
                        dve.wait_ge(sem("ln_out"), nth(which) + (min(2 * k + 2, KC) if which == "b" else k + 1))
                        for s in range(n // S):
                            ss = slice(s * S, (s + 1) * S)
                            ins = V.tensor_scalar(zz[:, k, ss], XC[:, k, ss], SC1[:, l, q, k, s:s + 1],
                                                  MOD[:, l, 24 * q + k, s:s + 1], ALU.mult, ALU.add)
                        tell(ins, "h_raw")
                    if k:
                        dve.wait_ge(sem("h_high"), before + k)
                        tell(rest(lo[:, k - 1, :], zz[:, k - 1, :], hi[:, k - 1, :]), "h_split")

                return chunk

            dve.wait_ge(sem("ctx_in"), 16)
            dve.wait_ge(sem("mods"), 4)
            h_chunk = modulate(0, 0, 512, "b")
            for k in range(KC + 1):
                h_chunk(k)
            dve.wait_ge(sem("na_bias"), 16 * 32)
            for h in range(8):
                feed("l0in", h // 2)
                step(V.tensor_tensor(na_bias[:, h, :, :], na_bias[:, h, :, :], bc(c_("na_mask"), 2), ALU.add))
            feed("l0in", 6)
            for m in range(5):
                b = bank(dve, ("qms", m))
                frees(V.tensor_scalar(tq[:, m, :], b[:, :], 1.0 / 64, 1e-6, ALU.mult, ALU.add), ("qms", m))
                evacuated(dve, ("qms", m))
                step(V.tensor_copy(SV[0:1, 55:56], tq[0:1, m, 0:1]), "q0_ms")
            feed("l0in", 8)
            for m in range(5):
                feed("l0in", 8 + m // 2)
                dve.wait_ge(sem("q0_rms"), m + 1)
                step(V.reciprocal(tq[:, m, :], tq[:, m, :]))
                g = p_("q_gain") if m < 4 else p_("k_gain")
                step(V.scalar_tensor_tensor(Q0[:, m, :], Q0[:, m, :], g, tq[:, m, :], ALU.mult, ALU.mult), "q0_normed")
            feed("l0in", 13)
            for m in range(5):
                b = bank(dve, ("rope0", m))
                frees(V.tensor_tensor(tq[:, m, 0:S], b[:, 0:S], c_("sin64"), ALU.mult), ("rope0", m))
                evacuated(dve, ("rope0", m))
                step(V.tensor_tensor(Q0[:, m, 0:S], Q0[:, m, 0:S], c_("cos64"), ALU.mult))
                step(V.tensor_tensor(Q0[:, m, 0:S], Q0[:, m, 0:S], tq[:, m, 0:S], ALU.add), "q0_roped")
            feed("l0in", 17)
            attention("att2", att2, att2_P, att2_L)

            def y_low(y, hi, lo, before):
                for k in range(KC):
                    dve.wait_ge(sem("y_high"), before + k + 1)
                    tell(rest(lo[:, k, :], y[:, k, :], hi[:, k, :]), "y_split")

            def residual(name, n, stage=None):
                zz, _ = ln_bufs(n)
                for m in range(KC):
                    if stage is not None:
                        feed(stage, (m * HF + HF - 1) // BLOCKS)
                    else:
                        feed(name(m)[0], m)
                    evacuated(dve, name(m))
                    part = lnst[:, m % 2, 0:n]
                    if stage is not None and stage[-1] == "B":
                        step(V.tensor_tensor(zz[:, m, :], zz[:, m, :], part, ALU.add), "z_written")
                    else:
                        step(V.scalar_tensor_tensor(zz[:, m, :], XC[:, m, 0:n], ALPHA2, part, ALU.mult, ALU.add),
                             "z_written")
                    if stage is None or stage[-1] == "B":
                        step(V.tensor_copy(SV[0:1, 54:55], zz[0:1, m, 0:1]), "mean_in")

            y_low(yT0, y0_hi, y0_lo, 0)
            residual(lambda m: ("l0out", m), 512)
            feed("l0upA", 0)
            layer_norm("c", 512, 1e-6, modulate(0, 1, 512, "c"))

            def ffn(l, n):
                ns = n // S
                cw = p_(f"l{l}conv").rearrange("p (w j) -> p w j", w=3)
                cb = p_(f"l{l}convb")
                step(V.memset(gp[:, :, :, :], 0.0), "pad_zero")
                raw, split = 0, 0
                for half, part in enumerate("AB"):
                    chunks = range(UP_A) if half == 0 else range(UP_A, FF)
                    for j in chunks:
                        feed(f"l{l}up{part}", 2 * (j - chunks[0]))
                        evacuated(dve, (f"l{l}g", j))
                        if j >= 2:
                            dve.wait_ge(sem("ff_silu"), l * FF + j - 1)
                        g = gp[:, j % 2, 0:ns, :]
                        c = cg_[:, j % 2, 0:n].rearrange("p (a b) -> p a b", a=ns)
                        step(V.tensor_scalar(c, g[:, :, 0:S], cw[:, 0, j:j + 1], cb[:, j:j + 1], ALU.mult, ALU.add))
                        step(V.scalar_tensor_tensor(c, g[:, :, 1:S + 1], cw[:, 1, j:j + 1], c, ALU.mult, ALU.add))
                        step(V.scalar_tensor_tensor(c, g[:, :, 2:S + 2], cw[:, 2, j:j + 1], c, ALU.mult, ALU.add),
                             "conv_done")
                        while raw <= j - 1:
                            hidden(l, raw, n)
                            raw += 1
                        while split <= j - 2:
                            hidden_low(l, split, n)
                            split += 1
                    hidden(l, raw, n)
                    raw += 1
                    while split < (half + 1) * HF:
                        hidden_low(l, split, n)
                        split += 1
                    residual(lambda m: (f"l{l}down", half, m), n, f"l{l}down{part}")

            def hidden(l, j, n):
                dve.wait_ge(sem("ff_silu"), l * FF + j + 1)
                if j >= 2:
                    dve.wait_ge(sem("ff_split"), l * FF + j - 1)
                b = bank(dve, (f"l{l}v", j))
                ins = V.tensor_tensor(u_raw[:, j % 2, 0:n], sg_[:, j % 2, 0:n], b[:, 0:n], ALU.mult)
                frees(ins, (f"l{l}v", j))
                evacuated(dve, (f"l{l}v", j))
                step(V.tensor_copy(SV[0:1, 56:57], u_raw[0:1, j % 2, 0:1]), "ff_raw")

            def hidden_low(l, j, n):
                dve.wait_ge(sem("ff_high"), l * FF + j + 1)
                tell(rest(u_lo[:, j % HF, 0:n], u_raw[:, j % 2, 0:n], u_hi[:, j % HF, 0:n]), "ff_split")

            ffn(0, 512)
            feed("l1in", 0)
            layer_norm("d", 512, 1e-6, modulate(1, 0, 512, "d"))
            feed("l1in", 8)
            b = bank(dve, "cqms")
            frees(V.tensor_scalar(lnst[:, 0, 0:S], b[:, 0:S], 1.0 / 768, 1e-6, ALU.mult, ALU.add), "cqms")
            b = bank(dve, "ckvms1")
            frees(V.tensor_scalar(lnst[:, 1, :], b[:, :], 1.0 / 256, 1e-6, ALU.mult, ALU.add), "ckvms1")
            evacuated(dve, "cqms")
            step(V.tensor_copy(SV[0:1, 57:58], lnst[0:1, 0, 0:1]), "cq_ms")
            evacuated(dve, "ckvms1")
            step(V.tensor_copy(SV[0:1, 57:58], lnst[0:1, 1, 0:1]), "cq_ms")
            dve.wait_ge(sem("cq_rms"), 1)
            V.reciprocal(lnst[:, 0, 0:S], lnst[:, 0, 0:S])
            step(V.reciprocal(lnst[:, 1, :], lnst[:, 1, :]))
            for k in range(6):
                tell(V.scalar_tensor_tensor(cq1[:, k, :], cq1[:, k, :], p_("cq_gain")[:, k:k + 1], lnst[:, 0, 0:S],
                                            ALU.mult, ALU.mult), "cq_normed")
            for k in range(6):
                dve.wait_ge(sem("cq_high"), k + 1)
                tell(rest(cq_lo[:, k, :], cq1[:, k, :], cq_hi[:, k, :]), "cq_split")
            for k in range(2):
                tell(V.scalar_tensor_tensor(ckv1[:, k, :], ckv1[:, k, :], p_("ckv_gain")[:, k:k + 1], lnst[:, 1, :],
                                            ALU.mult, ALU.mult), "ckv_normed1")
            kr = slice(64, 96)
            b = bank(dve, "krope")
            frees(V.tensor_tensor(tq1[kr, 0, 0:S], b[kr, 0:S], c_("sinm")[kr, :], ALU.mult), "krope")
            evacuated(dve, "krope")
            step(V.tensor_tensor(kr1[kr, 0:S], kr1[kr, 0:S], c_("cosm")[kr, :], ALU.mult))
            step(V.tensor_tensor(kr1[kr, 0:S], kr1[kr, 0:S], tq1[kr, 0, 0:S], ALU.add))
            for q in range(2):
                step(V.tensor_copy(kT1[kr, q, :], kr1[kr, :]), "kr_placed")
            feed("l1uq", stage_tiles["l1uq"] - 1)
            for m in range(8):
                b = bank(dve, ("qrope", m))[0:96, :].rearrange(flat2, a=2)
                t = tq1[0:96, m % 2, :].rearrange(flat2, a=2)
                qq = q1[0:96, 2 * m:2 * m + 2, :]
                frees(V.tensor_tensor(t, b, bc(c_("sinm")[0:96, :], 2), ALU.mult), ("qrope", m))
                evacuated(dve, ("qrope", m))
                step(V.tensor_tensor(qq, qq, bc(c_("cosm")[0:96, :], 2), ALU.mult))
                step(V.tensor_tensor(qq, qq, t, ALU.add), "q1_roped")
            attention("att3", att3, att2_P, None)
            y_low(yT1, y1_hi, y1_lo, KC)
            residual(lambda m: ("l1out", m), S)
            feed("l1upA", 0)
            layer_norm("e", S, 1e-6, modulate(1, 1, S, "e"))
            ffn(1, S)
            layer_norm("f", S, 1e-6)
            for k in range(KC):
                dve.wait_ge(sem("ln_out"), nth("f") + k + 1)
                step(V.tensor_copy(SV[0:1, 58:59], X1[0:1, k, 0:1]), "result_chunks")


def shape_constants():
    c = np.zeros((P, NCONST), np.float32)

    def put(name, a, rows=P):
        o, n = CONST[name]
        c[:rows, o:o + n] = a

    put("ident", np.eye(P))
    put("ones", np.ones((P, P)))
    half = np.arange(P) // 64
    put("blockones", (half[:, None] == half[None, :]))
    rot = np.zeros((P, P))
    for i in range(0, P, 2):
        rot[i + 1, i] = -1.0
        rot[i, i + 1] = 1.0
    put("rot", rot)
    pos = np.arange(S)

    def rope(dim):
        inv = (np.float32(10000.0) ** (-np.arange(0, dim // 2, 2, dtype=np.float32) / np.float32(dim // 2)))
        ang = np.concatenate([(pos // 64)[:, None].astype(np.float32) * inv,
                              (pos % 64)[:, None].astype(np.float32) * inv], -1).astype(np.float32)
        return np.repeat(np.cos(ang), 2, 1).T, np.repeat(np.sin(ang), 2, 1).T

    co, si = rope(64)
    put("cos64", np.tile(co, (2, 1)))
    put("sin64", np.tile(si, (2, 1)))
    co, si = rope(32)
    a = np.zeros((P, S))
    a[0:64] = 1.0
    a[64:96] = co
    put("cosm", a)
    a = np.zeros((P, S))
    a[64:96] = si
    put("sinm", a)
    dist = 255 - np.arange(512)
    dd = np.maximum(dist, 0)
    df = np.maximum(dd, 1).astype(np.float32)
    large = 16 + (np.log(df / np.float32(16)) / np.float32(math.log(128.0)) * np.float32(16)).astype(np.int32)
    bucket = np.where(dd < 16, dd, np.minimum(large, 31))
    t = np.zeros((34, 512))
    ok = dist >= 0
    t[bucket[ok], np.nonzero(ok)[0]] = 1.0
    count = ok * ((dist <= 128) * 1 + (dist % 4 == 0) + (dist % 16 == 0))
    t[32] = np.where(count > 0, np.log(np.maximum(count, 1)), NEG)
    t[33] = np.where(ok, 0.0, NEG)
    put("buckets", t, 34)
    col = np.arange(64)
    start = np.clip(col - 8, 0, 48)
    inside = (col[None, :] >= start[:, None]) & (col[None, :] < start[:, None] + 16)
    put("na_mask", np.tile(np.where(inside, 0.0, NEG), (2, 4)))
    i, j = np.arange(64)[:, None], np.arange(64)[None, :]
    put("upper", np.tile(i < j, (2, 1)))
    put("upper_incl", np.tile(i <= j, (2, 1)))
    put("lower", np.tile(i > j, (2, 1)))
    put("diag16", np.tile(i // 16 == j // 16, (2, 1)))
    put("eye64", np.tile(i == j, (2, 1)))
    put("heads_c", (np.arange(P) // 32)[:, None] == (np.arange(256) // 64)[None, :])
    q = np.arange(P)[:, None]
    put("causal", np.concatenate([np.where(np.arange(S)[None, :] <= q + P * n, 0.0, NEG) for n in range(2)], 1))
    put("scan_ones", np.ones((P, 64)))
    return c


def lay_out(v):
    f32 = np.float32

    def blocks(w, order="mk"):
        kk, mm = w.shape
        b = w.reshape(kk // P, P, mm // P, P)
        b = b.transpose(2, 0, 1, 3) if order == "mk" else b.transpose(0, 2, 1, 3)
        return b.reshape(-1, P, P)

    def tiles(bl):
        n = -(-len(bl) // BLOCKS)
        if len(bl) < n * BLOCKS:
            bl = np.concatenate([bl, np.zeros((n * BLOCKS - len(bl), P, P), f32)])
        return bl.reshape(n, BLOCKS, P, P).transpose(0, 2, 1, 3).reshape(n, P, TILE)

    wi = v["w_in"][0]

    def cols(name, a=0, b=None):
        o = IN_OFF[name]
        return wi[:, o + a:o + (b if b is not None else dict(IN_NAMES)[name])]

    small = np.zeros((D, P), f32)
    small[:, R_W:R_W + 16] = cols("d", 768, 784)
    small[:, R_A:R_A + 16] = cols("d", 784, 800)
    small[:, R_G:R_G + 32] = cols("d", 800, 832)
    small[:, R_C:R_C + 16] = cols("c_a")
    iwp = np.zeros((D, P), f32)
    iwp[:, 0:8] = cols("b_iw")
    w1 = np.concatenate([cols("b_iq"), np.tile(cols("b_ik"), (1, 4)), iwp, np.tile(cols("b_ckv"), (1, 2)),
                         cols("b_q"), small, cols("d", 0, 768), cols("c_q"), cols("c_k"), cols("c_v"), cols("c_g"),
                         cols("a_q"), cols("a_k"), cols("a_v")], 1)
    w1 = tiles(blocks(w1))
    for name in ("c_v", "a_v"):
        n = IN_BLOCKS.index(name[0] + "v0")
        w1[n:n + 2] = cols(name).reshape(2, 4, P, 256).transpose(0, 2, 1, 3).reshape(2, P, TILE)
    parts = [w1]
    for l in range(2):
        parts.append(v[f"l{l}_w_ada_2"].reshape(KC, P, ADA // 1024, 1024).transpose(2, 0, 1, 3).reshape(-1, P, TILE))
    gt = blocks(cols("gate")).reshape(4, KC, KC, P, P)
    br = np.stack([blocks(v["w_branch"][0, n]).reshape(KC, 2, P, P) for n in range(4)])
    mg = np.concatenate([gt.transpose(1, 0, 2, 3, 4).reshape(KC, 32, P, P),
                         br.transpose(1, 0, 2, 3, 4).reshape(KC, 8, P, P)], 1).reshape(-1, P, P)
    parts.append(tiles(mg))
    parts.append(tiles(blocks(v["w_out"][0])))
    moe = {"gate": v["moe_w_gate"][0], "up": v["moe_w_up"][0], "down": v["moe_w_down"][0]}
    parts.append(np.concatenate([tiles(blocks(moe[kind][e], "km" if kind == "down" else "mk"))
                                 for kind, e in moe_tiles()]))
    w = v["l0_w_in_2"]
    qa = w[:, 0:512].reshape(D, 2, 4, 64).transpose(0, 2, 1, 3).reshape(D, 512)
    parts.append(tiles(blocks(np.concatenate([qa, w[:, 512:1792]], 1))))
    parts.append(w[:, 1792:].reshape(4, 2, P, 512).transpose(0, 2, 1, 3).reshape(4, P, TILE))
    w = v["l0_w_out_2"]
    wa = w[0:512].reshape(2, 4, 64, D).transpose(1, 0, 2, 3).reshape(512, D)
    parts.append(tiles(blocks(np.concatenate([wa, w[512:]], 0))))

    def ff(l):
        up = tiles(blocks(v[f"l{l}_w_up_2"]).reshape(2, FF, KC, P, P).transpose(1, 0, 2, 3, 4).reshape(-1, P, P))
        down = v[f"l{l}_w_down_2"]
        return [up[:2 * UP_A], tiles(blocks(down[:HF * P])), up[2 * UP_A:], tiles(blocks(down[HF * P:]))]

    parts += ff(0)
    w = v["l1_w_in_2"]
    krp = np.zeros((D, P), f32)
    krp[:, 64:96] = w[:, 1024:1056]
    parts.append(tiles(blocks(np.concatenate([w[:, 768:1024], krp, w[:, 0:768]], 1))))
    uq = np.zeros((768, 16, P), f32)
    uq[:, :, 0:96] = v["l1_w_uq_2"].reshape(768, 16, 96)
    parts.append(tiles(blocks(uq.reshape(768, 2048))))
    ukv = v["l1_w_ukv_2"].reshape(2, P, 16, 2, 64)
    for which in (1, 0):
        parts.append(ukv[:, :, :, which, :].reshape(2, P, TILE))
    parts.append(tiles(blocks(v["l1_w_out_2"])))
    parts += ff(1)
    wall = np.concatenate(parts)
    assert wall.shape[0] == stream_plan()[1], (wall.shape, stream_plan()[1], [x.shape[0] for x in parts])

    par = np.zeros((P, NPARAM), f32)

    def put(name, a, r0=0):
        o, n = PARAM[name]
        a = np.asarray(a, f32)
        par[r0:r0 + a.shape[0], o:o + a.shape[1]] = a

    def col(a):
        return np.asarray(a, f32).reshape(-1, P).T

    put("kv_gain", np.tile(v["b_kv_gain"][0], 2)[:, None])
    put("c_a_bias", col(v["c_a_bias"][0]))
    put("c_norm_gain", col(v["c_norm_gain"][0]))
    mu = v["d_mu"][0]
    o = PARAM["d_mu"][0]
    par[R_W:R_W + 16, o] = mu[768:784]
    par[R_A:R_A + 16, o] = mu[784:800]
    par[R_G:R_G + 32, o] = mu[800:832]
    par[:, o + 1:o + 7] = col(mu[:768])
    for nm in ("d_w0", "d_a0", "d_k_k", "d_k_a", "d_r_k", "d_gn_w", "d_gn_b"):
        put(nm, col(v[nm][0]))
    for n in range(2):
        put(f"ln{n + 1}g", col(v["ln_g"][0, n]))
        put(f"ln{n + 1}b", col(v["ln_b"][0, n]))
    for l in range(2):
        put(f"bada{l}", col(v[f"l{l}_b_ada_2"]))
        for n in range(1, 3):
            for s in "gb":
                put(f"l{l}ln{n}{s}", col(v[f"l{l}_ln{n}_{s}_2"]))
        put(f"l{l}conv", np.concatenate([col(v[f"l{l}_conv_w_2"][n]) for n in range(3)], 1))
        put(f"l{l}convb", col(v[f"l{l}_conv_b_2"]))
    put("q_gain", np.tile(v["l0_q_gain_2"], 2)[:, None])
    put("k_gain", np.tile(v["l0_k_gain_2"], 2)[:, None])
    put("cq_gain", col(v["l1_cq_gain_2"]))
    put("ckv_gain", col(v["l1_ckv_gain_2"]))
    put("cond", np.stack([col(v["c_2"][0]), col(v["c_ctx_2"])], 2).reshape(P, 16))
    put("lora", v["d_w2"][0], R_W)
    put("lora", v["d_a2"][0], R_A)
    put("lora", v["d_g2"][0], R_G)
    put("lora", v["c_a_up"][0], R_C)
    put("w_uv", v["b_w_uv"][0].transpose(1, 0, 2).reshape(64, 256))
    r = np.concatenate([v["router_g"][0], v["router_e"][0]], 1)
    put("router", r.reshape(KC, P, 36).transpose(1, 0, 2).reshape(P, 288))
    put("router_bias", np.tile(np.concatenate([v["router_g_bias"][0], v["router_e_bias"][0]])[None], (P, 1)))
    rows = np.zeros((34, 8), f32)
    rows[0:32] = v["rpb_table"]
    rows[32, 0:4] = 1.0
    rows[33, 4:8] = 1.0
    put("rpb_rows", rows)
    rpb = np.zeros((8, 7, P), f32)
    rpb[:, :, 48:79] = v["l0_rpb_2"][:, 4:11, :]
    xt = np.ascontiguousarray(v["x"][0].T).reshape(KC, P, S)
    ct = np.ascontiguousarray(v["ctx_2"][0].T).reshape(KC, P, S)
    return {"wall": wall, "consts": shape_constants(), "params": par, "xin": xt, "ctxin": ct,
            "rpb_pad": rpb.reshape(8, 896)}


def kernel(**inputs):
    import concourse.bacc as bacc
    from concourse.bass_utils import run_bass_kernel_spmd

    nc = bacc.Bacc("TRN2", target_bir_lowering=False, num_devices=1)
    arrays = {k: np.ascontiguousarray(a) for k, a in lay_out({k: np.asarray(a) for k, a in inputs.items()}).items()}
    aps = [nc.dram_tensor(k, a.shape, F32, kind="ExternalInput").ap() for k, a in arrays.items()]
    out = nc.dram_tensor("out", [KC, P, S], F32, kind="ExternalOutput").ap()
    build(nc, *aps, out)
    r = run_bass_kernel_spmd(nc, [arrays], core_ids=[0])
    return np.ascontiguousarray(r.results[0]["out"].reshape(D, S).T[None])
```
